# Optimizing a Trainium2 kernel written in Bass

```python
import jax, jax.numpy as jnp
from jax import lax
import numpy as np

D_MODEL = 1024
BATCH = 1
SEQ = 256
DEPTH = 2
DEC_BATCH = 8
DEC_SEQ = 4
PAST_LEN = 2048
PAGE_SIZE = 128

N_MIXERS = 2
N_A_LAYERS = (DEPTH + 1) // 2
N_B_LAYERS = DEPTH // 2
MIX_WIDTH = D_MODEL // 2
N_MEM = 256
N_XHEADS = 4
XHEAD_DIM = (D_MODEL // 2) // N_XHEADS
XATTN_WIDTH = N_XHEADS * XHEAD_DIM
CONV_A_WIDTH = 31
CONV_B_WIDTH = 3
N_EXPERTS = 64
TOP_K = 8
N_GROUPS = 8
TOPK_GROUPS = 4
EXPERT_FF = D_MODEL // 4
SHARED_FF = EXPERT_FF
ROUTED_SCALE = 2.5
EXPERT_BLOCK = 128
LN_EPS = 1e-5
DEEPNORM_ALPHA = (2 * DEPTH) ** 0.25
DEEPNORM_BETA = (8 * DEPTH) ** -0.25

kernel_name = "interleaved_conv_memxattn_moe_step"

def layer_norm(x, g, b):
    xf = x.astype(jnp.float32)
    mu = jnp.mean(xf, axis=-1, keepdims=True)
    var = jnp.mean(jnp.square(xf - mu), axis=-1, keepdims=True)
    return ((xf - mu) * lax.rsqrt(var + LN_EPS) * g.astype(jnp.float32) + b.astype(jnp.float32)).astype(x.dtype)

def causal_depthwise_conv(u, hist, w):
    width, ch = w.shape
    full = jnp.concatenate([hist.astype(u.dtype), u], axis=1)
    y = lax.conv_general_dilated(full, w.astype(u.dtype)[:, None, :], window_strides=(1,), padding='VALID',
                                 dimension_numbers=('NWC', 'WIO', 'NWC'), feature_group_count=ch)
    return y, full[:, full.shape[1] - (width - 1):]

def memory_attention(q, mem_k, mem_v):
    q = q.reshape(q.shape[0], q.shape[1], N_XHEADS, XHEAD_DIM)
    s = jnp.einsum('blhd,bmhd->bhlm', q, mem_k.astype(q.dtype)).astype(jnp.float32) * (XHEAD_DIM ** -0.5)
    p = jax.nn.softmax(s, axis=-1).astype(q.dtype)
    o = jnp.einsum('bhlm,bmhd->blhd', p, mem_v.astype(q.dtype))
    return o.reshape(o.shape[0], o.shape[1], XATTN_WIDTH)

def route(xt, w_router, router_bias):
    t = xt.shape[0]
    scores = jax.nn.sigmoid((xt @ w_router).astype(jnp.float32))
    biased = scores + router_bias.astype(jnp.float32)
    grp = biased.reshape(t, N_GROUPS, N_EXPERTS // N_GROUPS)
    grp_score = jnp.sum(lax.top_k(grp, 2)[0], axis=-1)
    _, grp_idx = lax.top_k(grp_score, TOPK_GROUPS)
    grp_mask = jnp.any(grp_idx[..., None] == jnp.arange(N_GROUPS), axis=-2)
    expert_mask = jnp.repeat(grp_mask, N_EXPERTS // N_GROUPS, axis=-1)
    _, idx = lax.top_k(jnp.where(expert_mask, biased, -jnp.inf), TOP_K)
    w = jnp.take_along_axis(scores, idx, axis=-1)
    w = w / jnp.sum(w, axis=-1, keepdims=True) * ROUTED_SCALE
    return idx, w

def routed_experts(xt, idx, gate, w_gate, w_up, w_down):
    t, d = xt.shape
    n_slots = t * TOP_K
    flat_e = idx.reshape(n_slots)
    order = jnp.argsort(flat_e)
    sorted_e = flat_e[order]
    sorted_tok = (order // TOP_K).astype(jnp.int32)
    sorted_gate = gate.reshape(n_slots)[order]
    counts = jnp.zeros((N_EXPERTS,), jnp.int32).at[flat_e].add(1)
    padded = (counts + EXPERT_BLOCK - 1) // EXPERT_BLOCK * EXPERT_BLOCK
    pad_end = jnp.cumsum(padded)
    pad_start = pad_end - padded
    start = jnp.cumsum(counts) - counts
    dest = pad_start[sorted_e] + jnp.arange(n_slots, dtype=jnp.int32) - start[sorted_e]
    n_blocks = -(-n_slots // EXPERT_BLOCK) + N_EXPERTS
    slot_tok = jnp.full((n_blocks * EXPERT_BLOCK,), t, jnp.int32).at[dest].set(sorted_tok)
    slot_gate = jnp.zeros((n_blocks * EXPERT_BLOCK,), xt.dtype).at[dest].set(sorted_gate.astype(xt.dtype))
    block_expert = jnp.minimum(jnp.searchsorted(pad_end, jnp.arange(n_blocks) * EXPERT_BLOCK, side='right'),
                               N_EXPERTS - 1).astype(jnp.int32)
    x_pad = jnp.concatenate([xt, jnp.zeros((1, d), xt.dtype)], axis=0)

    def body(y, blk):
        toks, gts, e = blk
        xb = x_pad[toks]
        h = jax.nn.silu(xb @ w_gate[e]) * (xb @ w_up[e])
        return y.at[toks].add((h @ w_down[e]) * gts[:, None]), None

    y, _ = lax.scan(body, jnp.zeros((t + 1, d), xt.dtype),
                    (slot_tok.reshape(n_blocks, EXPERT_BLOCK), slot_gate.reshape(n_blocks, EXPERT_BLOCK), block_expert))
    return y[:t]

def setup_inputs(seed: int = 0) -> dict:
    key = jax.random.key(seed)
    ks = iter(jax.random.split(key, 40))

    def nrm(shape, scale):
        return jax.random.normal(next(ks), shape, jnp.float32) * scale

    d, c, f, e = D_MODEL, MIX_WIDTH, EXPERT_FF, N_EXPERTS
    beta = DEEPNORM_BETA
    win_a = 2 * c + XATTN_WIDTH
    win_b = 3 * c + XATTN_WIDTH
    w_kv = jnp.concatenate([nrm((DEPTH, d, XATTN_WIDTH), d ** -0.5),
                            nrm((DEPTH, d, XATTN_WIDTH), d ** -0.5 * beta)], axis=-1)
    return {
        "x_prompt": nrm((BATCH, SEQ, d), 1.0),
        "x_sample": nrm((DEC_BATCH, DEC_SEQ, d), 1.0),
        "mem_prompt": nrm((BATCH, N_MEM, d), 1.0),
        "cache_mem_k": nrm((DEPTH, DEC_BATCH, N_MEM, N_XHEADS, XHEAD_DIM), 1.0),
        "cache_mem_v": nrm((DEPTH, DEC_BATCH, N_MEM, N_XHEADS, XHEAD_DIM), beta),
        "state_conv_a": nrm((N_A_LAYERS, DEC_BATCH, CONV_A_WIDTH - 1, c), 0.5),
        "state_conv_b": nrm((N_B_LAYERS, DEC_BATCH, CONV_B_WIDTH - 1, c), 0.5),
        "w_in_a": nrm((N_A_LAYERS, d, win_a), d ** -0.5),
        "conv_a_w": nrm((N_A_LAYERS, CONV_A_WIDTH, c), CONV_A_WIDTH ** -0.5),
        "conv_a_b": nrm((N_A_LAYERS, c), 0.02),
        "norm_a_g": 1.0 + nrm((N_A_LAYERS, c), 0.02),
        "norm_a_b": nrm((N_A_LAYERS, c), 0.02),
        "w_in_b": nrm((N_B_LAYERS, d, win_b), d ** -0.5),
        "conv_b_w": nrm((N_B_LAYERS, CONV_B_WIDTH, c), CONV_B_WIDTH ** -0.5),
        "w_kv": w_kv,
        "w_out": nrm((DEPTH, c + XATTN_WIDTH, d), (c + XATTN_WIDTH) ** -0.5 * beta),
        "ln1_g": 1.0 + nrm((DEPTH, d), 0.02),
        "ln1_b": nrm((DEPTH, d), 0.02),
        "w_router": nrm((DEPTH, d, e), d ** -0.5),
        "router_bias": nrm((DEPTH, e), 0.01),
        "w_gate": nrm((DEPTH, e, d, f), d ** -0.5),
        "w_up": nrm((DEPTH, e, d, f), d ** -0.5),
        "w_down": nrm((DEPTH, e, f, d), f ** -0.5 * beta),
        "ws_gate": nrm((DEPTH, d, SHARED_FF), d ** -0.5),
        "ws_up": nrm((DEPTH, d, SHARED_FF), d ** -0.5),
        "ws_down": nrm((DEPTH, SHARED_FF, d), SHARED_FF ** -0.5 * beta),
        "ln2_g": 1.0 + nrm((DEPTH, d), 0.02),
        "ln2_b": nrm((DEPTH, d), 0.02),
    }

def reference(x_prompt, x_sample, mem_prompt, cache_mem_k, cache_mem_v, state_conv_a, state_conv_b,
              w_in_a, conv_a_w, conv_a_b, norm_a_g, norm_a_b, w_in_b, conv_b_w, w_kv, w_out, ln1_g, ln1_b,
              w_router, router_bias, w_gate, w_up, w_down, ws_gate, ws_up, ws_down, ln2_g, ln2_b):
    c = MIX_WIDTH

    def token_sublayer(x, hist, mem_k, mem_v, i):
        j = i // N_MIXERS
        if i % N_MIXERS == 0:
            u = x @ w_in_a[j]
            a, g, q = jnp.split(u, [c, 2 * c], axis=-1)
            conv, new_hist = causal_depthwise_conv(a * jax.nn.sigmoid(g), hist, conv_a_w[j])
            mix = jax.nn.silu(layer_norm(conv + conv_a_b[j], norm_a_g[j], norm_a_b[j]))
        else:
            u = x @ w_in_b[j]
            b_gate, c_gate, h, q = jnp.split(u, [c, 2 * c, 3 * c], axis=-1)
            conv, new_hist = causal_depthwise_conv(c_gate * h, hist, conv_b_w[j])
            mix = b_gate * conv
        attn = memory_attention(q, mem_k, mem_v)
        out = jnp.concatenate([mix, attn], axis=-1) @ w_out[i]
        return layer_norm(DEEPNORM_ALPHA * x + out, ln1_g[i], ln1_b[i]), new_hist

    def channel_sublayer(x, i):
        xt = x.reshape(-1, x.shape[-1])
        idx, gate = route(xt, w_router[i], router_bias[i])
        shared = (jax.nn.silu(xt @ ws_gate[i]) * (xt @ ws_up[i])) @ ws_down[i]
        y = routed_experts(xt, idx, gate, w_gate[i], w_up[i], w_down[i]) + shared
        return layer_norm(DEEPNORM_ALPHA * x + y.reshape(x.shape), ln2_g[i], ln2_b[i])

    hp, hs = x_prompt, x_sample
    new_k, new_v = [], []
    conv_a_p, conv_b_p, conv_a_s, conv_b_s = [], [], [], []
    for i in range(DEPTH):
        j = i // N_MIXERS
        kv = mem_prompt @ w_kv[i]
        k_p = kv[..., :XATTN_WIDTH].reshape(kv.shape[0], kv.shape[1], N_XHEADS, XHEAD_DIM)
        v_p = kv[..., XATTN_WIDTH:].reshape(kv.shape[0], kv.shape[1], N_XHEADS, XHEAD_DIM)
        new_k.append(k_p)
        new_v.append(v_p)
        is_a = i % N_MIXERS == 0
        width = CONV_A_WIDTH if is_a else CONV_B_WIDTH
        hist_s = state_conv_a[j] if is_a else state_conv_b[j]
        zero_hist = jnp.zeros((hp.shape[0], width - 1, c), hp.dtype)
        hp, hist_p_new = token_sublayer(hp, zero_hist, k_p, v_p, i)
        hs, hist_s_new = token_sublayer(hs, hist_s, cache_mem_k[i], cache_mem_v[i], i)
        if is_a:
            conv_a_p.append(hist_p_new)
            conv_a_s.append(hist_s_new)
        else:
            conv_b_p.append(hist_p_new)
            conv_b_s.append(hist_s_new)
        hp = channel_sublayer(hp, i)
        hs = channel_sublayer(hs, i)

    return (hp, hs, jnp.stack(new_k), jnp.stack(new_v), jnp.stack(conv_a_p), jnp.stack(conv_b_p),
            jnp.stack(conv_a_s), jnp.stack(conv_b_s))


_drawn_inputs = setup_inputs


def setup_inputs(seed=0):
    import zlib

    import numpy as np

    out = dict(_drawn_inputs(seed))
    spreads = {}
    factors = {'norm_a_b': 2.751}
    for name, (base, spread) in spreads.items():
        noise = np.random.default_rng([zlib.crc32(name.encode()), seed]).standard_normal(out[name].shape)
        drawn = base * np.exp(spread * noise) if base else spread * noise
        out[name] = __import__('jax').numpy.asarray(drawn.astype(out[name].dtype))
    for name, factor in factors.items():
        out[name] = (out[name] * factor).astype(out[name].dtype)
    return out
```

```python
from contextlib import ExitStack

import concourse.bass as bass
from concourse import mybir

F32 = mybir.dt.float32
F32R = mybir.dt.float32r
I32 = mybir.dt.int32
ALU = mybir.AluOpType
ACT = mybir.ActivationFunctionType
AX = mybir.AxisListType

P = 128
D = 1024
C = D // P
SEQ, NB, NS = 256, 8, 4
TOK = SEQ + NB * NS
ROWS = [P, P, NB * NS]
START = [0, P, 2 * P]
T = len(ROWS)
CH = 512
CC = CH // P
H, HD, MEM = 4, 128, 256
DEPTH = 2
ALPHA = (2 * DEPTH) ** 0.25
EPS = 1e-5
SCALE = HD ** -0.5
WIDTH = [31, 3]
E, FF = 64, 256
GROUPS, TOP_GROUPS, ROUTED = 8, 4, 2.5
PAIRS = E // 2
WIN = 64
PASSES = -(-TOK // WIN)
NPARAM = [34, 3]
BIG = 1e30
SLOTS = 6
MIX_TILES = [13, 14]
FIRST_TILE = [0, MIX_TILES[0] + 3 * PAIRS]
BANKS = 7


def job_list(layer):
    jobs = [(("xT", t, hf), "act" if hf == 0 else "dve") for t in range(T) for hf in range(2)]
    jobs += [(("params",), "act")] + [(("hist", q), "dve") for q in range(2 if layer == 0 else 1)]
    if layer == 0:
        jobs += [(("g", m), "act") for m in range(4)] + [(("a", m), "dve") for m in range(4)]
    else:
        jobs += [(("c", m), "act") for m in range(4)] + [(("h", m), "dve") for m in range(4)]
        jobs += [(("b", m), "act") for m in range(4)]
    jobs += [(("q", m), "act") for m in range(4)]
    jobs += [(("newp",), "act"), (("news",), "act")]
    jobs += [(("memT", m, hf), "act" if hf == 0 else "dve") for m in range(2) for hf in range(2)]
    jobs += [(("kv", n, m), "act") for n in range(2) for m in range(2)]
    jobs += [(("kT", hp), "dve") for hp in range(2)]
    jobs += [(("sc", hp, t), "act") for hp in range(2) for t in range(2)]
    jobs += [(("PT", h), "dve") for h in range(H)]
    jobs += [(("o", h), "act") for h in range(H)]
    jobs += [(("KT", b, hp), "act" if hp == 0 else "dve") for b in range(NB) for hp in range(2)]
    jobs += [(("scs",), "act"), (("PTs",), "dve"), (("os",), "act")]
    if layer == 0:
        jobs += [(("mean",), "dve"), (("var",), "act")]
    jobs += [(("out", n, t), "dve") for n in range(2) for t in range(T)]
    jobs += [(("x1T", t, hf), "act" if hf == 0 else "dve") for t in range(T) for hf in range(2)]
    jobs += [(("logits", t), "act") for t in range(T)]
    jobs += [(("sgate", f), "act") for f in range(2)] + [(("sup", f), "dve") for f in range(2)]
    jobs += [(("sdown", t, n), "dve") for t in range(T) for n in range(2)]
    jobs += [(("rank", t), "dve") for t in range(T)] + [(("count",), "dve")]
    return jobs


def number_jobs():
    table, count, turn = {}, {"pe": 0, "act": 0, "dve": 0}, 0
    for layer in range(DEPTH):
        holder = {}
        for name, drainer in job_list(layer):
            if name == ("scs",):
                bank = BANKS
            else:
                bank, turn = turn % BANKS, turn + 1
            count["pe"] += 1
            count[drainer] += 1
            table[(layer, *name)] = (bank, count["pe"], drainer, count[drainer], holder.get(bank))
            holder[bank] = (layer, *name)
    return table


JOBS = number_jobs()


def build_program(nc, I, O):
    with ExitStack() as ctx:
        sem = lambda name: ctx.enter_context(nc.semaphore(name))
        sb = lambda name, shape, dt=F32: ctx.enter_context(nc.sbuf_tensor(name, shape, dt))

        ring = sb("ring", [P, SLOTS, 4096])
        x = sb("x", [P, T, D])
        y = sb("y", [P, T, D])
        xT = sb("xT", [P, C, TOK])
        lnp = sb("lnp", [P, 2, D])
        ident = sb("ident", [P, P])
        tri = sb("tri", [P, P])
        ones = sb("ones", [P, P])
        eps = sb("eps", [P, 1])
        iota_win = sb("iota_win", [P, WIN])
        iota_tok = sb("iota_tok", [P, TOK])
        valid = sb("valid", [P, T])
        tokid = sb("tokid", [P, T])
        thresholds = sb("thresholds", [1, PASSES - 1])
        passes = sb("passes", [1, DEPTH], I32)
        passes_f = sb("passes_f", [1, 8])
        bn = sb("bn", [P, T, 2, 6])
        mv = sb("mv", [P, T, 2])
        rstd = sb("rstd", [P, T])
        top = sb("top", [P, T, 9, 8])
        grp = sb("grp", [P, T, 12])
        grpr = sb("grpr", [P, T, 12])
        gsum = sb("gsum", [P, T])
        mx = sb("mx", [P, 10])
        sums = sb("sums", [P, 10])

        mix = ExitStack()
        mb = lambda name, shape, dt=F32: mix.enter_context(nc.sbuf_tensor(name, shape, dt))
        cb = mb("cb", [P, CC, 558])
        catT = mb("catT", [P, C, TOK])
        kv = mb("kv", [P, 2, D])
        memT = mb("memT", [P, C, MEM])
        kT = mb("kT", [P, H, MEM])
        qm = mb("qm", [P, H, 288])
        prow = mb("prow", [34, CH])
        Ps = mb("Ps", [P, MEM])
        PTs = mb("PTs", [P, 2, P])
        pcol = mb("pcol", [P, CC, 34])
        sig = mb("sig", [P, CC, TOK])
        ct = mb("ct", [P, CC, TOK])
        qT = mb("qT", [P, H, TOK])
        wr = mb("wr", [P, C, E])
        rb = mb("rb", [P, E])
        mix.close()
        PT = memT.rearrange("p (h m) q -> p h m q", h=H)
        Pm = y[:, 0:2, :].rearrange("p t (h q) -> p t h q", h=H)
        KT = [xT[:, :, :].rearrange("p c q -> p (c q)")[:, 1024 * b:1024 * b + 1024]
              .rearrange("p (h q) -> p h q", h=H) for b in range(2)]

        new_cols = lambda n: PTs[:, :, :].rearrange("p m q -> p (m q)")[:, 0:CC * NB * n].rearrange(
            "p (c s) -> p c s", c=CC)

        xh = sb("xh", [P, T, C, P], F32R)
        xl = sb("xl", [P, T, C, P], F32R)
        slots = sb("slots", [P, PAIRS + 1, 12])
        score = sb("score", [P, T, E])
        cand = sb("cand", [P, T, E])
        mask = sb("mask", [P, T, E])
        gates = sb("gates", [P, T, E])
        xs = sb("xs", [P, 2, C, P])
        yh = sb("yh", [P, D], F32R)
        yl = sb("yl", [P, D], F32R)
        sel = sb("sel", [P, 2, T, P], F32R)
        back = sb("back", [P, 2, TOK], F32R)
        cols = sb("cols", [P, 2, T, 5])
        slotv = sb("slotv", [P, 2, 5])
        slotg = sb("slotg", [P, 2])
        sg = sb("sg", [P, FF])
        hs = sb("hs", [P, FF])
        hT = sb("hT", [P, 2, P])
        window = sb("window", [P, WIN])

        ps = ctx.enter_context(nc.psum_tensor("ps", [P, 8, 512], F32))
        GATHER, GU, SMALL, DOWN, COMBINE = 0, 2, 3, 4, 6

        x_loaded = sem("x_loaded")
        mem_loaded = [sem(f"mem_loaded{layer}") for layer in range(DEPTH)]
        small_loaded = sem("small_loaded")
        ln_loaded = sem("ln_loaded")
        landed = [sem(f"landed{s}") for s in range(SLOTS)]
        tile_used = sem("tile_used")
        consts_ready = sem("consts_ready")
        pool_seq = sem("pool_seq")
        filled = sem("filled")
        drained = {"act": sem("drained_act"), "dve": sem("drained_dve")}
        dve_seq = sem("dve_seq")
        glu_ready = sem("glu_ready")
        max_ready = sem("max_ready")
        prob_ready = sem("prob_ready")
        qmask_ready = sem("qmask_ready")
        centred = sem("centred")
        var_ready = sem("var_ready")
        rstd_ready = sem("rstd_ready")
        ln_done = sem("ln_done")
        conv_ready = sem("conv_ready")
        mix_ready = sem("mix_ready")
        hi_ready = sem("hi_ready")
        lo_ready = sem("lo_ready")
        mask_ready = sem("mask_ready")
        shared_h = sem("shared_h")
        passes_ready = sem("passes_ready")
        stored = sem("stored")
        y_stored = sem("y_stored")
        hist_stored = sem("hist_stored")
        cols_ready = sem("cols_ready")
        sel_built = sem("sel_built")
        gathered = sem("gathered")
        slotv_mm = sem("slotv_mm")
        xs_ready = sem("xs_ready")
        slotv_ready = sem("slotv_ready")
        slots_ready = sem("slots_ready")
        silu_done = sem("silu_done")
        h_done = sem("h_done")
        hT_done = sem("hT_done")
        hT_copied = sem("hT_copied")
        yh_done = sem("yh_done")
        yl_done = sem("yl_done")
        combined = sem("combined")
        added = sem("added")
        more_sems = [{n: sem(f"more_{n}{layer}") for n in (
            "landed", "slotm", "cols", "sel", "gathered", "xs", "slotv", "slots", "gate", "up", "silu", "h", "hT",
            "hTc", "down", "yh", "yl", "combined", "added", "shift")} for layer in range(DEPTH)]

        def wait(eng, s, v):
            if not isinstance(v, int) or v > 0:
                eng.wait_ge(s, v)

        def psum_of(layer, *name):
            return ps[:, JOBS[(layer, *name)][0], :]

        def wait_filled(eng, layer, *name):
            eng.wait_ge(filled, JOBS[(layer, *name)][1])

        def wait_drained(eng, layer, *name):
            _, _, drainer, n, _ = JOBS[(layer, *name)]
            eng.wait_ge(drained[drainer], n)

        uses = [0] * SLOTS
        landing = {}

        def tile_plan():
            for layer in range(DEPTH):
                g = FIRST_TILE[layer]
                for n in range(MIX_TILES[layer]):
                    uses[(g + n) % SLOTS] += 2 if n == MIX_TILES[layer] - 2 else 1
                    landing[g + n] = 16 * uses[(g + n) % SLOTS]
                for n in range(MIX_TILES[layer], MIX_TILES[layer] + 3 * PAIRS):
                    uses[(g + n) % SLOTS] += 1
                    landing[g + n] = 16 * uses[(g + n) % SLOTS]

        tile_plan()

        def tile_at(layer, n):
            return ring[:, (FIRST_TILE[layer] + n) % SLOTS, :]

        def wait_tile(eng, layer, n):
            g = FIRST_TILE[layer] + n
            eng.wait_ge(landed[g % SLOTS], landing[g])

        N_IN = [3, 4]

        def tile_no(layer, what, i=0):
            order = {"in": 0, "kv": N_IN[layer], "K": N_IN[layer] + 2, "V": N_IN[layer] + 4,
                     "out": N_IN[layer] + 6, "sgu": N_IN[layer] + 8, "sd": N_IN[layer] + 9}
            return order[what] + i

        def last_job(layer, n):
            n -= N_IN[layer]
            if n < 0:
                return (["g", "a", "q"] if layer == 0 else ["c", "h", "b", "q"])[n], 3
            return [("kv", 0, 1), ("kv", 1, 1), ("KT", 3, 1), ("KT", 7, 1), ("os",), ("os",), ("out", 0, T - 1),
                    ("out", 1, T - 1), ("sup", 1), ("sdown", T - 1, 1)][n]

        def wait_tile_used(eng, g):
            if g < 0:
                return
            layer = int(g >= FIRST_TILE[1])
            n = g - FIRST_TILE[layer]
            if n < MIX_TILES[layer]:
                wait_filled(eng, layer, *last_job(layer, n))
            else:
                eng.wait_ge(tile_used, 3 * PAIRS * layer + n - MIX_TILES[layer] + 1)

        IN_COLS = [[1, 0, 2], [1, 2, 0, 3]]
        w_in = [I["w_in_a"][0].rearrange("(p c) n -> p c n", c=C), I["w_in_b"][0].rearrange("(p c) n -> p c n", c=C)]
        experts = {}
        for layer in range(DEPTH):
            experts[layer] = [I["w_gate"][layer].rearrange("e (p c) f -> e p (c f)", c=C),
                              I["w_up"][layer].rearrange("e (p c) f -> e p (c f)", c=C),
                              I["w_down"][layer].rearrange("e (p c) d -> e p (c d)", c=2)]

        conv_end = []
        block = ctx.enter_context(nc.Block())

        @block.sync
        def _(sp):
            sp.dma_start(x[:, 0:2, :], I["x_prompt"][0].rearrange("(t p) d -> p t d", p=P)).then_inc(x_loaded, 16)
            sp.dma_start(x[0:ROWS[2], 2, :], I["x_sample"].rearrange("b s d -> (b s) d")).then_inc(x_loaded, 16)

            def load_tile(layer, n):
                g = FIRST_TILE[layer] + n
                dst = ring[:, g % SLOTS, :]
                wait_tile_used(sp, g - SLOTS)
                if n < N_IN[layer]:
                    m = IN_COLS[layer][n]
                    sp.dma_start(dst.rearrange("p (c n) -> p c n", c=C),
                                 w_in[layer][:, :, 512 * m:512 * m + 512]).then_inc(landed[g % SLOTS], 16)
                    return
                n -= N_IN[layer]
                if n < 2:
                    sp.dma_start(dst.rearrange("p (c n) -> p c n", c=C),
                                 I["w_kv"][layer].rearrange("(p c) n -> p c n", c=C)[:, :, 512 * n:512 * n + 512]
                                 ).then_inc(landed[g % SLOTS], 16)
                elif n < 6:
                    cache = I["cache_mem_k"] if n < 4 else I["cache_mem_v"]
                    b = 4 * (n % 2)
                    sp.dma_start(dst.rearrange("p (b n) -> p b n", b=4),
                                 cache[layer, b:b + 4].rearrange("b (p m) h d -> p b (m h d)", m=2)
                                 ).then_inc(landed[g % SLOTS], 16)
                elif n < 8:
                    sp.dma_start(dst.rearrange("p (c n) -> p c n", c=C),
                                 I["w_out"][layer].rearrange("(c p) n -> p c n", c=C)[:, :, 512 * (n - 6):512 * (n - 5)]
                                 ).then_inc(landed[g % SLOTS], 16)
                elif n == 8:
                    for i, w in enumerate(("ws_gate", "ws_up")):
                        sp.dma_start(dst[:, 2048 * i:2048 * i + 2048],
                                     I[w][layer].rearrange("(p c) f -> p (c f)", c=C)).then_inc(landed[g % SLOTS], 16)
                else:
                    sp.dma_start(dst[:, 0:2048], I["ws_down"][layer].rearrange("(p c) d -> p (c d)", c=2)
                                 ).then_inc(landed[g % SLOTS], 16)

            for layer in range(DEPTH):
                more = more_sems[layer]
                for n in range(MIX_TILES[layer]):
                    load_tile(layer, n)
                    if layer == 0 and n == 0:
                        sp.dma_start(kv[:, :, :], I["mem_prompt"][0].rearrange("(m p) d -> p m d", p=P)
                                     ).then_inc(mem_loaded[0], 16)
                g0 = FIRST_TILE[layer] + MIX_TILES[layer]

                def load_pair(k, b, c):
                    g = g0 + 3 * b + c
                    sp.dma_start(ring[:, g % SLOTS, :].rearrange("p (e n) -> p e n", e=2),
                                 experts[layer][c][bass.ds(2 * k, 2)].rearrange("e p n -> p e n")
                                 ).then_inc(landed[g % SLOTS], 16)

                for b in range(2):
                    for c in range(3):
                        wait_tile_used(sp, g0 + 3 * b + c - SLOTS)
                        load_pair(b, b, c)
                with sp.Fori(1, PAIRS // 2) as j:
                    for b in range(2):
                        for c in range(3):
                            sp.wait_ge(tile_used, 3 * PAIRS * layer - 5 + 6 * j + 3 * b + c)
                            load_pair(2 * j + b, b, c)
                sp.wait_ge(passes_ready, layer + 1)
                npass = sp.value_load(passes[0:1, layer:layer + 1], min_val=1, max_val=PASSES)
                with sp.If(npass > 1):
                    sp.wait_ge(added, 6 * PAIRS * (layer + 1))
                    with sp.Fori(1, npass) as p:
                        with sp.Fori(0, PAIRS) as k:
                            sp.wait_ge(more["added"], 6 * PAIRS * (p - 1) + 6 * k + 1)
                            for c in range(3):
                                sp.dma_start(ring[:, c, :].rearrange("p (e n) -> p e n", e=2),
                                             experts[layer][c][bass.ds(2 * k, 2)].rearrange("e p n -> p e n")
                                             ).then_inc(more["landed"], 16)
                    sp.wait_ge(ln_done, T * (2 * layer + 2))
            sp.wait_ge(ln_done, 3 * 2 * DEPTH)
            sp.dma_start(O[0][0].rearrange("(t p) d -> p t d", p=P), x[:, 0:2, :]).then_inc(y_stored, 16)
            sp.dma_start(O[1].rearrange("b s d -> (b s) d"), x[0:ROWS[2], 2, :]).then_inc(y_stored, 16)
            sp.wait_ge(y_stored, 32)
            sp.wait_ge(stored, 16 * 4 * DEPTH)
            sp.wait_ge(hist_stored, 16)

        @block.gpsimd
        def _(pool):
            def load_small(layer):
                if layer == 0:
                    pool.dma_start(prow[0:31, :], I["conv_a_w"][0]).then_inc(small_loaded, 16)
                    pool.dma_start(prow[31:32, :], I["conv_a_b"]).then_inc(small_loaded, 16)
                    pool.dma_start(prow[32:33, :], I["norm_a_g"]).then_inc(small_loaded, 16)
                    pool.dma_start(prow[33:34, :], I["norm_a_b"]).then_inc(small_loaded, 16)
                    pool.dma_start(y[0:120, 2, :].rearrange("r (q n) -> r q n", q=2),
                                   I["state_conv_a"][0].rearrange("(q b) r n -> (b r) q n", q=2)
                                   ).then_inc(small_loaded, 16)
                else:
                    pool.dma_start(prow[0:3, :], I["conv_b_w"][0]).then_inc(small_loaded, 16)
                    pool.dma_start(y[0:16, 2, 0:CH], I["state_conv_b"][0].rearrange("b r n -> (b r) n")
                                   ).then_inc(small_loaded, 16)
                pool.dma_start(wr[:, :, :], I["w_router"][layer].rearrange("(p c) e -> p c e", c=C)
                               ).then_inc(small_loaded, 16)
                pool.dma_start(rb[:, :], I["router_bias"][layer:layer + 1, :].to_broadcast([P, E])
                               ).then_inc(small_loaded, 16)

            def load_norm(q):
                g, b = (I["ln1_g"], I["ln1_b"]) if q % 2 == 0 else (I["ln2_g"], I["ln2_b"])
                pool.dma_start(lnp[:, 0, :], g[q // 2:q // 2 + 1, :].to_broadcast([P, D])).then_inc(ln_loaded, 16)
                pool.dma_start(lnp[:, 1, :], b[q // 2:q // 2 + 1, :].to_broadcast([P, D])).then_inc(ln_loaded, 16)

            pool.memset(ident[:, :], 0.0).then_inc(pool_seq, 1)
            pool.memset(ones[:, :], 1.0).then_inc(pool_seq, 1)
            pool.memset(valid[:, :], 1.0).then_inc(pool_seq, 1)
            pool.memset(eps[:, :], EPS)
            pool.iota(iota_win[:, :], pattern=[[1, WIN]], base=0, channel_multiplier=0,
                      allow_small_or_imprecise_dtypes=True)
            pool.iota(iota_tok[:, :], pattern=[[1, TOK]], base=1, channel_multiplier=0,
                      allow_small_or_imprecise_dtypes=True)
            pool.iota(tokid[:, :], pattern=[[P, T]], base=1, channel_multiplier=1,
                      allow_small_or_imprecise_dtypes=True)
            pool.iota(thresholds[:, :], pattern=[[WIN, PASSES - 1]], base=WIN, channel_multiplier=0,
                      allow_small_or_imprecise_dtypes=True)
            pool.wait_ge(pool_seq, 3)
            pool.affine_select(out=ident[:, :], in_=ident[:, :], compare_op=ALU.not_equal, fill=1.0, base=0,
                               pattern=[[-1, P]], channel_multiplier=1)
            pool.affine_select(out=tri[:, :], in_=ones[:, :], compare_op=ALU.is_gt, fill=0.0, base=0,
                               pattern=[[1, P]], channel_multiplier=-1)
            pool.affine_select(out=valid[:, 2:3], in_=valid[:, 2:3], compare_op=ALU.is_gt, fill=0.0,
                               base=ROWS[2], pattern=[[0, 1]], channel_multiplier=-1).then_inc(consts_ready, 1)
            load_small(0)
            load_norm(0)
            pool.dma_start(O[6][0, :, 0:26, :], I["state_conv_a"][0, :, 4:30, :]).then_inc(hist_stored, 16)

            for layer in range(DEPTH):
                if layer == 1:
                    pool.wait_ge(ln_done, 6 * layer)
                    pool.dma_start(kv[:, :, :], I["mem_prompt"][0].rearrange("(m p) d -> p m d", p=P)
                                   ).then_inc(mem_loaded[1], 16)
                    load_small(1)
                newp, news = (O[4], O[6]) if layer == 0 else (O[5], O[7])
                np_, ns_ = (30, 4) if layer == 0 else (2, 2)
                wait_drained(pool, layer, "newp")
                pool.dma_start(newp[0, 0], y[0:np_, 2, 0:CH]).then_inc(stored, 16)
                wait_drained(pool, layer, "news")
                dst = news[0, :, 26:30, :] if layer == 0 else news[0]
                pool.dma_start(dst, y[0:NB * ns_, 2, CH:2 * CH]).then_inc(stored, 16)
                wait_drained(pool, layer, "kv", 0, 1)
                pool.dma_start(O[2][layer, 0].rearrange("(m p) h d -> p m (h d)", p=P), kv[:, :, 0:CH]
                               ).then_inc(stored, 16)
                wait_drained(pool, layer, "kv", 1, 1)
                pool.dma_start(O[3][layer, 0].rearrange("(m p) h d -> p m (h d)", p=P), kv[:, :, CH:2 * CH]
                               ).then_inc(stored, 16)
                pool.wait_ge(ln_done, T * (2 * layer + 1))
                load_norm(2 * layer + 1)
                if layer + 1 < DEPTH:
                    pool.wait_ge(ln_done, T * (2 * layer + 2))
                    load_norm(2 * layer + 2)

        @block.scalar
        def _(act):
            copy = lambda out, in_: act.activation(out, in_, ACT.Copy)

            def norm_std(q):
                for t in range(T):
                    act.wait_ge(var_ready, T * q + t + 1)
                    act.activation(rstd[0:ROWS[t], t:t + 1], mv[0:ROWS[t], t, 1:2], ACT.Sqrt,
                                   bias=eps[0:ROWS[t], :]).then_inc(rstd_ready, 1)

            def drain(layer, *name):
                wait_filled(act, layer, *name)
                return psum_of(layer, *name)

            act.wait_ge(consts_ready, 1)
            for layer in range(DEPTH):
                more = more_sems[layer]
                done = drained["act"]
                for t in range(T):
                    b = drain(layer, "xT", t, 0)
                    r = ROWS[t]
                    copy(xT[:, 0:4, START[t]:START[t] + r], b[:, 0:4 * r].rearrange("p (c r) -> p c r", c=4)).then_inc(done, 1)
                b = drain(layer, "params")
                n = NPARAM[layer]
                copy(pcol[:, :, 0:n], b[:, 0:CC * n].rearrange("p (c n) -> p c n", c=CC)).then_inc(done, 1)
                if layer == 0:
                    for m in range(4):
                        b = drain(layer, "g", m)
                        act.activation(sig[:, m, :], b[:, 0:TOK], ACT.Sigmoid).then_inc(done, 1)
                else:
                    for m in range(4):
                        b = drain(layer, "c", m)
                        copy(sig[:, m, :], b[:, 0:TOK]).then_inc(done, 1)
                    for m in range(4):
                        b = drain(layer, "b", m)
                        copy(ct[:, m, :], b[:, 0:TOK]).then_inc(done, 1)
                for m in range(4):
                    b = drain(layer, "q", m)
                    copy(qT[:, m, :], b[:, 0:TOK]).then_inc(done, 1)
                np_, ns_ = (30, 32) if layer == 0 else (2, 16)
                b = drain(layer, "newp")
                copy(y[0:np_, 2, 0:CH], b[0:np_, :]).then_inc(done, 1)
                b = drain(layer, "news")
                copy(y[0:ns_, 2, CH:2 * CH], b[0:ns_, :]).then_inc(done, 1)
                for m in range(2):
                    b = drain(layer, "memT", m, 0)
                    copy(memT[:, 0:4, P * m:P * m + P], b.rearrange("p (c r) -> p c r", c=4)).then_inc(done, 1)
                for n in range(2):
                    for m in range(2):
                        b = drain(layer, "kv", n, m)
                        if n == 0 and m == 0:
                            wait_filled(act, layer, "memT", 1, 1)
                        copy(kv[:, m, 512 * n:512 * n + 512], b).then_inc(done, 1)
                for j, (hp, t) in enumerate([(hp, t) for hp in range(2) for t in range(2)]):
                    act.wait_ge(max_ready, 5 * layer + j + 1)
                    b = psum_of(layer, "sc", hp, t)
                    for i in range(2):
                        k = 2 * j + i
                        ins = act.activation(Pm[:, t, 2 * hp + i, :], b[:, MEM * i:MEM * i + MEM], ACT.Exp,
                                             bias=mx[:, k:k + 1], scale=SCALE, accum_out=sums[:, k:k + 1])
                    ins.then_inc(done, 1)
                for h in range(H):
                    b = drain(layer, "o", h)
                    copy(catT[:, CC + h, 0:SEQ], b[:, 0:SEQ]).then_inc(done, 1)
                for s in range(NB):
                    b = drain(layer, "KT", s, 0)
                    copy(KT[s % 2][:, 0:2, :], b.rearrange("p (h q) -> p h q", h=2)).then_inc(done, 1)
                act.wait_ge(max_ready, 5 * layer + 5)
                act.activation(Ps[:, :], ps[:, BANKS, 0:MEM], ACT.Exp, bias=mx[:, 8:9], scale=SCALE,
                               accum_out=sums[:, 8:9]).then_inc(done, 1)
                b = drain(layer, "os")
                copy(catT[:, CC:C, SEQ:TOK], b[:, 0:H * 32].rearrange("p (h q) -> p h q", h=H)).then_inc(done, 1)
                if layer == 0:
                    b = drain(layer, "var")
                    act.activation(sig[:, 1, :], b[:, 0:TOK], ACT.Sqrt, bias=eps[:, :], scale=1.0 / CH).then_inc(done, 1)
                    for cc in range(CC):
                        act.wait_ge(conv_ready, cc + 1)
                        act.activation(catT[:, cc, :], ct[:, cc, :], ACT.Silu, bias=pcol[:, cc, 33:34],
                                       scale=pcol[:, cc, 32:33]).then_inc(mix_ready, 1)
                norm_std(2 * layer)
                act.wait_ge(stored, 16 * (4 * layer + 4))
                for t in range(T):
                    b = drain(layer, "x1T", t, 0)
                    r = ROWS[t]
                    copy(xT[:, 0:4, START[t]:START[t] + r], b[:, 0:4 * r].rearrange("p (c r) -> p c r", c=4)).then_inc(done, 1)
                    copy(xh[0:r, t, :, :], x[0:r, t, :].rearrange("p (j c) -> p c j", c=C)).then_inc(hi_ready, 1)
                for t in range(T):
                    b = drain(layer, "logits", t)
                    act.activation(score[0:ROWS[t], t, :], b[0:ROWS[t], 0:E], ACT.Sigmoid).then_inc(done, 1)
                for f in range(2):
                    b = drain(layer, "sgate", f)
                    act.activation(sig[:, f, :], b[:, 0:TOK], ACT.Silu).then_inc(done, 1)

                def copy_xs(k, b):
                    act.wait_ge(gathered, (PAIRS + 1) * layer + k + 1)
                    copy(xs[:, b, :, :].rearrange("p c s -> p (c s)"),
                         ps[:, GATHER:GATHER + 2, :].rearrange("p b n -> p (b n)")).then_inc(xs_ready, 1)

                def round_y(k):
                    act.wait_ge(tile_used, 3 * PAIRS * layer + 3 * k + 3)
                    copy(yh[:, :], ps[:, DOWN:DOWN + 2, :].rearrange("p b n -> p (b n)")).then_inc(yh_done, 1)

                def step(k, b):
                    act.wait_ge(tile_used, 3 * PAIRS * layer + 3 * k + 2)
                    act.activation(sg[:, :], ps[:, GU, 0:FF], ACT.Silu).then_inc(silu_done, 1)
                    copy_xs(k + 1, 1 - b)
                    act.wait_ge(hT_done, PAIRS * layer + k + 1)
                    copy(hT[:, :, :], ps[:, SMALL, 0:FF].rearrange("p (f s) -> p f s", f=2)).then_inc(hT_copied, 1)

                copy_xs(0, 0)
                step(0, 0)
                round_y(0)
                step(1, 1)
                with act.Fori(1, PAIRS // 2) as j:
                    for b in range(2):
                        round_y(2 * j + (b - 1))
                        step(2 * j + b, b)
                round_y(PAIRS - 1)

                act.wait_ge(passes_ready, layer + 1)
                npass = act.value_load(passes[0:1, layer:layer + 1], min_val=1, max_val=PASSES)
                with act.If(npass > 1):
                    with act.Fori(1, npass) as p:
                        with act.Fori(0, PAIRS) as k:
                            n = (p - 1) * PAIRS + k
                            act.wait_ge(more["gathered"], n + 1)
                            copy(xs[:, 0, :, :].rearrange("p c s -> p (c s)"),
                                 ps[:, GATHER:GATHER + 2, :].rearrange("p b n -> p (b n)")).then_inc(more["xs"], 1)
                            act.wait_ge(more["up"], n + 1)
                            act.activation(sg[:, :], ps[:, GU, 0:FF], ACT.Silu).then_inc(more["silu"], 1)
                            act.wait_ge(more["hT"], n + 1)
                            copy(hT[:, :, :], ps[:, SMALL, 0:FF].rearrange("p (f s) -> p f s", f=2)
                                 ).then_inc(more["hTc"], 1)
                            act.wait_ge(more["down"], n + 1)
                            copy(yh[:, :], ps[:, DOWN:DOWN + 2, :].rearrange("p b n -> p (b n)")
                                 ).then_inc(more["yh"], 1)
                norm_std(2 * layer + 1)

        @block.vector
        def _(dve):
            links = [0]

            def link(ins):
                links[0] += 1
                ins.then_inc(dve_seq, 1)
                dve.wait_ge(dve_seq, links[0])

            done = drained["dve"]

            def drain(layer, *name):
                wait_filled(dve, layer, *name)
                return psum_of(layer, *name)

            def bcast(ap, shape):
                return ap.to_broadcast(shape)

            def conv_parts(layer):
                w = WIDTH[layer]
                return w, SEQ + w - 1, NS + w - 1

            def conv_taps(layer, cc, j0, j1):
                w, pw, sw = conv_parts(layer)
                for j in range(j0, j1):
                    for part in range(2):
                        if part == 0:
                            out = catT[:, cc, 0:SEQ]
                            src = cb[:, cc, j:j + SEQ]
                        else:
                            out = catT[:, cc, SEQ:TOK].rearrange("p (b s) -> p b s", b=NB)
                            src = cb[:, cc, pw:pw + NB * sw].rearrange("p (b s) -> p b s", b=NB)[:, :, j:j + NS]
                        if j == 0 and layer == 0:
                            ins = dve.tensor_scalar(out, src, pcol[:, cc, 0:1], pcol[:, cc, 31:32], ALU.mult, ALU.add)
                        elif j == 0:
                            ins = dve.tensor_scalar(out, src, pcol[:, cc, 0:1], None, ALU.mult)
                        else:
                            dve.wait_ge(dve_seq, links[0] - 1)
                            ins = dve.scalar_tensor_tensor(out, src, pcol[:, cc, j:j + 1], out, ALU.mult, ALU.add)
                        ins.then_inc(dve_seq, 1)
                        links[0] += 1

            def normalise(q, src):
                for t in range(T):
                    r = ROWS[t]
                    for i in range(2):
                        ins = dve.bn_stats(bn[0:r, t, i, :], src[0:r, t, 512 * i:512 * i + 512])
                    link(ins)
                    dve.bn_aggr(mv[0:r, t, :], bn[0:r, t, :, :].rearrange("p a b -> p (a b)")).then_inc(var_ready, 1)
                dve.wait_ge(ln_loaded, 32 * (q + 1))
                for t in range(T):
                    r = ROWS[t]
                    dve.wait_ge(var_ready, T * q + t + 1)
                    dve.wait_ge(rstd_ready, T * q + t + 1)
                    link(dve.reciprocal(rstd[0:r, t:t + 1], rstd[0:r, t:t + 1]))
                    link(dve.tensor_scalar(x[0:r, t, :], src[0:r, t, :], mv[0:r, t, 0:1], rstd[0:r, t:t + 1],
                                           ALU.subtract, ALU.mult))
                    link(dve.tensor_tensor(x[0:r, t, :], x[0:r, t, :], lnp[0:r, 0, :], ALU.mult))
                    dve.tensor_tensor(x[0:r, t, :], x[0:r, t, :], lnp[0:r, 1, :], ALU.add).then_inc(ln_done, 1)

            dve.wait_ge(consts_ready, 1)

            for layer in range(DEPTH):
                more = more_sems[layer]
                w, pw, sw = conv_parts(layer)
                for t in range(T):
                    b = drain(layer, "xT", t, 1)
                    r = ROWS[t]
                    dve.tensor_copy(xT[:, 4:8, START[t]:START[t] + r],
                                    b[:, 0:4 * r].rearrange("p (c r) -> p c r", c=4)).then_inc(done, 1)
                dve.memset(cb[:, :, 0:w - 1], 0.0)
                link(dve.memset(qm[:, :, :], 0.0))
                samples = cb[:, :, pw:pw + NB * sw].rearrange("p c (b s) -> p c b s", b=NB)
                for q in range(2 if layer == 0 else 1):
                    b = drain(layer, "hist", q)
                    nb = 4 if layer == 0 else 8
                    for cc in range(CC):
                        n = nb * (w - 1)
                        ins = dve.tensor_copy(samples[:, cc, nb * q:nb * q + nb, 0:w - 1],
                                              b[:, cc * n:cc * n + n].rearrange("p (b r) -> p b r", b=nb))
                    ins.then_inc(done, 1)
                for m in range(CC):
                    b = drain(layer, "a" if layer == 0 else "h", m)
                    wait_drained(dve, layer, "g" if layer == 0 else "c", m)
                    dve.tensor_tensor(cb[:, m, w - 1:pw], b[:, 0:SEQ], sig[:, m, 0:SEQ], ALU.mult)
                    dve.tensor_tensor(samples[:, m, :, w - 1:sw], b[:, SEQ:TOK].rearrange("p (b s) -> p b s", b=NB),
                                      sig[:, m, SEQ:TOK].rearrange("p (b s) -> p b s", b=NB), ALU.mult
                                      ).then_inc(done, 1)
                nn = min(w - 1, NS)
                dve.wait_ge(drained["dve"], JOBS[(layer, "a" if layer == 0 else "h", 3)][3])
                dve.tensor_copy(new_cols(nn).rearrange("p c (b s) -> p c b s", b=NB), samples[:, :, :, sw - nn:sw])
                for h in range(H):
                    wait_drained(dve, layer, "q", h)
                    ins = dve.tensor_copy(qm[:, h, :].rearrange("p (b z) -> p b z", z=36)[:, :, 0:NS],
                                          qT[:, h, SEQ:TOK].rearrange("p (b s) -> p b s", b=NB))
                ins.then_inc(qmask_ready, 1)
                dve.wait_ge(qmask_ready, layer + 1)

                wait_drained(dve, layer, "params")
                steps = [(cc, j, min(j + 4, w)) for cc in range(CC) for j in range(0, w, 4)]

                def conv_some(n):
                    for _ in range(min(n, len(steps))):
                        conv_taps(layer, *steps.pop(0))

                conv_some(6)
                for m in range(2):
                    b = drain(layer, "memT", m, 1)
                    dve.tensor_copy(memT[:, 4:8, P * m:P * m + P], b.rearrange("p (c r) -> p c r", c=4)).then_inc(done, 1)
                conv_some(8)
                for hp in range(2):
                    b = drain(layer, "kT", hp)
                    dve.tensor_copy(kT[:, 2 * hp:2 * hp + 2, :], b.rearrange("p (h q) -> p h q", h=2)).then_inc(done, 1)
                order = [(hp, t) for hp in range(2) for t in range(2)]

                def soft_max(j):
                    b = drain(layer, "sc", *order[j])
                    link(dve.tensor_reduce(mx[:, 2 * j:2 * j + 2], b.rearrange("p (h q) -> p h q", h=2), AX.X, ALU.max))
                    dve.tensor_scalar(mx[:, 2 * j:2 * j + 2], mx[:, 2 * j:2 * j + 2], -SCALE, None, ALU.mult
                                      ).then_inc(max_ready, 1)

                def soft_norm(j):
                    hp, t = order[j]
                    wait_drained(dve, layer, "sc", hp, t)
                    link(dve.reciprocal(sums[:, 2 * j:2 * j + 2], sums[:, 2 * j:2 * j + 2]))
                    for i in range(2):
                        pr = Pm[:, t, 2 * hp + i, :]
                        ins = dve.tensor_scalar(pr, pr, sums[:, 2 * j + i:2 * j + i + 1], None, ALU.mult)
                    ins.then_inc(prob_ready, 1)

                soft_max(0)
                for j in range(4):
                    if j + 1 < 4:
                        soft_max(j + 1)
                    soft_norm(j)
                for h in range(H):
                    b = drain(layer, "PT", h)
                    if h == 0:
                        wait_filled(dve, layer, "kv", 1, 1)
                    dve.tensor_copy(PT[:, h, :, :], b.rearrange("p (m q) -> p m q", m=2)).then_inc(done, 1)
                for s in range(NB):
                    b = drain(layer, "KT", s, 1)
                    dve.tensor_copy(KT[s % 2][:, 2:4, :], b.rearrange("p (h q) -> p h q", h=2)).then_inc(done, 1)
                    conv_some(2)
                drain(layer, "scs")
                link(dve.tensor_reduce(mx[:, 8:9], ps[:, BANKS, 0:MEM], AX.X, ALU.max))
                dve.tensor_scalar(mx[:, 8:9], mx[:, 8:9], -SCALE, None, ALU.mult).then_inc(max_ready, 1)
                wait_drained(dve, layer, "scs")
                link(dve.reciprocal(sums[:, 8:9], sums[:, 8:9]))
                dve.tensor_scalar(Ps[:, :], Ps[:, :], sums[:, 8:9], None, ALU.mult).then_inc(prob_ready, 1)
                b = drain(layer, "PTs")
                dve.tensor_copy(PTs[:, :, :], b[:, 0:2 * P].rearrange("p (m q) -> p m q", m=2)).then_inc(done, 1)
                conv_some(len(steps))

                if layer == 0:
                    conv_end.append(links[0])
                    b = drain(layer, "mean")
                    dve.wait_ge(dve_seq, links[0])
                    for cc in range(CC):
                        ins = dve.scalar_tensor_tensor(ct[:, cc, :], b[:, 0:TOK], -1.0 / CH, catT[:, cc, :],
                                                       ALU.mult, ALU.add)
                    ins.then_inc(done, 1)
                    wait_drained(dve, layer, "mean")
                    for cc in range(CC):
                        ins = dve.tensor_tensor(catT[:, cc, :], ct[:, cc, :], ct[:, cc, :], ALU.mult)
                    ins.then_inc(centred, 1)
                    wait_drained(dve, layer, "var")
                    link(dve.reciprocal(sig[:, 0, :], sig[:, 1, :]))
                    dve.wait_ge(centred, 1)
                    for cc in range(CC):
                        ins = dve.tensor_tensor(ct[:, cc, :], ct[:, cc, :], sig[:, 0, :], ALU.mult)
                        ins.then_inc(conv_ready, 1)
                else:
                    dve.wait_ge(dve_seq, links[0])
                    for cc in range(CC):
                        if cc == 0:
                            wait_drained(dve, layer, "b", 3)
                        dve.tensor_tensor(catT[:, cc, :], catT[:, cc, :], ct[:, cc, :], ALU.mult).then_inc(mix_ready, 1)
                for n in range(2):
                    for t in range(T):
                        r = ROWS[t]
                        b = drain(layer, "out", n, t)
                        xv = x[0:r, t, 512 * n:512 * n + 512]
                        dve.scalar_tensor_tensor(xv, xv, ALPHA, b[0:r, :], ALU.mult, ALU.add).then_inc(done, 1)
                wait_drained(dve, layer, "out", 1, T - 1)
                normalise(2 * layer, x)
                for t in range(T):
                    b = drain(layer, "x1T", t, 1)
                    r = ROWS[t]
                    dve.tensor_copy(xT[:, 4:8, START[t]:START[t] + r],
                                    b[:, 0:4 * r].rearrange("p (c r) -> p c r", c=4)).then_inc(done, 1)

                if layer == 0:
                    dve.wait_ge(stored, 16 * 4)
                else:
                    dve.wait_ge(stored, 16 * 8)
                dve.memset(slots[:, :, :], -1.0)
                dve.memset(score[32:64, 2, :], 0.0)
                dve.memset(score[64:128, 2, :], 0.0)
                link(dve.memset(grp[:, :, 8:12], -BIG))
                wait_drained(dve, layer, "logits", T - 1)
                rbb = rb[:, :].unsqueeze(1).to_broadcast([P, T, E])
                link(dve.tensor_tensor(cand[:, :, :], score[:, :, :], rbb, ALU.add))
                for t in range(T):
                    for g in range(GROUPS):
                        ins = dve.max(top[:, t, g, :], cand[:, t, 8 * g:8 * g + 8])
                link(ins)
                link(dve.tensor_tensor(grp[:, :, 0:8], top[:, :, 0:8, 0], top[:, :, 0:8, 1], ALU.add))
                for t in range(T):
                    ins = dve.max(top[:, t, 8, :], grp[:, t, 0:8])
                link(ins)
                link(dve.memset(top[:, :, 8, TOP_GROUPS:8], -BIG))
                for t in range(T):
                    ins = dve.match_replace(out=grpr[:, t, :], in_to_replace=top[:, t, 8, :], in_values=grp[:, t, :],
                                            imm_value=BIG)
                link(ins)
                link(dve.tensor_scalar(grpr[:, :, 0:8], grpr[:, :, 0:8], BIG * 0.5, None, ALU.is_ge))
                link(dve.tensor_scalar(grp[:, :, 0:8], grpr[:, :, 0:8], BIG, -BIG, ALU.mult, ALU.add))
                c4 = cand[:, :, :].rearrange("p t (g e) -> p t g e", g=GROUPS)
                link(dve.tensor_tensor(c4, c4, grpr[:, :, 0:8].unsqueeze(3).to_broadcast([P, T, GROUPS, 8]), ALU.mult))
                link(dve.tensor_tensor(c4, c4, grp[:, :, 0:8].unsqueeze(3).to_broadcast([P, T, GROUPS, 8]), ALU.add))
                for t in range(T):
                    ins = dve.max(top[:, t, 0, :], cand[:, t, :])
                link(ins)
                for t in range(T):
                    ins = dve.match_replace(out=mask[:, t, :], in_to_replace=top[:, t, 0, :], in_values=cand[:, t, :],
                                            imm_value=BIG)
                link(ins)
                for t in range(T):
                    ins = dve.tensor_scalar(mask[:, t, :], mask[:, t, :], BIG * 0.5, valid[:, t:t + 1],
                                            ALU.is_ge, ALU.mult)
                ins.then_inc(mask_ready, 1)
                dve.wait_ge(mask_ready, layer + 1)
                for t in range(T):
                    ins = dve.tensor_tensor(gates[:, t, :], score[:, t, :], mask[:, t, :], ALU.mult)
                link(ins)
                link(dve.tensor_reduce(gsum[:, :], gates[:, :, :], AX.X, ALU.add))
                link(dve.reciprocal(gsum[:, :], gsum[:, :]))
                sl = slots[:, 0:PAIRS, :].rearrange("p k (t f) -> p k t f", t=T)
                for t in range(T):
                    r = ROWS[t]
                    dve.tensor_scalar(sl[0:r, :, t, 0:2], gates[0:r, t, :].rearrange("p (k h) -> p k h", h=2),
                                      gsum[0:r, t:t + 1], ROUTED, ALU.mult, ALU.mult)
                for f in range(2):
                    b = drain(layer, "sup", f)
                    wait_drained(dve, layer, "sgate", f)
                    dve.tensor_tensor(qT[:, f, :], b[:, 0:TOK], sig[:, f, :], ALU.mult).then_inc(done, 1)
                for t in range(T):
                    for n in range(2):
                        r = ROWS[t]
                        b = drain(layer, "sdown", t, n)
                        dve.scalar_tensor_tensor(y[0:r, t, 512 * n:512 * n + 512], x[0:r, t, 512 * n:512 * n + 512],
                                                 ALPHA, b[0:r, :], ALU.mult, ALU.add).then_inc(done, 1)
                for t in range(T):
                    r = ROWS[t]
                    b = drain(layer, "rank", t)
                    dve.scalar_tensor_tensor(cand[0:r, t, :], b[0:r, 0:E], 1.0, mask[0:r, t, :], ALU.add, ALU.mult
                                             ).then_inc(done, 1)
                wait_drained(dve, layer, "rank", T - 1)
                for t in range(T):
                    r = ROWS[t]
                    dve.tensor_scalar(sl[0:r, :, t, 2:4], cand[0:r, t, :].rearrange("p (k h) -> p k h", h=2),
                                      -1.0, None, ALU.add)
                b = drain(layer, "count")
                dve.tensor_reduce(passes_f[:, 0:1], b[0:1, 0:E], AX.X, ALU.max).then_inc(done, 1)
                wait_drained(dve, layer, "count")
                link(dve.tensor_scalar(passes_f[:, 1:PASSES], thresholds[:, :], passes_f[:, 0:1], None, ALU.is_lt))
                link(dve.tensor_reduce(passes_f[:, 6:7], passes_f[:, 1:PASSES], AX.X, ALU.add))
                dve.tensor_scalar(passes[:, layer:layer + 1], passes_f[:, 6:7], 1.0, None, ALU.add
                                  ).then_inc(passes_ready, 1)
                dve.wait_ge(passes_ready, layer + 1)
                for t in range(T):
                    r = ROWS[t]
                    dve.wait_ge(hi_ready, T * layer + t + 1)
                    dve.tensor_tensor(xl[0:r, t, :, :], x[0:r, t, :].rearrange("p (j c) -> p c j", c=C),
                                      xh[0:r, t, :, :].bitcast(F32), ALU.subtract).then_inc(lo_ready, 1)

                s0 = (PAIRS + 1) * layer
                for b in range(2):
                    dve.tensor_copy(cols[:, b, :, 4], tokid[:, :])

                def build_sel(k, b, iota, ready, built, n, shifted=None):
                    dve.tensor_copy(cols[:, b, :, 0:4], slots[:, :, :].rearrange("p k f -> p (k f)")[
                        :, bass.ds(12 * k, 12)].rearrange("p (t f) -> p t f", t=T)).then_inc(ready, 1)
                    dve.wait_ge(ready, n)
                    if shifted is not None:
                        dve.wait_ge(more["shift"], shifted)
                    dve.tensor_tensor(sel[:, b, :, :].rearrange("p t (h s) -> p t h s", h=2),
                                      iota[:, :].unsqueeze(1).unsqueeze(1).to_broadcast([P, T, 2, WIN]),
                                      cols[:, b, :, 2:4].unsqueeze(3).to_broadcast([P, T, 2, WIN]),
                                      ALU.is_equal).then_inc(built, 1)

                def take_slotv(b):
                    return dve.tensor_copy(slotv[:, b, :], ps[:, SMALL, FF:FF + 5])

                def build_back(b, built):
                    dve.tensor_copy(slotg[0:WIN, b:b + 1], slotv[0:WIN, b, 0:1])
                    dve.tensor_copy(slotg[WIN:P, b:b + 1], slotv[WIN:P, b, 1:2])
                    dve.tensor_scalar(back[:, b, :], iota_tok[:, :], slotv[:, b, 4:5], None, ALU.is_equal
                                      ).then_inc(built, 1)

                def swiglu(b):
                    return dve.scalar_tensor_tensor(hs[:, :], ps[:, GU, FF:2 * FF], slotg[:, b:b + 1], sg[:, :],
                                                    ALU.mult, ALU.mult)

                def low_y():
                    return dve.tensor_tensor(yl[:, :], ps[:, DOWN:DOWN + 2, :].rearrange("p b n -> p (b n)"),
                                             yh[:, :].bitcast(F32), ALU.subtract)

                def add_back(m):
                    t, n = m // 2, m % 2
                    r = ROWS[t]
                    yv = y[0:r, t, 512 * n:512 * n + 512]
                    return dve.tensor_tensor(yv, yv, ps[0:r, COMBINE + m % 2, :], ALU.add)

                def add_all(k):
                    for m in range(6):
                        dve.wait_ge(combined, 6 * PAIRS * layer + 6 * k + m + 1)
                        wait(dve, added, 6 * PAIRS * layer + 6 * k + m - 5)
                        add_back(m).then_inc(added, 1)

                def slots_of(k, b):
                    dve.wait_ge(slotv_ready, s0 + k + 1)
                    build_back(b, slots_ready)

                def select(k, b):
                    build_sel(k, b, iota_win, cols_ready, sel_built, s0 + k + 1)

                def step(k, b, first):
                    select(k + 1, 1 - b)
                    if not first:
                        dve.wait_ge(yh_done, PAIRS * layer + k)
                        low_y().then_inc(yl_done, 1)
                    dve.wait_ge(slotv_mm, s0 + k + 2)
                    take_slotv(1 - b).then_inc(slotv_ready, 1)
                    dve.wait_ge(silu_done, PAIRS * layer + k + 1)
                    dve.wait_ge(slots_ready, s0 + k + 1)
                    swiglu(b).then_inc(h_done, 1)
                    if not first:
                        add_all(k - 1)
                    slots_of(k + 1, 1 - b)

                select(0, 0)
                dve.wait_ge(slotv_mm, s0 + 1)
                take_slotv(0).then_inc(slotv_ready, 1)
                slots_of(0, 0)
                step(0, 0, True)
                step(1, 1, False)
                with dve.Fori(1, PAIRS // 2) as j:
                    for b in range(2):
                        step(2 * j + b, b, False)
                dve.wait_ge(yh_done, PAIRS * (layer + 1))
                low_y().then_inc(yl_done, 1)
                add_all(PAIRS - 1)

                npass = dve.value_load(passes[0:1, layer:layer + 1], min_val=1, max_val=PASSES)
                with dve.If(npass > 1):
                    dve.wait_ge(added, 6 * PAIRS * (layer + 1))
                    dve.tensor_copy(window[:, 0:WIN // 2], iota_win[:, 0:WIN // 2]).then_inc(more["added"], 1)
                    dve.tensor_copy(window[:, WIN // 2:], iota_win[:, WIN // 2:]).then_inc(more["shift"], 1)
                    with dve.Fori(1, npass) as p:
                        dve.wait_ge(more["shift"], p)
                        dve.tensor_scalar(window[:, :], window[:, :], float(WIN), None,
                                          ALU.add).then_inc(more["shift"], 1)
                        with dve.Fori(0, PAIRS) as k:
                            n = (p - 1) * PAIRS + k
                            build_sel(k, 0, window, more["cols"], more["sel"], n + 1, p + 1)
                            dve.wait_ge(more["slotm"], n + 1)
                            take_slotv(0).then_inc(more["slotv"], 1)
                            dve.wait_ge(more["slotv"], n + 1)
                            build_back(0, more["slots"])
                            dve.wait_ge(more["silu"], n + 1)
                            dve.wait_ge(more["slots"], n + 1)
                            swiglu(0).then_inc(more["h"], 1)
                            dve.wait_ge(more["yh"], n + 1)
                            low_y().then_inc(more["yl"], 1)
                            for m in range(6):
                                dve.wait_ge(more["combined"], 6 * n + m + 1)
                                add_back(m).then_inc(more["added"], 1)
                            dve.wait_ge(more["added"], 6 * n + 7)
                dve.wait_ge(added, 6 * PAIRS * (layer + 1))
                normalise(2 * layer + 1, y)

        @block.tensor
        def _(pe):
            def start(layer, *name):
                bank, _, _, _, before = JOBS[(layer, *name)]
                if before is not None:
                    wait_drained(pe, *before)
                return ps[:, bank, :]

            def turn(out, in_, r, c):
                return pe.transpose(out, in_, ident[0:r, 0:r])

            pe.wait_ge(consts_ready, 1)
            pe.wait_ge(x_loaded, 32)
            for layer in range(DEPTH):
                more = more_sems[layer]
                w = WIDTH[layer]
                pw, sw = SEQ + w - 1, NS + w - 1

                def transpose_x(name, q):
                    for t in range(T):
                        if q >= 0:
                            pe.wait_ge(ln_done, T * q + t + 1)
                        r = ROWS[t]
                        xv = x[0:r, t, :].rearrange("p (j c) -> p c j", c=C)
                        for hf in range(2):
                            b = start(layer, name, t, hf)
                            for c in range(4):
                                ins = turn(b[:, r * c:r * c + r], xv[:, 4 * hf + c, :], r, P)
                            ins.then_inc(filled, 1)

                transpose_x("xT", 2 * layer - 1)
                b = start(layer, "params")
                pe.wait_ge(small_loaded, 16 * (7 if layer == 0 else 7 + 4))
                n = NPARAM[layer]
                for cc in range(CC):
                    ins = turn(b[:, n * cc:n * cc + n], prow[0:n, P * cc:P * cc + P], n, P)
                ins.then_inc(filled, 1)
                for q in range(2 if layer == 0 else 1):
                    b = start(layer, "hist", q)
                    n = (4 if layer == 0 else 8) * (w - 1)
                    for cc in range(CC):
                        ins = turn(b[:, n * cc:n * cc + n], y[0:n, 2, CH * q + P * cc:CH * q + P * cc + P], n, P)
                    ins.then_inc(filled, 1)
                wait_drained(pe, layer, "xT", T - 1, 0)
                wait_drained(pe, layer, "xT", T - 1, 1)
                for n, part in enumerate(["g", "a", "q"] if layer == 0 else ["c", "h", "b", "q"]):
                    wait_tile(pe, layer, n)
                    wt = tile_at(layer, n).rearrange("p (c n) -> p c n", c=C)
                    for m in range(4):
                        b = start(layer, part, m)
                        for c in range(C):
                            ins = pe.matmul(b[:, 0:TOK], wt[:, c, P * m:P * m + P], xT[:, c, :], start=c == 0, stop=c == C - 1)
                        ins.then_inc(filled, 1)
                wait_drained(pe, layer, "a" if layer == 0 else "h", 3)
                b = start(layer, "newp")
                n = w - 1
                for cc in range(CC):
                    ins = turn(b[0:n, P * cc:P * cc + P], cb[:, cc, pw - n:pw], P, n)
                ins.then_inc(filled, 1)
                b = start(layer, "news")
                n = min(w - 1, NS)
                pe.wait_ge(qmask_ready, layer + 1)
                for cc in range(CC):
                    ins = turn(b[0:NB * n, P * cc:P * cc + P], new_cols(n)[:, cc, :], P, NB * n)
                ins.then_inc(filled, 1)
                pe.wait_ge(mem_loaded[layer], 16)
                for m in range(2):
                    mv_ = kv[:, m, :].rearrange("p (j c) -> p c j", c=C)
                    for hf in range(2):
                        b = start(layer, "memT", m, hf)
                        for c in range(4):
                            ins = turn(b[:, P * c:P * c + P], mv_[:, 4 * hf + c, :], P, P)
                        ins.then_inc(filled, 1)
                wait_drained(pe, layer, "memT", 1, 0)
                wait_drained(pe, layer, "memT", 1, 1)
                for n in range(2):
                    tn = tile_no(layer, "kv", n)
                    wait_tile(pe, layer, tn)
                    wt = tile_at(layer, tn).rearrange("p (c n) -> p c n", c=C)
                    for m in range(2):
                        b = start(layer, "kv", n, m)
                        for c in range(C):
                            ins = pe.matmul(b, memT[:, c, P * m:P * m + P], wt[:, c, :], start=c == 0, stop=c == C - 1)
                        ins.then_inc(filled, 1)
                wait_drained(pe, layer, "kv", 0, 1)
                for hp in range(2):
                    b = start(layer, "kT", hp)
                    for i in range(2):
                        for m in range(2):
                            h = 2 * hp + i
                            ins = turn(b[:, MEM * i + P * m:MEM * i + P * m + P], kv[:, m, HD * h:HD * h + HD], P, P)
                    ins.then_inc(filled, 1)
                wait_drained(pe, layer, "kT", 1)
                wait_drained(pe, layer, "q", 3)
                for hp in range(2):
                    for t in range(2):
                        b = start(layer, "sc", hp, t)
                        for i in range(2):
                            h = 2 * hp + i
                            ins = pe.matmul(b[:, MEM * i:MEM * i + MEM], qT[:, h, P * t:P * t + P], kT[:, h, :],
                                            start=True, stop=True)
                        ins.then_inc(filled, 1)
                for h in range(H):
                    pe.wait_ge(prob_ready, 5 * layer + 2 * (h // 2) + 2)
                    b = start(layer, "PT", h)
                    for m in range(2):
                        for t in range(2):
                            ins = turn(b[:, MEM * m + P * t:MEM * m + P * t + P], Pm[:, t, h, P * m:P * m + P], P, P)
                    ins.then_inc(filled, 1)
                wait_drained(pe, layer, "kv", 1, 1)
                for h in range(H):
                    wait_drained(pe, layer, "PT", h)
                    b = start(layer, "o", h)
                    for m in range(2):
                        ins = pe.matmul(b[:, 0:SEQ], kv[:, m, CH + HD * h:CH + HD * h + HD], PT[:, h, m, :],
                                        start=m == 0, stop=m == 1)
                    ins.then_inc(filled, 1)
                pe.wait_ge(qmask_ready, layer + 1)

                def sample_scores(s):
                    wait_drained(pe, layer, "KT", s, 0)
                    wait_drained(pe, layer, "KT", s, 1)
                    for h in range(H):
                        ins = pe.matmul(ps[32 * h:32 * h + 32, BANKS, 0:MEM], qm[:, h, 32 * s:32 * s + 32],
                                        KT[s % 2][:, h, :], start=s == 0, stop=s == NB - 1)
                    return ins

                for s in range(NB):
                    if s % 4 == 0:
                        tn = tile_no(layer, "K", s // 4)
                        wait_tile(pe, layer, tn)
                        kt = tile_at(layer, tn).rearrange("p (b m n) -> p b m n", b=4, m=2)
                    for hp in range(2):
                        b = start(layer, "KT", s, hp)
                        for i in range(2):
                            for m in range(2):
                                h = 2 * hp + i
                                ins = turn(b[:, MEM * i + P * m:MEM * i + P * m + P],
                                           kt[:, s % 4, m, HD * h:HD * h + HD], P, P)
                        ins.then_inc(filled, 1)
                    if s >= 1:
                        sample_scores(s - 1)
                ins = sample_scores(NB - 1)
                ins.then_inc(filled, 1)
                pe.wait_ge(prob_ready, 5 * layer + 5)
                b = start(layer, "PTs")
                for m in range(2):
                    ins = turn(b[:, P * m:P * m + P], Ps[:, P * m:P * m + P], P, P)
                ins.then_inc(filled, 1)
                wait_drained(pe, layer, "PTs")
                b = start(layer, "os")
                for s in range(NB):
                    tn = tile_no(layer, "V", s // 4)
                    if s % 4 == 0:
                        wait_tile(pe, layer, tn)
                    vt = tile_at(layer, tn).rearrange("p (b m n) -> p b m n", b=4, m=2)
                    for h in range(H):
                        for m in range(2):
                            q = 32 * h + NS * s
                            ins = pe.matmul(b[:, q:q + NS], vt[:, s % 4, m, HD * h:HD * h + HD], PTs[:, m, q:q + NS],
                                            start=m == 0, stop=m == 1)
                ins.then_inc(filled, 1)
                if layer == 0:
                    pe.wait_ge(dve_seq, conv_end[0])
                    b = start(layer, "mean")
                    for cc in range(CC):
                        ins = pe.matmul(b[:, 0:TOK], ones[:, :], catT[:, cc, :], start=cc == 0, stop=cc == CC - 1)
                    ins.then_inc(filled, 1)
                    pe.wait_ge(centred, 1)
                    b = start(layer, "var")
                    for cc in range(CC):
                        ins = pe.matmul(b[:, 0:TOK], ones[:, :], catT[:, cc, :], start=cc == 0, stop=cc == CC - 1)
                    ins.then_inc(filled, 1)
                wait_drained(pe, layer, "os")
                pe.wait_ge(mix_ready, 4 * layer + 4)
                for n in range(2):
                    tn = tile_no(layer, "out", n)
                    wait_tile(pe, layer, tn)
                    wt = tile_at(layer, tn).rearrange("p (c n) -> p c n", c=C)
                    for t in range(T):
                        r = ROWS[t]
                        b = start(layer, "out", n, t)
                        for c in range(C):
                            ins = pe.matmul(b[0:r, :], catT[:, c, START[t]:START[t] + r], wt[:, c, :],
                                            start=c == 0, stop=c == C - 1)
                        ins.then_inc(filled, 1)
                transpose_x("x1T", 2 * layer)
                wait_drained(pe, layer, "x1T", T - 1, 0)
                wait_drained(pe, layer, "x1T", T - 1, 1)
                for t in range(T):
                    r = ROWS[t]
                    b = start(layer, "logits", t)
                    for c in range(C):
                        ins = pe.matmul(b[0:r, 0:E], xT[:, c, START[t]:START[t] + r], wr[:, c, :],
                                        start=c == 0, stop=c == C - 1)
                    ins.then_inc(filled, 1)
                tn = tile_no(layer, "sgu")
                wait_tile(pe, layer, tn)
                for i, part in enumerate(["sgate", "sup"]):
                    wt = tile_at(layer, tn)[:, 2048 * i:2048 * i + 2048].rearrange("p (c j f) -> p c f j", c=C, f=2)
                    for f in range(2):
                        b = start(layer, part, f)
                        for c in range(C):
                            ins = pe.matmul(b[:, 0:TOK], wt[:, c, f, :], xT[:, c, :], start=c == 0, stop=c == C - 1)
                        ins.then_inc(filled, 1)
                tn = tile_no(layer, "sd")
                wait_tile(pe, layer, tn)
                wt = tile_at(layer, tn)[:, 0:2048].rearrange("p (f n) -> p f n", f=2)
                wait_drained(pe, layer, "sup", 1)
                for t in range(T):
                    r = ROWS[t]
                    for n in range(2):
                        b = start(layer, "sdown", t, n)
                        for f in range(2):
                            ins = pe.matmul(b[0:r, :], qT[:, f, START[t]:START[t] + r], wt[:, f, 512 * n:512 * n + 512],
                                            start=f == 0, stop=f == 1)
                        ins.then_inc(filled, 1)
                pe.wait_ge(mask_ready, layer + 1)
                for t in range(T):
                    r = ROWS[t]
                    b = start(layer, "rank", t)
                    for u in range(t):
                        pe.matmul(b[0:r, 0:E], ones[:, 0:r], mask[:, u, :], start=u == 0, stop=False)
                    pe.matmul(b[0:r, 0:E], tri[0:r, 0:r], mask[0:r, t, :], start=t == 0, stop=True).then_inc(filled, 1)
                b = start(layer, "count")
                for t in range(T):
                    ins = pe.matmul(b[:, 0:E], ones[:, :], mask[:, t, :], start=t == 0, stop=t == T - 1)
                ins.then_inc(filled, 1)

                s0 = (PAIRS + 1) * layer
                g0 = FIRST_TILE[layer] + MIX_TILES[layer]

                def slot_mm(b):
                    for t in range(T):
                        r = ROWS[t]
                        ins = pe.matmul(ps[:, SMALL, FF:FF + 5], sel[0:r, b, t, :].bitcast(F32), cols[0:r, b, t, :],
                                        start=t == 0, stop=t == T - 1)
                    return ins

                def gather_mm(b):
                    for c in range(C):
                        out = ps[:, GATHER + c // 4, P * (c % 4):P * (c % 4) + P]
                        for t in range(T):
                            r = ROWS[t]
                            for half in (xh, xl):
                                ins = pe.matmul(out, half[0:r, t, c, :], sel[0:r, b, t, :],
                                                start=t == 0 and half is xh, stop=t == T - 1 and half is xl)
                    return ins

                def hidden_mm(slot, part, b):
                    wt = ring[:, slot, :].rearrange("p (e c f) -> p e c f", e=2, c=C)
                    for c in range(C):
                        for e in range(2):
                            ins = pe.matmul(ps[WIN * e:WIN * e + WIN, GU, FF * part:FF * part + FF],
                                            xs[:, b, c, WIN * e:WIN * e + WIN], wt[:, e, c, :],
                                            start=c == 0, stop=c == C - 1)
                    return ins

                def turn_hidden():
                    hv = hs[:, :].rearrange("p (j f) -> p f j", f=2)
                    for f in range(2):
                        ins = turn(ps[:, SMALL, P * f:P * f + P], hv[:, f, :], P, P)
                    return ins

                def down_mm(slot):
                    wt = ring[:, slot, :].rearrange("p (e f n) -> p e f n", e=2, f=2)
                    for n in range(2):
                        for f in range(2):
                            for e in range(2):
                                ins = pe.matmul(ps[WIN * e:WIN * e + WIN, DOWN + n, :], hT[:, f, WIN * e:WIN * e + WIN],
                                                wt[:, e, f, 512 * n:512 * n + 512], start=f == 0, stop=f == 1)
                    return ins

                def combine_mm(m, b):
                    t, n = m // 2, m % 2
                    r = ROWS[t]
                    for half in (yh, yl):
                        ins = pe.matmul(ps[0:r, COMBINE + m % 2, :], back[:, b, START[t]:START[t] + r],
                                        half[:, 512 * n:512 * n + 512], start=half is yh, stop=half is yl)
                    return ins

                def gather(k, b):
                    pe.wait_ge(sel_built, s0 + k + 1)
                    wait(pe, hT_copied, PAIRS * layer + k - 1)
                    slot_mm(b).then_inc(slotv_mm, 1)
                    wait(pe, xs_ready, s0 + k)
                    gather_mm(b).then_inc(gathered, 1)

                def combine(k, b):
                    pe.wait_ge(yh_done, PAIRS * layer + k + 1)
                    pe.wait_ge(yl_done, PAIRS * layer + k + 1)
                    pe.wait_ge(slots_ready, s0 + k + 1)
                    for m in range(6):
                        wait(pe, added, 6 * PAIRS * layer + 6 * k + m - 1)
                        combine_mm(m, b).then_inc(combined, 1)

                def arrived(c, k, j, b):
                    g = g0 + 3 * b + c
                    pe.wait_ge(landed[g % SLOTS], landing[g] + 16 * j)

                def step(k, j, b, first):
                    pe.wait_ge(xs_ready, s0 + k + 1)
                    wait(pe, h_done, PAIRS * layer + k)
                    arrived(0, k, j, b)
                    hidden_mm((g0 + 3 * b) % SLOTS, 0, b).then_inc(tile_used, 1)
                    arrived(1, k, j, b)
                    hidden_mm((g0 + 3 * b + 1) % SLOTS, 1, b).then_inc(tile_used, 1)
                    gather(k + 1, 1 - b)
                    pe.wait_ge(h_done, PAIRS * layer + k + 1)
                    pe.wait_ge(slotv_ready, s0 + k + 2)
                    turn_hidden().then_inc(hT_done, 1)
                    if not first:
                        combine(k - 1, 1 - b)
                    pe.wait_ge(hT_copied, PAIRS * layer + k + 1)
                    arrived(2, k, j, b)
                    down_mm((g0 + 3 * b + 2) % SLOTS).then_inc(tile_used, 1)

                for t in range(T):
                    pe.wait_ge(lo_ready, T * layer + t + 1)
                wait_drained(pe, layer, "count")
                wait_drained(pe, layer, "sgate", 1)
                gather(0, 0)
                step(0, 0, 0, True)
                step(1, 0, 1, False)
                with pe.Fori(1, PAIRS // 2) as j:
                    for b in range(2):
                        step(2 * j + b, j, b, False)
                combine(PAIRS - 1, 1)

                pe.wait_ge(passes_ready, layer + 1)
                npass = pe.value_load(passes[0:1, layer:layer + 1], min_val=1, max_val=PASSES)
                with pe.If(npass > 1):
                    pe.wait_ge(added, 6 * PAIRS * (layer + 1))
                    with pe.Fori(1, npass) as p:
                        with pe.Fori(0, PAIRS) as k:
                            n = (p - 1) * PAIRS + k
                            pe.wait_ge(more["added"], 6 * n + 1)
                            pe.wait_ge(more["sel"], n + 1)
                            slot_mm(0).then_inc(more["slotm"], 1)
                            gather_mm(0).then_inc(more["gathered"], 1)
                            pe.wait_ge(more["xs"], n + 1)
                            pe.wait_ge(more["landed"], 48 * n + 48)
                            hidden_mm(0, 0, 0)
                            hidden_mm(1, 1, 0).then_inc(more["up"], 1)
                            pe.wait_ge(more["h"], n + 1)
                            pe.wait_ge(more["slotv"], n + 1)
                            turn_hidden().then_inc(more["hT"], 1)
                            pe.wait_ge(more["hTc"], n + 1)
                            down_mm(2).then_inc(more["down"], 1)
                            pe.wait_ge(more["yl"], n + 1)
                            pe.wait_ge(more["slots"], n + 1)
                            for m in range(6):
                                pe.wait_ge(more["added"], 6 * n + m + 1)
                                combine_mm(m, 0).then_inc(more["combined"], 1)


INS = ["x_prompt", "x_sample", "mem_prompt", "cache_mem_k", "cache_mem_v", "state_conv_a", "state_conv_b",
       "w_in_a", "conv_a_w", "conv_a_b", "norm_a_g", "norm_a_b", "w_in_b", "conv_b_w", "w_kv", "w_out", "ln1_g",
       "ln1_b", "w_router", "router_bias", "w_gate", "w_up", "w_down", "ws_gate", "ws_up", "ws_down", "ln2_g", "ln2_b"]
OUTS = [(1, 256, 1024), (8, 4, 1024), (2, 1, 256, 4, 128), (2, 1, 256, 4, 128), (1, 1, 30, 512), (1, 1, 2, 512),
        (1, 8, 30, 512), (1, 8, 2, 512)]


def kernel(**inputs):
    import numpy as np
    import concourse.bacc as bacc
    from concourse.bass_utils import run_bass_kernel_spmd

    nc = bacc.Bacc("TRN2", target_bir_lowering=False, num_devices=1)
    arrays, ins = {}, {}
    for name in INS:
        a = np.ascontiguousarray(inputs[name])
        arrays[f"in_{name}"] = a
        ins[name] = nc.dram_tensor(f"in_{name}", a.shape, mybir.dt.from_np(a.dtype), kind="ExternalInput").ap()
    outs = [nc.dram_tensor(f"out_{i}", shape, F32, kind="ExternalOutput").ap() for i, shape in enumerate(OUTS)]
    build_program(nc, ins, outs)
    r = run_bass_kernel_spmd(nc, [arrays], core_ids=[0])
    return tuple(r.results[0][f"out_{i}"] for i in range(len(OUTS)))
```

```python
from contextlib import ExitStack

import concourse.bass as bass
from concourse import mybir

F32 = mybir.dt.float32
F32R = mybir.dt.float32r
BF16 = mybir.dt.bfloat16
I32 = mybir.dt.int32
ALU = mybir.AluOpType
ACT = mybir.ActivationFunctionType
AX = mybir.AxisListType

P = 128
D = 1024
C = D // P
SEQ, NB, NS = 256, 8, 4
TOK = SEQ + NB * NS
ROWS = [P, P, NB * NS]
START = [0, P, 2 * P]
T = len(ROWS)
CH = 512
CC = CH // P
H, HD, MEM = 4, 128, 256
DEPTH = 2
ALPHA = (2 * DEPTH) ** 0.25
EPS = 1e-5
SCALE = HD ** -0.5
WIDTH = [31, 3]
E, FF = 64, 256
GROUPS, TOP_GROUPS, ROUTED = 8, 4, 2.5
PAIRS = E // 2
WIN = 64
PASSES = -(-TOK // WIN)
NPARAM = [34, 3]
BIG = 1e30
SLOTS = 6
MIX_TILES = [13, 14]
FIRST_TILE = [0, MIX_TILES[0] + 3 * PAIRS]
BANKS = 7


def job_list(layer):
    memory = [(("memT", m, hf), "act") for m in range(2) for hf in range(2)]
    memory += [(("kv", n, m), "act") for n in range(2) for m in range(2)]
    memory += [(("kT", hp), "act") for hp in range(2)]
    jobs = [(("xT", t, hf), "act" if hf == 0 else "dve") for t in range(T) for hf in range(2)]
    small = [(("params",), "act")] + [(("hist", q), "dve") for q in range(2 if layer == 0 else 1)]
    if layer == 0:
        jobs += [(("g", m), "act") for m in range(4)] + small + [(("a", m), "dve") for m in range(4)]
    else:
        jobs = memory + jobs + [(("c", m), "act") for m in range(4)] + small
        jobs += [(("h", m), "dve") for m in range(4)] + [(("b", m), "act") for m in range(4)]
    jobs += [(("q", m), "act") for m in range(4)]
    if layer == 0:
        jobs += memory
    jobs += [(("newp",), "act"), (("news",), "act")]
    jobs += [(("sc", hp, t), "act") for hp in range(2) for t in range(2)]
    jobs += [(("KT", b, hp), "act") for b in range(NB) for hp in range(2)]
    jobs += [(("scs",), "act")]
    jobs += [(("PT", h), "act") for h in range(H)]
    jobs += [(("o", h), "act") for h in range(H)]
    jobs += [(("PTs",), "act"), (("os",), "act"), (("osT",), "act")]
    jobs += [(("mean",), "dve"), (("var",), "act")] if layer == 0 else []
    jobs += [(("out", t, n), "dve") for t in range(T) for n in range(2)]
    jobs += [(("x1T", t, hf), "act" if hf == 0 else "dve") for t in range(T) for hf in range(2)]
    jobs += [(("logits", t), "act") for t in range(T)]
    jobs += [(("sgate", f), "act") for f in range(2)] + [(("sup", f), "dve") for f in range(2)]
    jobs += [(("sdown", t, n), "dve") for t in range(T) for n in range(2)]
    jobs += [(("rank", t), "dve") for t in range(T)] + [(("count",), "dve")]
    return jobs


def number_jobs():
    table, count, turn = {}, {"pe": 0, "act": 0, "dve": 0}, 0
    for layer in range(DEPTH):
        holder = {}
        for name, drainer in job_list(layer):
            if name == ("scs",):
                bank = BANKS
            else:
                bank, turn = turn % BANKS, turn + 1
            count["pe"] += 1
            count[drainer] += 1
            table[(layer, *name)] = (bank, count["pe"], drainer, count[drainer], holder.get(bank))
            holder[bank] = (layer, *name)
    return table


JOBS = number_jobs()


def build_program(nc, I, O):
    with ExitStack() as ctx:
        sem = lambda name: ctx.enter_context(nc.semaphore(name))
        sb = lambda name, shape, dt=F32: ctx.enter_context(nc.sbuf_tensor(name, shape, dt))

        ring = sb("ring", [P, SLOTS, 4096])
        x = sb("x", [P, T, D])
        y = sb("y", [P, T, D])
        xT = sb("xT", [P, C, TOK])
        lnp = sb("lnp", [P, 2, D])
        ident = sb("ident", [P, P])
        tri = sb("tri", [P, P])
        ones = sb("ones", [P, P])
        eps = sb("eps", [P, 1])
        iota_win = sb("iota_win", [P, WIN])
        iota_tok = sb("iota_tok", [P, TOK])
        valid = sb("valid", [P, T])
        tokid = sb("tokid", [P, T])
        thresholds = sb("thresholds", [1, PASSES - 1])
        passes = sb("passes", [1, DEPTH], I32)
        passes_f = sb("passes_f", [1, 8])
        bn = sb("bn", [P, T, 2, 6])
        mv = sb("mv", [P, T, 2])
        rstd = sb("rstd", [P, T])
        top = sb("top", [P, T, 9, 8])
        grp = sb("grp", [P, T, 12])
        grpr = sb("grpr", [P, T, 12])
        gsum = sb("gsum", [P, T])
        mx = sb("mx", [P, 10])
        sums = sb("sums", [P, 10])

        mix = ExitStack()
        mb = lambda name, shape, dt=F32: mix.enter_context(nc.sbuf_tensor(name, shape, dt))
        kv = mb("kv", [P, 2, D])
        memT = mb("memT", [P, C, MEM])
        cb = mb("cb", [P, CC, 558])
        catT = mb("catT", [P, C, TOK])
        kT = mb("kT", [P, H, MEM])
        qm = mb("qm", [P, H, 288])
        prow = mb("prow", [34, CH])
        Ps = mb("Ps", [P, MEM])
        PTs = mb("PTs", [P, 2, P])
        pcol = mb("pcol", [P, CC, 34])
        sig = mb("sig", [P, CC, TOK])
        ct = mb("ct", [P, CC, TOK])
        qT = mb("qT", [P, H, TOK])
        wr = mb("wr", [P, C, E])
        rb = mb("rb", [P, E])
        mix.close()
        PT = memT.rearrange("p (h m) q -> p h m q", h=H)
        Pm = y[:, 0:2, :].rearrange("p t (h q) -> p t h q", h=H)
        KT = [xT[:, :, :].rearrange("p c q -> p (c q)")[:, 1024 * b:1024 * b + 1024]
              .rearrange("p (h q) -> p h q", h=H) for b in range(2)]

        spread = cb[:, :, :].rearrange("p c n -> p (c n)")[:, 0:2 * H * MEM].rearrange("p (g z) -> p g z", z=MEM)

        new_cols = lambda n: PTs[:, :, :].rearrange("p m q -> p (m q)")[:, 0:CC * NB * n].rearrange(
            "p (c s) -> p c s", c=CC)

        xb = sb("xb", [P, 2, 3, C, P], BF16)
        xb2 = sb("xb2", [P, C, P], BF16)
        xb2m = sb("xb2m", [P, C, P], BF16)
        slots = sb("slots", [P, PAIRS + 1, 12])
        score = sb("score", [P, T, E])
        cand = sb("cand", [P, T, E])
        mask = sb("mask", [P, T, E])
        gates = sb("gates", [P, T, E])
        xs = sb("xs", [P, 2, C, P])
        yh = sb("yh", [P, D], F32R)
        yl = sb("yl", [P, D], F32R)
        sel = sb("sel", [P, 2, T, P])
        selb = sb("selb", [P, 2, T, P], BF16)
        back = sb("back", [P, 2, TOK], F32R)
        cols = sb("cols", [P, 2, T, 5])
        slotv = sb("slotv", [P, 2, 5])
        slotg = sb("slotg", [P, 2])
        sg = sb("sg", [P, FF])
        hs = sb("hs", [P, FF])
        hT = sb("hT", [P, 2, P])
        window = sb("window", [P, WIN])

        ps = ctx.enter_context(nc.psum_tensor("ps", [P, 8, 512], F32))
        GATHER, GU, SMALL, DOWN, COMBINE = 0, 2, 3, 4, 6

        x_loaded = sem("x_loaded")
        mem_loaded = [sem(f"mem_loaded{layer}") for layer in range(DEPTH)]
        small_loaded = [sem(f"small_loaded{layer}") for layer in range(DEPTH)]
        router_loaded = [sem(f"router_loaded{layer}") for layer in range(DEPTH)]
        ln_loaded = sem("ln_loaded")
        landed = [sem(f"landed{s}") for s in range(SLOTS)]
        tile_used = sem("tile_used")
        consts_ready = sem("consts_ready")
        pool_seq = sem("pool_seq")
        filled = sem("filled")
        drained = {"act": sem("drained_act"), "dve": sem("drained_dve")}
        dve_seq = sem("dve_seq")
        glu_ready = sem("glu_ready")
        max_ready = sem("max_ready")
        prob_ready = sem("prob_ready")
        qmask_ready = sem("qmask_ready")
        spread_cleared = sem("spread_cleared")
        centred = sem("centred")
        var_ready = sem("var_ready")
        rstd_ready = sem("rstd_ready")
        ln_done = sem("ln_done")
        conv_ready = sem("conv_ready")
        mix_ready = sem("mix_ready")
        part0_ready = sem("part0_ready")
        rest_ready = sem("rest_ready")
        part1_ready = sem("part1_ready")
        part2_ready = sem("part2_ready")
        mask_ready = sem("mask_ready")
        shared_h = sem("shared_h")
        passes_ready = sem("passes_ready")
        stored = sem("stored")
        y_stored = sem("y_stored")
        hist_stored = sem("hist_stored")
        cols_ready = sem("cols_ready")
        sel_built = sem("sel_built")
        gathered = sem("gathered")
        slotv_mm = sem("slotv_mm")
        xs_ready = sem("xs_ready")
        slotv_ready = sem("slotv_ready")
        slots_ready = sem("slots_ready")
        silu_done = sem("silu_done")
        h_done = sem("h_done")
        hT_done = sem("hT_done")
        hT_copied = sem("hT_copied")
        yh_done = sem("yh_done")
        yl_done = sem("yl_done")
        combined = sem("combined")
        added = sem("added")
        more_sems = [{n: sem(f"more_{n}{layer}") for n in (
            "landed", "slotm", "cols", "sel", "gathered", "xs", "slotv", "slots", "gate", "up", "silu", "h", "hT",
            "hTc", "down", "yh", "yl", "combined", "added", "shift")} for layer in range(DEPTH)]

        def wait(eng, s, v):
            if not isinstance(v, int) or v > 0:
                eng.wait_ge(s, v)

        def psum_of(layer, *name):
            return ps[:, JOBS[(layer, *name)][0], :]

        def wait_filled(eng, layer, *name):
            eng.wait_ge(filled, JOBS[(layer, *name)][1])

        def wait_drained(eng, layer, *name):
            _, _, drainer, n, _ = JOBS[(layer, *name)]
            eng.wait_ge(drained[drainer], n)

        uses = [0] * SLOTS
        landing = {}

        def tile_plan():
            for layer in range(DEPTH):
                g = FIRST_TILE[layer]
                for n in range(MIX_TILES[layer]):
                    uses[(g + n) % SLOTS] += 2 if n == MIX_TILES[layer] - 2 else 1
                    landing[g + n] = 16 * uses[(g + n) % SLOTS]
                for n in range(MIX_TILES[layer], MIX_TILES[layer] + 3 * PAIRS):
                    uses[(g + n) % SLOTS] += 1
                    landing[g + n] = 16 * uses[(g + n) % SLOTS]

        tile_plan()

        def tile_at(layer, n):
            return ring[:, (FIRST_TILE[layer] + n) % SLOTS, :]

        def wait_tile(eng, layer, n):
            g = FIRST_TILE[layer] + n
            eng.wait_ge(landed[g % SLOTS], landing[g])

        IN_PARTS = [["g", "a", "q"], ["c", "h", "b", "q"]]
        tiles = []
        for layer in range(DEPTH):
            ins = [(("in", i), (part, 3)) for i, part in enumerate(IN_PARTS[layer])]
            kvs = [(("kv", n), ("kv", n, 1)) for n in range(2)]
            tiles.append((ins + kvs if layer == 0 else kvs + ins)
                         + [(("K", 0), ("KT", 3, 1)), (("K", 1), ("KT", 7, 1)), (("V", 0), ("os",)), (("V", 1), ("os",)),
                            (("out", 0), ("out", T - 1, 0)), (("out", 1), ("out", T - 1, 1)),
                            (("sgu", 0), ("sup", 1)), (("sd", 0), ("sdown", T - 1, 1))])

        def tile_no(layer, what, i=0):
            return [name for name, _ in tiles[layer]].index((what, i))

        def last_job(layer, n):
            return tiles[layer][n][1]

        def wait_tile_used(eng, g):
            if g < 0:
                return
            layer = int(g >= FIRST_TILE[1])
            n = g - FIRST_TILE[layer]
            if n < MIX_TILES[layer]:
                wait_filled(eng, layer, *last_job(layer, n))
            else:
                pair, part = divmod(n - MIX_TILES[layer], 3)
                eng.wait_ge(tile_used, 2 * (PAIRS * layer + pair) + (2 if part == 2 else 1))

        IN_COLS = [[1, 0, 2], [1, 2, 0, 3]]
        w_in = [I["w_in_a"][0].rearrange("(p c) n -> p c n", c=C), I["w_in_b"][0].rearrange("(p c) n -> p c n", c=C)]
        experts = {}
        for layer in range(DEPTH):
            experts[layer] = [I["w_gate"][layer].rearrange("e (p c) f -> e p (c f)", c=C),
                              I["w_up"][layer].rearrange("e (p c) f -> e p (c f)", c=C),
                              I["w_down"][layer].rearrange("e (p c) d -> e p (c d)", c=2)]

        BEFORE_QUERIES, BEFORE_SCORES, BEFORE_SAMPLES = 6, 11, 8
        conv_end = []
        block = ctx.enter_context(nc.Block())

        @block.sync
        def _(sp):
            sp.dma_start(x[:, 0:2, :], I["x_prompt"][0].rearrange("(t p) d -> p t d", p=P)).then_inc(x_loaded, 16)
            sp.dma_start(x[0:ROWS[2], 2, :], I["x_sample"].rearrange("b s d -> (b s) d")).then_inc(x_loaded, 16)

            def load_tile(layer, n):
                g = FIRST_TILE[layer] + n
                dst = ring[:, g % SLOTS, :]
                wait_tile_used(sp, g - SLOTS)
                what, i = tiles[layer][n][0]
                if what == "in":
                    m = IN_COLS[layer][i]
                    sp.dma_start(dst.rearrange("p (c n) -> p c n", c=C),
                                 w_in[layer][:, :, 512 * m:512 * m + 512]).then_inc(landed[g % SLOTS], 16)
                elif what == "kv":
                    sp.dma_start(dst.rearrange("p (c n) -> p c n", c=C),
                                 I["w_kv"][layer].rearrange("(p c) n -> p c n", c=C)[:, :, 512 * i:512 * i + 512]
                                 ).then_inc(landed[g % SLOTS], 16)
                elif what in ("K", "V"):
                    cache = I["cache_mem_k"] if what == "K" else I["cache_mem_v"]
                    sp.dma_start(dst.rearrange("p (b n) -> p b n", b=4),
                                 cache[layer, 4 * i:4 * i + 4].rearrange("b (p m) h d -> p b (m h d)", m=2)
                                 ).then_inc(landed[g % SLOTS], 16)
                elif what == "out":
                    sp.dma_start(dst.rearrange("p (c n) -> p c n", c=C),
                                 I["w_out"][layer].rearrange("(c p) n -> p c n", c=C)[:, :, 512 * i:512 * i + 512]
                                 ).then_inc(landed[g % SLOTS], 16)
                elif what == "sgu":
                    for i, w in enumerate(("ws_gate", "ws_up")):
                        sp.dma_start(dst[:, 2048 * i:2048 * i + 2048],
                                     I[w][layer].rearrange("(p c) f -> p (c f)", c=C)).then_inc(landed[g % SLOTS], 16)
                else:
                    sp.dma_start(dst[:, 0:2048], I["ws_down"][layer].rearrange("(p c) d -> p (c d)", c=2)
                                 ).then_inc(landed[g % SLOTS], 16)

            for layer in range(DEPTH):
                more = more_sems[layer]
                for n in range(MIX_TILES[layer]):
                    load_tile(layer, n)
                    if n == (2 if layer == 0 else 1):
                        if layer == 1:
                            sp.wait_ge(gathered, PAIRS + 1)
                        sp.dma_start(kv[:, :, :], I["mem_prompt"][0].rearrange("(m p) d -> p m d", p=P)
                                     ).then_inc(mem_loaded[layer], 16)
                g0 = FIRST_TILE[layer] + MIX_TILES[layer]

                def load_pair(k, b, c):
                    g = g0 + 3 * b + c
                    sp.dma_start(ring[:, g % SLOTS, :].rearrange("p (e n) -> p e n", e=2),
                                 experts[layer][c][bass.ds(2 * k, 2)].rearrange("e p n -> p e n")
                                 ).then_inc(landed[g % SLOTS], 16)

                for b in range(2):
                    for c in range(3):
                        wait_tile_used(sp, g0 + 3 * b + c - SLOTS)
                        load_pair(b, b, c)
                with sp.Fori(1, PAIRS // 2) as j:
                    for b in range(2):
                        for c in range(3):
                            sp.wait_ge(tile_used, 2 * PAIRS * layer + 4 * j + 2 * b - 4 + (2 if c == 2 else 1))
                            load_pair(2 * j + b, b, c)
                sp.wait_ge(passes_ready, layer + 1)
                npass = sp.value_load(passes[0:1, layer:layer + 1], min_val=1, max_val=PASSES)
                with sp.If(npass > 1):
                    sp.wait_ge(added, 6 * PAIRS * (layer + 1))
                    with sp.Fori(1, npass) as p:
                        with sp.Fori(0, PAIRS) as k:
                            sp.wait_ge(more["added"], 6 * PAIRS * (p - 1) + 6 * k + 1)
                            for c in range(3):
                                sp.dma_start(ring[:, c, :].rearrange("p (e n) -> p e n", e=2),
                                             experts[layer][c][bass.ds(2 * k, 2)].rearrange("e p n -> p e n")
                                             ).then_inc(more["landed"], 16)
                    sp.wait_ge(ln_done, T * (2 * layer + 2))
            for t in range(2):
                sp.wait_ge(ln_done, T * (2 * DEPTH - 1) + t + 1)
                sp.dma_start(O[0][0, P * t:P * t + P, :], x[:, t, :]).then_inc(y_stored, 16)
            sp.wait_ge(ln_done, T * 2 * DEPTH)
            sp.dma_start(O[1].rearrange("b s d -> (b s) d"), x[0:ROWS[2], 2, :]).then_inc(y_stored, 16)
            sp.wait_ge(y_stored, 48)
            sp.wait_ge(stored, 16 * 4 * DEPTH)
            sp.wait_ge(hist_stored, 16)

        @block.gpsimd
        def _(pool):
            def load_norm(q):
                g, b = (I["ln1_g"], I["ln1_b"]) if q % 2 == 0 else (I["ln2_g"], I["ln2_b"])
                pool.dma_start(lnp[:, 0, :], g[q // 2:q // 2 + 1, :].to_broadcast([P, D])).then_inc(ln_loaded, 16)
                pool.dma_start(lnp[:, 1, :], b[q // 2:q // 2 + 1, :].to_broadcast([P, D])).then_inc(ln_loaded, 16)

            pool.memset(ident[:, :], 0.0).then_inc(pool_seq, 1)
            pool.memset(ones[:, :], 1.0).then_inc(pool_seq, 1)
            pool.memset(valid[:, :], 1.0).then_inc(pool_seq, 1)
            pool.memset(eps[:, :], EPS)
            pool.iota(iota_win[:, :], pattern=[[1, WIN]], base=0, channel_multiplier=0,
                      allow_small_or_imprecise_dtypes=True)
            pool.iota(iota_tok[:, :], pattern=[[1, TOK]], base=1, channel_multiplier=0,
                      allow_small_or_imprecise_dtypes=True)
            pool.iota(tokid[:, :], pattern=[[P, T]], base=1, channel_multiplier=1,
                      allow_small_or_imprecise_dtypes=True)
            pool.iota(thresholds[:, :], pattern=[[WIN, PASSES - 1]], base=WIN, channel_multiplier=0,
                      allow_small_or_imprecise_dtypes=True)
            pool.wait_ge(pool_seq, 3)
            pool.affine_select(out=ident[:, :], in_=ident[:, :], compare_op=ALU.not_equal, fill=1.0, base=0,
                               pattern=[[-1, P]], channel_multiplier=1)
            pool.affine_select(out=tri[:, :], in_=ones[:, :], compare_op=ALU.is_gt, fill=0.0, base=0,
                               pattern=[[1, P]], channel_multiplier=-1)
            pool.affine_select(out=valid[:, 2:3], in_=valid[:, 2:3], compare_op=ALU.is_gt, fill=0.0,
                               base=ROWS[2], pattern=[[0, 1]], channel_multiplier=-1).then_inc(consts_ready, 1)
            load_norm(0)
            pool.dma_start(O[6][0, :, 0:26, :], I["state_conv_a"][0, :, 4:30, :]).then_inc(hist_stored, 16)

            for layer in range(DEPTH):
                newp, news = (O[4], O[6]) if layer == 0 else (O[5], O[7])
                np_, ns_ = (30, 4) if layer == 0 else (2, 2)
                wait_drained(pool, layer, "newp")
                pool.dma_start(newp[0, 0], y[0:np_, 2, 0:CH]).then_inc(stored, 16)
                wait_drained(pool, layer, "news")
                dst = news[0, :, 26:30, :] if layer == 0 else news[0]
                pool.dma_start(dst, y[0:NB * ns_, 2, CH:2 * CH]).then_inc(stored, 16)
                wait_drained(pool, layer, "kv", 0, 1)
                pool.dma_start(O[2][layer, 0].rearrange("(m p) h d -> p m (h d)", p=P), kv[:, :, 0:CH]
                               ).then_inc(stored, 16)
                wait_drained(pool, layer, "kv", 1, 1)
                pool.dma_start(O[3][layer, 0].rearrange("(m p) h d -> p m (h d)", p=P), kv[:, :, CH:2 * CH]
                               ).then_inc(stored, 16)
                pool.wait_ge(ln_done, T * (2 * layer + 1))
                load_norm(2 * layer + 1)
                if layer + 1 < DEPTH:
                    pool.wait_ge(ln_done, T * (2 * layer + 2))
                    load_norm(2 * layer + 2)

        @block.scalar
        def _(act):
            copy = lambda out, in_: act.activation(out, in_, ACT.Copy)

            def norm_std(q):
                for t in range(T):
                    act.wait_ge(var_ready, T * q + t + 1)
                    act.activation(rstd[0:ROWS[t], t:t + 1], mv[0:ROWS[t], t, 1:2], ACT.Sqrt,
                                   bias=eps[0:ROWS[t], :]).then_inc(rstd_ready, 1)

            def drain(layer, *name):
                wait_filled(act, layer, *name)
                return psum_of(layer, *name)

            def load_small(layer):
                if layer == 0:
                    act.dma_start(prow[0:31, :], I["conv_a_w"][0]).then_inc(small_loaded[layer], 16)
                    act.dma_start(prow[31:32, :], I["conv_a_b"]).then_inc(small_loaded[layer], 16)
                    act.dma_start(prow[32:33, :], I["norm_a_g"]).then_inc(small_loaded[layer], 16)
                    act.dma_start(prow[33:34, :], I["norm_a_b"]).then_inc(small_loaded[layer], 16)
                    act.dma_start(y[0:120, 2, :].rearrange("r (q n) -> r q n", q=2),
                                   I["state_conv_a"][0].rearrange("(q b) r n -> (b r) q n", q=2)
                                   ).then_inc(small_loaded[layer], 16)
                else:
                    act.dma_start(prow[0:3, :], I["conv_b_w"][0]).then_inc(small_loaded[layer], 16)
                    act.dma_start(y[0:16, 2, 0:CH], I["state_conv_b"][0].rearrange("b r n -> (b r) n")
                                   ).then_inc(small_loaded[layer], 16)
                act.dma_start(wr[:, :, :], I["w_router"][layer].rearrange("(p c) e -> p c e", c=C)
                               ).then_inc(router_loaded[layer], 16)
                act.dma_start(rb[:, :], I["router_bias"][layer:layer + 1, :].to_broadcast([P, E])
                               ).then_inc(router_loaded[layer], 16)

            load_small(0)
            act.wait_ge(consts_ready, 1)
            for layer in range(DEPTH):
                more = more_sems[layer]
                done = drained["act"]

                def drain_memT():
                    for m in range(2):
                        for hf in range(2):
                            b = drain(layer, "memT", m, hf)
                            copy(memT[:, 4 * hf:4 * hf + 4, P * m:P * m + P], b.rearrange("p (c r) -> p c r", c=4)
                                 ).then_inc(done, 1)

                def drain_kv():
                    wait_filled(act, layer, "memT", 1, 1)
                    for n in range(2):
                        for m in range(2):
                            b = drain(layer, "kv", n, m)
                            copy(kv[:, m, 512 * n:512 * n + 512], b).then_inc(done, 1)
                    for hp in range(2):
                        b = drain(layer, "kT", hp)
                        copy(kT[:, 2 * hp:2 * hp + 2, :], b.rearrange("p (h q) -> p h q", h=2)).then_inc(done, 1)

                if layer == 1:
                    drain_memT()
                    norm_std(1)
                    act.wait_ge(ln_done, 6 * layer)
                    load_small(1)
                if layer == 1:
                    drain_kv()
                for t in range(T):
                    b = drain(layer, "xT", t, 0)
                    r = ROWS[t]
                    copy(xT[:, 0:4, START[t]:START[t] + r], b[:, 0:4 * r].rearrange("p (c r) -> p c r", c=4)).then_inc(done, 1)
                for m in range(4):
                    b = drain(layer, "g" if layer == 0 else "c", m)
                    act.activation(sig[:, m, :], b[:, 0:TOK], ACT.Sigmoid if layer == 0 else ACT.Copy).then_inc(done, 1)
                b = drain(layer, "params")
                n = NPARAM[layer]
                copy(pcol[:, :, 0:n], b[:, 0:CC * n].rearrange("p (c n) -> p c n", c=CC)).then_inc(done, 1)
                if layer == 1:
                    for m in range(4):
                        b = drain(layer, "b", m)
                        copy(ct[:, m, :], b[:, 0:TOK]).then_inc(done, 1)
                for m in range(4):
                    b = drain(layer, "q", m)
                    copy(qT[:, m, :], b[:, 0:TOK]).then_inc(done, 1)
                if layer == 0:
                    drain_memT()
                    drain_kv()
                np_, ns_ = (30, 32) if layer == 0 else (2, 16)
                b = drain(layer, "newp")
                copy(y[0:np_, 2, 0:CH], b[0:np_, :]).then_inc(done, 1)
                b = drain(layer, "news")
                copy(y[0:ns_, 2, CH:2 * CH], b[0:ns_, :]).then_inc(done, 1)
                for j, (hp, t) in enumerate([(hp, t) for hp in range(2) for t in range(2)]):
                    act.wait_ge(max_ready, 5 * layer + j + 1)
                    b = psum_of(layer, "sc", hp, t)
                    for i in range(2):
                        k = 2 * j + i
                        ins = act.activation(Pm[:, t, 2 * hp + i, :], b[:, MEM * i:MEM * i + MEM], ACT.Exp,
                                             bias=mx[:, k:k + 1], scale=SCALE, accum_out=sums[:, k:k + 1])
                    ins.then_inc(done, 1)
                for s in range(NB):
                    for hp in range(2):
                        b = drain(layer, "KT", s, hp)
                        copy(KT[s % 2][:, 2 * hp:2 * hp + 2, :], b.rearrange("p (h q) -> p h q", h=2)
                             ).then_inc(done, 1)
                act.wait_ge(max_ready, 5 * layer + 5)
                act.activation(Ps[:, :], ps[:, BANKS, 0:MEM], ACT.Exp, bias=mx[:, 8:9], scale=SCALE,
                               accum_out=sums[:, 8:9]).then_inc(done, 1)
                for h in range(H):
                    b = drain(layer, "PT", h)
                    copy(PT[:, h, :, :], b.rearrange("p (m q) -> p m q", m=2)).then_inc(done, 1)
                for h in range(H):
                    b = drain(layer, "o", h)
                    copy(catT[:, CC + h, 0:SEQ], b[:, 0:SEQ]).then_inc(done, 1)
                b = drain(layer, "PTs")
                act.wait_ge(spread_cleared, layer + 1)
                bv = b[:, 0:2 * P].rearrange("p (g s n) -> p g s n", g=2 * H, s=NB)
                copy(spread[:, :, 0:36 * (NB - 1)].rearrange("p g (s z) -> p g s z", z=36)[:, :, :, 0:NS],
                     bv[:, :, 0:NB - 1, :])
                copy(spread[:, :, 36 * (NB - 1):MEM], bv[:, :, NB - 1, :]).then_inc(done, 1)
                b = drain(layer, "os")
                copy(PTs[:, 0, :], b[:, 0:P]).then_inc(done, 1)
                b = drain(layer, "osT")
                copy(catT[:, CC:C, SEQ:TOK], b[:, 0:P].rearrange("p (h q) -> p h q", h=H)).then_inc(done, 1)
                if layer == 0:
                    b = drain(layer, "var")
                    act.activation(sig[:, 1, :], b[:, 0:TOK], ACT.Sqrt, bias=eps[:, :], scale=1.0 / CH).then_inc(done, 1)
                if layer == 0:
                    for cc in range(CC):
                        act.wait_ge(conv_ready, cc + 1)
                        act.activation(catT[:, cc, :], ct[:, cc, :], ACT.Silu, bias=pcol[:, cc, 33:34],
                                       scale=pcol[:, cc, 32:33]).then_inc(mix_ready, 1)
                norm_std(2 * layer)
                act.wait_ge(stored, 16 * (4 * layer + 4))
                for t in range(T):
                    b = drain(layer, "x1T", t, 0)
                    r = ROWS[t]
                    copy(xT[:, 0:4, START[t]:START[t] + r], b[:, 0:4 * r].rearrange("p (c r) -> p c r", c=4)).then_inc(done, 1)
                    part0 = xb[:, t, 0, :, :] if t < 2 else xb2[0:r, :, :]
                    copy(part0, x[0:r, t, :].rearrange("p (j c) -> p c j", c=C)).then_inc(part0_ready, 1)
                for t in range(T):
                    b = drain(layer, "logits", t)
                    act.activation(score[0:ROWS[t], t, :], b[0:ROWS[t], 0:E], ACT.Sigmoid).then_inc(done, 1)
                for t in range(T):
                    act.wait_ge(rest_ready, T * layer + t + 1)
                    rest = y[0:ROWS[t], t, :].rearrange("p (c j) -> p c j", c=C)
                    if t < 2:
                        copy(xb[:, t, 1, :, :], rest).then_inc(part1_ready, 1)
                    else:
                        copy(xb2[32:64, :, :], rest)
                        copy(xb2m[0:32, :, :], rest).then_inc(part1_ready, 1)
                for f in range(2):
                    b = drain(layer, "sgate", f)
                    act.activation(sig[:, f, :], b[:, 0:TOK], ACT.Silu).then_inc(done, 1)

                def copy_xs(k, b):
                    act.wait_ge(gathered, (PAIRS + 1) * layer + k + 1)
                    copy(xs[:, b, :, :].rearrange("p c s -> p (c s)"),
                         ps[:, GATHER:GATHER + 2, :].rearrange("p b n -> p (b n)")).then_inc(xs_ready, 1)

                def round_y(k):
                    act.wait_ge(tile_used, 2 * PAIRS * layer + 2 * k + 2)
                    copy(yh[:, :], ps[:, DOWN:DOWN + 2, :].rearrange("p b n -> p (b n)")).then_inc(yh_done, 1)

                def step(k, b):
                    act.wait_ge(tile_used, 2 * PAIRS * layer + 2 * k + 1)
                    act.activation(sg[:, :], ps[:, GU, 0:FF], ACT.Silu).then_inc(silu_done, 1)
                    copy_xs(k + 1, 1 - b)
                    act.wait_ge(hT_done, PAIRS * layer + k + 1)
                    copy(hT[:, :, :], ps[:, SMALL, 0:FF].rearrange("p (f s) -> p f s", f=2)).then_inc(hT_copied, 1)

                copy_xs(0, 0)
                step(0, 0)
                round_y(0)
                step(1, 1)
                with act.Fori(1, PAIRS // 2) as j:
                    for b in range(2):
                        round_y(2 * j + (b - 1))
                        step(2 * j + b, b)
                round_y(PAIRS - 1)

                act.wait_ge(passes_ready, layer + 1)
                npass = act.value_load(passes[0:1, layer:layer + 1], min_val=1, max_val=PASSES)
                with act.If(npass > 1):
                    with act.Fori(1, npass) as p:
                        with act.Fori(0, PAIRS) as k:
                            n = (p - 1) * PAIRS + k
                            act.wait_ge(more["gathered"], n + 1)
                            copy(xs[:, 0, :, :].rearrange("p c s -> p (c s)"),
                                 ps[:, GATHER:GATHER + 2, :].rearrange("p b n -> p (b n)")).then_inc(more["xs"], 1)
                            act.wait_ge(more["up"], n + 1)
                            act.activation(sg[:, :], ps[:, GU, 0:FF], ACT.Silu).then_inc(more["silu"], 1)
                            act.wait_ge(more["hT"], n + 1)
                            copy(hT[:, :, :], ps[:, SMALL, 0:FF].rearrange("p (f s) -> p f s", f=2)
                                 ).then_inc(more["hTc"], 1)
                            act.wait_ge(more["down"], n + 1)
                            copy(yh[:, :], ps[:, DOWN:DOWN + 2, :].rearrange("p b n -> p (b n)")
                                 ).then_inc(more["yh"], 1)
            norm_std(2 * DEPTH - 1)

        @block.vector
        def _(dve):
            links = [0]

            def link(ins):
                links[0] += 1
                ins.then_inc(dve_seq, 1)
                dve.wait_ge(dve_seq, links[0])

            done = drained["dve"]

            def drain(layer, *name):
                wait_filled(dve, layer, *name)
                return psum_of(layer, *name)

            def bcast(ap, shape):
                return ap.to_broadcast(shape)

            def conv_parts(layer):
                w = WIDTH[layer]
                return w, SEQ + w - 1, NS + w - 1

            def conv_taps(layer, cc, j0, j1):
                w, pw, sw = conv_parts(layer)
                for j in range(j0, j1):
                    for part in range(2):
                        if part == 0:
                            out = catT[:, cc, 0:SEQ]
                            src = cb[:, cc, j:j + SEQ]
                        else:
                            out = catT[:, cc, SEQ:TOK].rearrange("p (b s) -> p b s", b=NB)
                            src = cb[:, cc, pw:pw + NB * sw].rearrange("p (b s) -> p b s", b=NB)[:, :, j:j + NS]
                        if j == 0 and layer == 0:
                            ins = dve.tensor_scalar(out, src, pcol[:, cc, 0:1], pcol[:, cc, 31:32], ALU.mult, ALU.add)
                        elif j == 0:
                            ins = dve.tensor_scalar(out, src, pcol[:, cc, 0:1], None, ALU.mult)
                        else:
                            dve.wait_ge(dve_seq, links[0] - 1)
                            ins = dve.scalar_tensor_tensor(out, src, pcol[:, cc, j:j + 1], out, ALU.mult, ALU.add)
                        ins.then_inc(dve_seq, 1)
                        links[0] += 1

            def norm_stats(q, src, t):
                r = ROWS[t]
                for i in range(2):
                    ins = dve.bn_stats(bn[0:r, t, i, :], src[0:r, t, 512 * i:512 * i + 512])
                link(ins)
                dve.bn_aggr(mv[0:r, t, :], bn[0:r, t, :, :].rearrange("p a b -> p (a b)")).then_inc(var_ready, 1)

            def norm_apply(q, src, t):
                r = ROWS[t]
                dve.wait_ge(rstd_ready, T * q + t + 1)
                link(dve.reciprocal(rstd[0:r, t:t + 1], rstd[0:r, t:t + 1]))
                dve.wait_ge(ln_loaded, 32 * (q + 1))
                link(dve.scalar_tensor_tensor(x[0:r, t, :], src[0:r, t, :], mv[0:r, t, 0:1], lnp[0:r, 0, :],
                                              ALU.subtract, ALU.mult))
                dve.scalar_tensor_tensor(x[0:r, t, :], x[0:r, t, :], rstd[0:r, t:t + 1], lnp[0:r, 1, :],
                                         ALU.mult, ALU.add).then_inc(ln_done, 1)

            dve.wait_ge(consts_ready, 1)

            for layer in range(DEPTH):
                more = more_sems[layer]
                w, pw, sw = conv_parts(layer)
                for t in range(T):
                    b = drain(layer, "xT", t, 1)
                    r = ROWS[t]
                    dve.tensor_copy(xT[:, 4:8, START[t]:START[t] + r],
                                    b[:, 0:4 * r].rearrange("p (c r) -> p c r", c=4)).then_inc(done, 1)
                dve.memset(cb[:, :, 0:w - 1], 0.0)
                link(dve.memset(qm[:, :, :], 0.0))
                samples = cb[:, :, pw:pw + NB * sw].rearrange("p c (b s) -> p c b s", b=NB)
                for q in range(2 if layer == 0 else 1):
                    b = drain(layer, "hist", q)
                    nb = 4 if layer == 0 else 8
                    for cc in range(CC):
                        n = nb * (w - 1)
                        ins = dve.tensor_copy(samples[:, cc, nb * q:nb * q + nb, 0:w - 1],
                                              b[:, cc * n:cc * n + n].rearrange("p (b r) -> p b r", b=nb))
                    ins.then_inc(done, 1)
                steps = [(cc, j, min(j + 4, w)) for cc in range(CC) for j in range(0, w, 4)]

                def conv_some(n):
                    for _ in range(min(n, len(steps))):
                        conv_taps(layer, *steps.pop(0))

                wait_drained(dve, layer, "params")
                for m in range(CC):
                    b = drain(layer, "a" if layer == 0 else "h", m)
                    wait_drained(dve, layer, "g" if layer == 0 else "c", m)
                    dve.tensor_tensor(cb[:, m, w - 1:pw], b[:, 0:SEQ], sig[:, m, 0:SEQ], ALU.mult)
                    dve.tensor_tensor(samples[:, m, :, w - 1:sw], b[:, SEQ:TOK].rearrange("p (b s) -> p b s", b=NB),
                                      sig[:, m, SEQ:TOK].rearrange("p (b s) -> p b s", b=NB), ALU.mult
                                      ).then_inc(done, 1)
                    wait_drained(dve, layer, "a" if layer == 0 else "h", m)
                    if layer == 0:
                        conv_some(1)
                nn = min(w - 1, NS)
                dve.tensor_copy(new_cols(nn).rearrange("p c (b s) -> p c b s", b=NB), samples[:, :, :, sw - nn:sw])
                conv_some(BEFORE_QUERIES)
                for h in range(H):
                    wait_drained(dve, layer, "q", h)
                    ins = dve.tensor_copy(qm[:, h, :].rearrange("p (b z) -> p b z", z=36)[:, :, 0:NS],
                                          qT[:, h, SEQ:TOK].rearrange("p (b s) -> p b s", b=NB))
                ins.then_inc(qmask_ready, 1)
                dve.wait_ge(qmask_ready, layer + 1)

                conv_some(BEFORE_SCORES)
                order = [(hp, t) for hp in range(2) for t in range(2)]

                def soft_max(j):
                    b = drain(layer, "sc", *order[j])
                    link(dve.tensor_reduce(mx[:, 2 * j:2 * j + 2], b.rearrange("p (h q) -> p h q", h=2), AX.X, ALU.max))
                    dve.tensor_scalar(mx[:, 2 * j:2 * j + 2], mx[:, 2 * j:2 * j + 2], -SCALE, None, ALU.mult
                                      ).then_inc(max_ready, 1)

                def soft_norm(j):
                    hp, t = order[j]
                    wait_drained(dve, layer, "sc", hp, t)
                    link(dve.reciprocal(sums[:, 2 * j:2 * j + 2], sums[:, 2 * j:2 * j + 2]))
                    for i in range(2):
                        pr = Pm[:, t, 2 * hp + i, :]
                        ins = dve.tensor_scalar(pr, pr, sums[:, 2 * j + i:2 * j + i + 1], None, ALU.mult)
                    ins.then_inc(prob_ready, 1)

                def soft_norm_samples():
                    wait_drained(dve, layer, "scs")
                    link(dve.reciprocal(sums[:, 8:9], sums[:, 8:9]))
                    dve.tensor_scalar(Ps[:, :], Ps[:, :], sums[:, 8:9], None, ALU.mult).then_inc(prob_ready, 1)

                soft_max(0)
                for j in range(4):
                    if j + 1 < 4:
                        soft_max(j + 1)
                    soft_norm(j)
                conv_some(BEFORE_SAMPLES)
                drain(layer, "scs")
                link(dve.tensor_reduce(mx[:, 8:9], ps[:, BANKS, 0:MEM], AX.X, ALU.max))
                dve.tensor_scalar(mx[:, 8:9], mx[:, 8:9], -SCALE, None, ALU.mult).then_inc(max_ready, 1)
                conv_some(2)
                soft_norm_samples()
                conv_some(len(steps))
                if layer == 0:
                    conv_end.append(links[0])
                wait_filled(dve, layer, "newp")
                if links[0]:
                    dve.wait_ge(dve_seq, links[0])
                dve.memset(spread, 0.0).then_inc(spread_cleared, 1)
                if layer == 0:
                    b = drain(layer, "mean")
                    for cc in range(CC):
                        ins = dve.scalar_tensor_tensor(ct[:, cc, :], b[:, 0:TOK], -1.0 / CH, catT[:, cc, :],
                                                       ALU.mult, ALU.add)
                    ins.then_inc(done, 1)
                    wait_drained(dve, layer, "mean")
                    for cc in range(CC):
                        ins = dve.tensor_tensor(catT[:, cc, :], ct[:, cc, :], ct[:, cc, :], ALU.mult)
                    ins.then_inc(centred, 1)
                    wait_drained(dve, layer, "var")
                    link(dve.reciprocal(sig[:, 0, :], sig[:, 1, :]))
                    for cc in range(CC):
                        dve.tensor_tensor(ct[:, cc, :], ct[:, cc, :], sig[:, 0, :], ALU.mult).then_inc(conv_ready, 1)
                else:
                    wait_drained(dve, layer, "b", 3)
                    for cc in range(CC):
                        dve.tensor_tensor(catT[:, cc, :], catT[:, cc, :], ct[:, cc, :], ALU.mult).then_inc(mix_ready, 1)
                for t in range(T):
                    for n in range(2):
                        r = ROWS[t]
                        b = drain(layer, "out", t, n)
                        xv = x[0:r, t, 512 * n:512 * n + 512]
                        dve.scalar_tensor_tensor(xv, xv, ALPHA, b[0:r, :], ALU.mult, ALU.add).then_inc(done, 1)
                    wait_drained(dve, layer, "out", t, 1)
                    norm_stats(2 * layer, x, t)
                    if t > 0:
                        norm_apply(2 * layer, x, t - 1)
                norm_apply(2 * layer, x, T - 1)
                for t in range(T):
                    b = drain(layer, "x1T", t, 1)
                    r = ROWS[t]
                    dve.tensor_copy(xT[:, 4:8, START[t]:START[t] + r],
                                    b[:, 0:4 * r].rearrange("p (c r) -> p c r", c=4)).then_inc(done, 1)

                if layer == 0:
                    dve.wait_ge(stored, 16 * 4)
                else:
                    dve.wait_ge(stored, 16 * 8)
                dve.memset(slots[:, :, :], -1.0)
                dve.memset(score[32:64, 2, :], 0.0)
                dve.memset(score[64:128, 2, :], 0.0)
                link(dve.memset(grp[:, :, 8:12], -BIG))
                wait_drained(dve, layer, "logits", T - 1)
                dve.wait_ge(router_loaded[layer], 32)
                rbb = rb[:, :].unsqueeze(1).to_broadcast([P, T, E])
                link(dve.tensor_tensor(cand[:, :, :], score[:, :, :], rbb, ALU.add))
                for t in range(T):
                    for g in range(GROUPS):
                        ins = dve.max(top[:, t, g, :], cand[:, t, 8 * g:8 * g + 8])
                link(ins)
                link(dve.tensor_tensor(grp[:, :, 0:8], top[:, :, 0:8, 0], top[:, :, 0:8, 1], ALU.add))
                for t in range(T):
                    ins = dve.max(top[:, t, 8, :], grp[:, t, 0:8])
                link(ins)
                link(dve.memset(top[:, :, 8, TOP_GROUPS:8], -BIG))
                for t in range(T):
                    ins = dve.match_replace(out=grpr[:, t, :], in_to_replace=top[:, t, 8, :], in_values=grp[:, t, :],
                                            imm_value=BIG)
                link(ins)
                link(dve.tensor_scalar(grpr[:, :, 0:8], grpr[:, :, 0:8], BIG * 0.5, None, ALU.is_ge))
                link(dve.tensor_scalar(grp[:, :, 0:8], grpr[:, :, 0:8], BIG, -BIG, ALU.mult, ALU.add))
                c4 = cand[:, :, :].rearrange("p t (g e) -> p t g e", g=GROUPS)
                link(dve.tensor_tensor(c4, c4, grpr[:, :, 0:8].unsqueeze(3).to_broadcast([P, T, GROUPS, 8]), ALU.mult))
                link(dve.tensor_tensor(c4, c4, grp[:, :, 0:8].unsqueeze(3).to_broadcast([P, T, GROUPS, 8]), ALU.add))
                for t in range(T):
                    ins = dve.max(top[:, t, 0, :], cand[:, t, :])
                link(ins)
                for t in range(T):
                    ins = dve.match_replace(out=mask[:, t, :], in_to_replace=top[:, t, 0, :], in_values=cand[:, t, :],
                                            imm_value=BIG)
                link(ins)
                for t in range(T):
                    ins = dve.tensor_scalar(mask[:, t, :], mask[:, t, :], BIG * 0.5, valid[:, t:t + 1],
                                            ALU.is_ge, ALU.mult)
                ins.then_inc(mask_ready, 1)
                dve.wait_ge(mask_ready, layer + 1)
                for t in range(T):
                    ins = dve.tensor_tensor(gates[:, t, :], score[:, t, :], mask[:, t, :], ALU.mult)
                link(ins)
                link(dve.tensor_reduce(gsum[:, :], gates[:, :, :], AX.X, ALU.add))
                link(dve.reciprocal(gsum[:, :], gsum[:, :]))
                sl = slots[:, 0:PAIRS, :].rearrange("p k (t f) -> p k t f", t=T)
                for t in range(T):
                    r = ROWS[t]
                    dve.tensor_scalar(sl[0:r, :, t, 0:2], gates[0:r, t, :].rearrange("p (k h) -> p k h", h=2),
                                      gsum[0:r, t:t + 1], ROUTED, ALU.mult, ALU.mult)
                def rest_after(t):
                    r = ROWS[t]
                    dve.wait_ge(part0_ready, T * layer + t + 1)
                    part0 = xb[:, t, 0, :, :] if t < 2 else xb2[0:r, :, :]
                    dve.tensor_tensor(y[0:r, t, :].rearrange("p (c j) -> p c j", c=C),
                                      x[0:r, t, :].rearrange("p (j c) -> p c j", c=C), part0, ALU.subtract
                                      ).then_inc(rest_ready, 1)

                def part2_of(t):
                    r = ROWS[t]
                    dve.wait_ge(part1_ready, T * layer + t + 1)
                    part1, part2 = (xb[:, t, 1, :, :], xb[:, t, 2, :, :]) if t < 2 else (xb2m[0:r, :, :], xb2[64:96, :, :])
                    dve.tensor_tensor(part2, y[0:r, t, :].rearrange("p (c j) -> p c j", c=C), part1, ALU.subtract
                                      ).then_inc(part2_ready, 1)

                for t in range(T):
                    rest_after(t)
                for t in range(T):
                    part2_of(t)
                for f in range(2):
                    b = drain(layer, "sup", f)
                    wait_drained(dve, layer, "sgate", f)
                    dve.tensor_tensor(qT[:, f, :], b[:, 0:TOK], sig[:, f, :], ALU.mult).then_inc(done, 1)
                for t in range(T):
                    for n in range(2):
                        r = ROWS[t]
                        b = drain(layer, "sdown", t, n)
                        dve.scalar_tensor_tensor(y[0:r, t, 512 * n:512 * n + 512], x[0:r, t, 512 * n:512 * n + 512],
                                                 ALPHA, b[0:r, :], ALU.mult, ALU.add).then_inc(done, 1)
                for t in range(T):
                    r = ROWS[t]
                    b = drain(layer, "rank", t)
                    dve.scalar_tensor_tensor(cand[0:r, t, :], b[0:r, 0:E], 1.0, mask[0:r, t, :], ALU.add, ALU.mult
                                             ).then_inc(done, 1)
                wait_drained(dve, layer, "rank", T - 1)
                for t in range(T):
                    r = ROWS[t]
                    dve.tensor_scalar(sl[0:r, :, t, 2:4], cand[0:r, t, :].rearrange("p (k h) -> p k h", h=2),
                                      -1.0, None, ALU.add)
                b = drain(layer, "count")
                dve.tensor_reduce(passes_f[:, 0:1], b[0:1, 0:E], AX.X, ALU.max).then_inc(done, 1)
                wait_drained(dve, layer, "count")
                link(dve.tensor_scalar(passes_f[:, 1:PASSES], thresholds[:, :], passes_f[:, 0:1], None, ALU.is_lt))
                link(dve.tensor_reduce(passes_f[:, 6:7], passes_f[:, 1:PASSES], AX.X, ALU.add))
                dve.tensor_scalar(passes[:, layer:layer + 1], passes_f[:, 6:7], 1.0, None, ALU.add
                                  ).then_inc(passes_ready, 1)
                dve.wait_ge(passes_ready, layer + 1)
                for i in (1, 2):
                    ins = dve.tensor_copy(slots[32 * i:32 * i + 32, :, 8:12], slots[0:32, :, 8:12])
                link(ins)

                s0 = (PAIRS + 1) * layer
                for b in range(2):
                    dve.tensor_copy(cols[:, b, :, 4], tokid[:, :])

                def build_sel(k, b, iota, ready, built, n, shifted=None):
                    dve.tensor_copy(cols[:, b, :, 0:4], slots[:, :, :].rearrange("p k f -> p (k f)")[
                        :, bass.ds(12 * k, 12)].rearrange("p (t f) -> p t f", t=T)).then_inc(ready, 1)
                    dve.wait_ge(ready, n)
                    if shifted is not None:
                        dve.wait_ge(more["shift"], shifted)
                    dve.tensor_tensor(sel[:, b, :, :].rearrange("p t (h s) -> p t h s", h=2),
                                      iota[:, :].unsqueeze(1).unsqueeze(1).to_broadcast([P, T, 2, WIN]),
                                      cols[:, b, :, 2:4].unsqueeze(3).to_broadcast([P, T, 2, WIN]),
                                      ALU.is_equal)
                    dve.tensor_tensor(selb[:, b, :, :].rearrange("p t (h s) -> p t h s", h=2),
                                      iota[:, :].unsqueeze(1).unsqueeze(1).to_broadcast([P, T, 2, WIN]),
                                      cols[:, b, :, 2:4].unsqueeze(3).to_broadcast([P, T, 2, WIN]),
                                      ALU.is_equal).then_inc(built, 1)

                def take_slotv(b):
                    return dve.tensor_copy(slotv[:, b, :], ps[:, SMALL, FF:FF + 5])

                def build_back(b, built):
                    dve.tensor_copy(slotg[0:WIN, b:b + 1], slotv[0:WIN, b, 0:1])
                    dve.tensor_copy(slotg[WIN:P, b:b + 1], slotv[WIN:P, b, 1:2])
                    dve.tensor_scalar(back[:, b, :], iota_tok[:, :], slotv[:, b, 4:5], None, ALU.is_equal
                                      ).then_inc(built, 1)

                def swiglu(b):
                    return dve.scalar_tensor_tensor(hs[:, :], ps[:, GU, FF:2 * FF], slotg[:, b:b + 1], sg[:, :],
                                                    ALU.mult, ALU.mult)

                def low_y():
                    return dve.tensor_tensor(yl[:, :], ps[:, DOWN:DOWN + 2, :].rearrange("p b n -> p (b n)"),
                                             yh[:, :].bitcast(F32), ALU.subtract)

                def add_back(m):
                    t, n = m // 2, m % 2
                    r = ROWS[t]
                    yv = y[0:r, t, 512 * n:512 * n + 512]
                    return dve.tensor_tensor(yv, yv, ps[0:r, COMBINE + m % 2, :], ALU.add)

                def add_some(k, m0, m1):
                    for m in range(m0, m1):
                        dve.wait_ge(combined, 6 * PAIRS * layer + 6 * k + m + 1)
                        wait(dve, added, 6 * PAIRS * layer + 6 * k + m - 5)
                        add_back(m).then_inc(added, 1)

                def slots_of(k, b):
                    dve.wait_ge(slotv_ready, s0 + k + 1)
                    build_back(b, slots_ready)

                def select(k, b):
                    build_sel(k, b, iota_win, cols_ready, sel_built, s0 + k + 1)

                def step(k, b, first):
                    select(k + 1, 1 - b)
                    if not first:
                        dve.wait_ge(yh_done, PAIRS * layer + k)
                        low_y().then_inc(yl_done, 1)
                        add_some(k - 1, 0, 2)
                    dve.wait_ge(silu_done, PAIRS * layer + k + 1)
                    dve.wait_ge(slots_ready, s0 + k + 1)
                    swiglu(b).then_inc(h_done, 1)
                    if not first:
                        add_some(k - 1, 2, 3)
                    dve.wait_ge(slotv_mm, s0 + k + 2)
                    take_slotv(1 - b).then_inc(slotv_ready, 1)
                    if not first:
                        add_some(k - 1, 3, 6)
                    slots_of(k + 1, 1 - b)

                select(0, 0)
                dve.wait_ge(slotv_mm, s0 + 1)
                take_slotv(0).then_inc(slotv_ready, 1)
                slots_of(0, 0)
                step(0, 0, True)
                step(1, 1, False)
                with dve.Fori(1, PAIRS // 2) as j:
                    for b in range(2):
                        step(2 * j + b, b, False)
                dve.wait_ge(yh_done, PAIRS * (layer + 1))
                low_y().then_inc(yl_done, 1)
                add_some(PAIRS - 1, 0, 6)

                npass = dve.value_load(passes[0:1, layer:layer + 1], min_val=1, max_val=PASSES)
                with dve.If(npass > 1):
                    dve.wait_ge(added, 6 * PAIRS * (layer + 1))
                    dve.tensor_copy(window[:, 0:WIN // 2], iota_win[:, 0:WIN // 2]).then_inc(more["added"], 1)
                    dve.tensor_copy(window[:, WIN // 2:], iota_win[:, WIN // 2:]).then_inc(more["shift"], 1)
                    with dve.Fori(1, npass) as p:
                        dve.wait_ge(more["shift"], p)
                        dve.tensor_scalar(window[:, :], window[:, :], float(WIN), None,
                                          ALU.add).then_inc(more["shift"], 1)
                        with dve.Fori(0, PAIRS) as k:
                            n = (p - 1) * PAIRS + k
                            build_sel(k, 0, window, more["cols"], more["sel"], n + 1, p + 1)
                            dve.wait_ge(more["slotm"], n + 1)
                            take_slotv(0).then_inc(more["slotv"], 1)
                            dve.wait_ge(more["slotv"], n + 1)
                            build_back(0, more["slots"])
                            dve.wait_ge(more["silu"], n + 1)
                            dve.wait_ge(more["slots"], n + 1)
                            swiglu(0).then_inc(more["h"], 1)
                            dve.wait_ge(more["yh"], n + 1)
                            low_y().then_inc(more["yl"], 1)
                            for m in range(6):
                                dve.wait_ge(more["combined"], 6 * n + m + 1)
                                add_back(m).then_inc(more["added"], 1)
                            dve.wait_ge(more["added"], 6 * n + 7)
                dve.wait_ge(added, 6 * PAIRS * (layer + 1))
                for t in range(T):
                    norm_stats(2 * layer + 1, y, t)
                    if t > 0:
                        norm_apply(2 * layer + 1, y, t - 1)
                norm_apply(2 * layer + 1, y, T - 1)

        @block.tensor
        def _(pe):
            def start(layer, *name):
                bank, _, _, _, before = JOBS[(layer, *name)]
                if before is not None:
                    wait_drained(pe, *before)
                return ps[:, bank, :]

            def turn(out, in_, r, c):
                return pe.transpose(out, in_, ident[0:r, 0:r])

            pe.wait_ge(consts_ready, 1)
            pe.wait_ge(x_loaded, 32)
            for layer in range(DEPTH):
                more = more_sems[layer]
                w = WIDTH[layer]
                pw, sw = SEQ + w - 1, NS + w - 1

                def transpose_x(name, q):
                    for t in range(T):
                        if q >= 0:
                            pe.wait_ge(ln_done, T * q + t + 1)
                        r = ROWS[t]
                        xv = x[0:r, t, :].rearrange("p (j c) -> p c j", c=C)
                        for hf in range(2):
                            b = start(layer, name, t, hf)
                            for c in range(4):
                                ins = turn(b[:, r * c:r * c + r], xv[:, 4 * hf + c, :], r, P)
                            ins.then_inc(filled, 1)

                def project_memory():
                    pe.wait_ge(mem_loaded[layer], 16)
                    for m in range(2):
                        mv_ = kv[:, m, :].rearrange("p (j c) -> p c j", c=C)
                        for hf in range(2):
                            b = start(layer, "memT", m, hf)
                            for c in range(4):
                                ins = turn(b[:, P * c:P * c + P], mv_[:, 4 * hf + c, :], P, P)
                            ins.then_inc(filled, 1)
                    wait_drained(pe, layer, "memT", 1, 1)
                    for n in range(2):
                        tn = tile_no(layer, "kv", n)
                        wait_tile(pe, layer, tn)
                        wt = tile_at(layer, tn).rearrange("p (c n) -> p c n", c=C)
                        for m in range(2):
                            b = start(layer, "kv", n, m)
                            for c in range(C):
                                ins = pe.matmul(b, memT[:, c, P * m:P * m + P], wt[:, c, :], start=c == 0, stop=c == C - 1)
                            ins.then_inc(filled, 1)
                    wait_drained(pe, layer, "kv", 0, 1)
                    for hp in range(2):
                        b = start(layer, "kT", hp)
                        for i in range(2):
                            for m in range(2):
                                h = 2 * hp + i
                                ins = turn(b[:, MEM * i + P * m:MEM * i + P * m + P], kv[:, m, HD * h:HD * h + HD], P, P)
                        ins.then_inc(filled, 1)

                def turn_small():
                    b = start(layer, "params")
                    pe.wait_ge(small_loaded[layer], 16 * (5 if layer == 0 else 2))
                    n = NPARAM[layer]
                    for cc in range(CC):
                        ins = turn(b[:, n * cc:n * cc + n], prow[0:n, P * cc:P * cc + P], n, P)
                    ins.then_inc(filled, 1)
                    for q in range(2 if layer == 0 else 1):
                        b = start(layer, "hist", q)
                        n = (4 if layer == 0 else 8) * (w - 1)
                        for cc in range(CC):
                            ins = turn(b[:, n * cc:n * cc + n], y[0:n, 2, CH * q + P * cc:CH * q + P * cc + P], n, P)
                        ins.then_inc(filled, 1)

                if layer == 1:
                    pe.wait_ge(added, 6 * PAIRS * layer)
                    project_memory()
                transpose_x("xT", 2 * layer - 1)
                wait_drained(pe, layer, "xT", T - 1, 0)
                wait_drained(pe, layer, "xT", T - 1, 1)
                for n, part in enumerate(IN_PARTS[layer]):
                    wait_tile(pe, layer, tile_no(layer, "in", n))
                    wt = tile_at(layer, tile_no(layer, "in", n)).rearrange("p (c n) -> p c n", c=C)
                    for m in range(4):
                        b = start(layer, part, m)
                        for c in range(C):
                            ins = pe.matmul(b[:, 0:TOK], wt[:, c, P * m:P * m + P], xT[:, c, :], start=c == 0, stop=c == C - 1)
                        ins.then_inc(filled, 1)
                    if n == 0:
                        turn_small()
                if layer == 0:
                    project_memory()
                wait_drained(pe, layer, "a" if layer == 0 else "h", 3)
                b = start(layer, "newp")
                n = w - 1
                for cc in range(CC):
                    ins = turn(b[0:n, P * cc:P * cc + P], cb[:, cc, pw - n:pw], P, n)
                ins.then_inc(filled, 1)
                b = start(layer, "news")
                n = min(w - 1, NS)
                pe.wait_ge(qmask_ready, layer + 1)
                for cc in range(CC):
                    ins = turn(b[0:NB * n, P * cc:P * cc + P], new_cols(n)[:, cc, :], P, NB * n)
                ins.then_inc(filled, 1)
                wait_drained(pe, layer, "kT", 1)
                wait_drained(pe, layer, "q", 3)
                for hp in range(2):
                    for t in range(2):
                        b = start(layer, "sc", hp, t)
                        for i in range(2):
                            h = 2 * hp + i
                            ins = pe.matmul(b[:, MEM * i:MEM * i + MEM], qT[:, h, P * t:P * t + P], kT[:, h, :],
                                            start=True, stop=True)
                        ins.then_inc(filled, 1)

                def sample_scores(s):
                    wait_drained(pe, layer, "KT", s, 1)
                    for h in range(H):
                        ins = pe.matmul(ps[32 * h:32 * h + 32, BANKS, 0:MEM], qm[:, h, 32 * s:32 * s + 32],
                                        KT[s % 2][:, h, :], start=s == 0, stop=s == NB - 1)
                    return ins

                for s in range(NB):
                    if s % 4 == 0:
                        tn = tile_no(layer, "K", s // 4)
                        wait_tile(pe, layer, tn)
                        kt = tile_at(layer, tn).rearrange("p (b m n) -> p b m n", b=4, m=2)
                    for hp in range(2):
                        b = start(layer, "KT", s, hp)
                        for i in range(2):
                            for m in range(2):
                                h = 2 * hp + i
                                ins = turn(b[:, MEM * i + P * m:MEM * i + P * m + P],
                                           kt[:, s % 4, m, HD * h:HD * h + HD], P, P)
                        ins.then_inc(filled, 1)
                    if s >= 1:
                        sample_scores(s - 1)
                ins = sample_scores(NB - 1)
                ins.then_inc(filled, 1)
                for h in range(H):
                    pe.wait_ge(prob_ready, 5 * layer + 2 * (h // 2) + 2)
                    b = start(layer, "PT", h)
                    for m in range(2):
                        for t in range(2):
                            ins = turn(b[:, MEM * m + P * t:MEM * m + P * t + P], Pm[:, t, h, P * m:P * m + P], P, P)
                    ins.then_inc(filled, 1)
                wait_drained(pe, layer, "kv", 1, 1)
                for h in range(H):
                    wait_drained(pe, layer, "PT", h)
                    b = start(layer, "o", h)
                    for m in range(2):
                        ins = pe.matmul(b[:, 0:SEQ], kv[:, m, CH + HD * h:CH + HD * h + HD], PT[:, h, m, :],
                                        start=m == 0, stop=m == 1)
                    ins.then_inc(filled, 1)
                pe.wait_ge(prob_ready, 5 * layer + 5)
                b = start(layer, "PTs")
                for m in range(2):
                    ins = turn(b[:, P * m:P * m + P], Ps[:, P * m:P * m + P], P, P)
                ins.then_inc(filled, 1)
                wait_drained(pe, layer, "PTs")
                b = start(layer, "os")
                for s in range(NB):
                    tn = tile_no(layer, "V", s // 4)
                    if s % 4 == 0:
                        wait_tile(pe, layer, tn)
                    vt = tile_at(layer, tn).rearrange("p (b m n) -> p b m n", b=4, m=2)
                    for m in range(2):
                        for h in range(H):
                            ins = pe.matmul(b[32 * h:32 * h + 32, 0:P], spread[:, H * m + h, 32 * s:32 * s + 32],
                                            vt[:, s % 4, m, HD * h:HD * h + HD],
                                            start=s == 0 and m == 0, stop=s == NB - 1 and m == 1)
                ins.then_inc(filled, 1)
                wait_drained(pe, layer, "os")
                b = start(layer, "osT")
                turn(b[:, 0:P], PTs[:, 0, :], P, P).then_inc(filled, 1)
                if layer == 0:
                    pe.wait_ge(dve_seq, conv_end[0])
                    b = start(layer, "mean")
                    for cc in range(CC):
                        ins = pe.matmul(b[:, 0:TOK], ones[:, :], catT[:, cc, :], start=cc == 0, stop=cc == CC - 1)
                    ins.then_inc(filled, 1)
                    pe.wait_ge(centred, 1)
                    b = start(layer, "var")
                    for cc in range(CC):
                        ins = pe.matmul(b[:, 0:TOK], ones[:, :], catT[:, cc, :], start=cc == 0, stop=cc == CC - 1)
                    ins.then_inc(filled, 1)
                wait_drained(pe, layer, "osT")
                pe.wait_ge(mix_ready, 4 * layer + 4)
                for t in range(T):
                    for n in range(2):
                        tn = tile_no(layer, "out", n)
                        if t == 0:
                            wait_tile(pe, layer, tn)
                        wt = tile_at(layer, tn).rearrange("p (c n) -> p c n", c=C)
                        r = ROWS[t]
                        b = start(layer, "out", t, n)
                        for c in range(C):
                            ins = pe.matmul(b[0:r, :], catT[:, c, START[t]:START[t] + r], wt[:, c, :],
                                            start=c == 0, stop=c == C - 1)
                        ins.then_inc(filled, 1)
                transpose_x("x1T", 2 * layer)
                wait_drained(pe, layer, "x1T", T - 1, 0)
                wait_drained(pe, layer, "x1T", T - 1, 1)
                pe.wait_ge(router_loaded[layer], 32)
                for t in range(T):
                    r = ROWS[t]
                    b = start(layer, "logits", t)
                    for c in range(C):
                        ins = pe.matmul(b[0:r, 0:E], xT[:, c, START[t]:START[t] + r], wr[:, c, :],
                                        start=c == 0, stop=c == C - 1)
                    ins.then_inc(filled, 1)
                tn = tile_no(layer, "sgu")
                wait_tile(pe, layer, tn)
                for i, part in enumerate(["sgate", "sup"]):
                    wt = tile_at(layer, tn)[:, 2048 * i:2048 * i + 2048].rearrange("p (c j f) -> p c f j", c=C, f=2)
                    for f in range(2):
                        b = start(layer, part, f)
                        for c in range(C):
                            ins = pe.matmul(b[:, 0:TOK], wt[:, c, f, :], xT[:, c, :], start=c == 0, stop=c == C - 1)
                        ins.then_inc(filled, 1)
                tn = tile_no(layer, "sd")
                wait_tile(pe, layer, tn)
                wt = tile_at(layer, tn)[:, 0:2048].rearrange("p (f n) -> p f n", f=2)
                wait_drained(pe, layer, "sup", 1)
                for t in range(T):
                    r = ROWS[t]
                    for n in range(2):
                        b = start(layer, "sdown", t, n)
                        for f in range(2):
                            ins = pe.matmul(b[0:r, :], qT[:, f, START[t]:START[t] + r], wt[:, f, 512 * n:512 * n + 512],
                                            start=f == 0, stop=f == 1)
                        ins.then_inc(filled, 1)
                pe.wait_ge(mask_ready, layer + 1)
                for t in range(T):
                    r = ROWS[t]
                    b = start(layer, "rank", t)
                    for u in range(t):
                        pe.matmul(b[0:r, 0:E], ones[:, 0:r], mask[:, u, :], start=u == 0, stop=False)
                    pe.matmul(b[0:r, 0:E], tri[0:r, 0:r], mask[0:r, t, :], start=t == 0, stop=True).then_inc(filled, 1)
                b = start(layer, "count")
                for t in range(T):
                    ins = pe.matmul(b[:, 0:E], ones[:, :], mask[:, t, :], start=t == 0, stop=t == T - 1)
                ins.then_inc(filled, 1)

                s0 = (PAIRS + 1) * layer
                g0 = FIRST_TILE[layer] + MIX_TILES[layer]

                def slot_mm(b):
                    for t in range(T):
                        r = ROWS[t]
                        ins = pe.matmul(ps[:, SMALL, FF:FF + 5], sel[0:r, b, t, :], cols[0:r, b, t, :],
                                        start=t == 0, stop=t == T - 1)
                    return ins

                def gather_mm(b):
                    for c in range(C):
                        out = ps[:, GATHER + c // 4, P * (c % 4):P * (c % 4) + P]
                        for t in range(2):
                            for part in range(3):
                                pe.matmul(out, xb[:, t, part, c, :], selb[:, b, t, :],
                                          start=t == 0 and part == 0, stop=False)
                        ins = pe.matmul(out, xb2[0:96, c, :], selb[0:96, b, 2, :], start=False, stop=True)
                    return ins

                def hidden_mm(slot, b, c0, c1):
                    wt = ring[:, slot:slot + 2, :].rearrange("p u (e c f) -> p e c u f", e=2, c=C)
                    for c in range(c0, c1):
                        for e in range(2):
                            ins = pe.matmul(ps[WIN * e:WIN * e + WIN, GU, :], xs[:, b, c, WIN * e:WIN * e + WIN],
                                            wt[:, e, c, :, :], start=c == 0, stop=c == C - 1)
                    return ins

                def turn_hidden():
                    hv = hs[:, :].rearrange("p (j f) -> p f j", f=2)
                    for f in range(2):
                        ins = turn(ps[:, SMALL, P * f:P * f + P], hv[:, f, :], P, P)
                    return ins

                def down_mm(slot):
                    wt = ring[:, slot, :].rearrange("p (e f n) -> p e f n", e=2, f=2)
                    for n in range(2):
                        for f in range(2):
                            for e in range(2):
                                ins = pe.matmul(ps[WIN * e:WIN * e + WIN, DOWN + n, :], hT[:, f, WIN * e:WIN * e + WIN],
                                                wt[:, e, f, 512 * n:512 * n + 512], start=f == 0, stop=f == 1)
                    return ins

                def combine_mm(m, b):
                    t, n = m // 2, m % 2
                    r = ROWS[t]
                    for half in (yh, yl):
                        ins = pe.matmul(ps[0:r, COMBINE + m % 2, :], back[:, b, START[t]:START[t] + r],
                                        half[:, 512 * n:512 * n + 512], start=half is yh, stop=half is yl)
                    return ins

                def gather(k, b):
                    pe.wait_ge(sel_built, s0 + k + 1)
                    wait(pe, hT_copied, PAIRS * layer + k - 1)
                    slot_mm(b).then_inc(slotv_mm, 1)
                    wait(pe, xs_ready, s0 + k)
                    gather_mm(b).then_inc(gathered, 1)

                def combine(k, b, m0, m1):
                    if m0 == 0:
                        pe.wait_ge(yh_done, PAIRS * layer + k + 1)
                        pe.wait_ge(yl_done, PAIRS * layer + k + 1)
                        pe.wait_ge(slots_ready, s0 + k + 1)
                    for m in range(m0, m1):
                        wait(pe, added, 6 * PAIRS * layer + 6 * k + m - 1)
                        combine_mm(m, b).then_inc(combined, 1)

                def arrived(c, k, j, b):
                    g = g0 + 3 * b + c
                    pe.wait_ge(landed[g % SLOTS], landing[g] + 16 * j)

                def step(k, j, b, first):
                    pe.wait_ge(xs_ready, s0 + k + 1)
                    wait(pe, h_done, PAIRS * layer + k)
                    arrived(0, k, j, b)
                    arrived(1, k, j, b)
                    slot = (g0 + 3 * b) % SLOTS
                    hidden_mm(slot, b, 0, C // 2)
                    if not first:
                        combine(k - 1, 1 - b, 0, 2)
                    hidden_mm(slot, b, C // 2, C).then_inc(tile_used, 1)
                    if not first:
                        combine(k - 1, 1 - b, 2, 4)
                    gather(k + 1, 1 - b)
                    pe.wait_ge(h_done, PAIRS * layer + k + 1)
                    pe.wait_ge(slotv_ready, s0 + k + 2)
                    turn_hidden().then_inc(hT_done, 1)
                    if not first:
                        combine(k - 1, 1 - b, 4, 6)
                    pe.wait_ge(hT_copied, PAIRS * layer + k + 1)
                    arrived(2, k, j, b)
                    down_mm((g0 + 3 * b + 2) % SLOTS).then_inc(tile_used, 1)

                for t in range(T):
                    pe.wait_ge(part2_ready, T * layer + t + 1)
                wait_drained(pe, layer, "count")
                wait_drained(pe, layer, "sgate", 1)
                gather(0, 0)
                step(0, 0, 0, True)
                step(1, 0, 1, False)
                with pe.Fori(1, PAIRS // 2) as j:
                    for b in range(2):
                        step(2 * j + b, j, b, False)
                combine(PAIRS - 1, 1, 0, 6)

                pe.wait_ge(passes_ready, layer + 1)
                npass = pe.value_load(passes[0:1, layer:layer + 1], min_val=1, max_val=PASSES)
                with pe.If(npass > 1):
                    pe.wait_ge(added, 6 * PAIRS * (layer + 1))
                    with pe.Fori(1, npass) as p:
                        with pe.Fori(0, PAIRS) as k:
                            n = (p - 1) * PAIRS + k
                            pe.wait_ge(more["added"], 6 * n + 1)
                            pe.wait_ge(more["sel"], n + 1)
                            slot_mm(0).then_inc(more["slotm"], 1)
                            gather_mm(0).then_inc(more["gathered"], 1)
                            pe.wait_ge(more["xs"], n + 1)
                            pe.wait_ge(more["landed"], 48 * n + 48)
                            hidden_mm(0, 0, 0, C).then_inc(more["up"], 1)
                            pe.wait_ge(more["h"], n + 1)
                            pe.wait_ge(more["slotv"], n + 1)
                            turn_hidden().then_inc(more["hT"], 1)
                            pe.wait_ge(more["hTc"], n + 1)
                            down_mm(2).then_inc(more["down"], 1)
                            pe.wait_ge(more["yl"], n + 1)
                            pe.wait_ge(more["slots"], n + 1)
                            for m in range(6):
                                pe.wait_ge(more["added"], 6 * n + m + 1)
                                combine_mm(m, 0).then_inc(more["combined"], 1)
                            pe.wait_ge(more["added"], 6 * n + 7)


INS = ["x_prompt", "x_sample", "mem_prompt", "cache_mem_k", "cache_mem_v", "state_conv_a", "state_conv_b",
       "w_in_a", "conv_a_w", "conv_a_b", "norm_a_g", "norm_a_b", "w_in_b", "conv_b_w", "w_kv", "w_out", "ln1_g",
       "ln1_b", "w_router", "router_bias", "w_gate", "w_up", "w_down", "ws_gate", "ws_up", "ws_down", "ln2_g", "ln2_b"]
OUTS = [(1, 256, 1024), (8, 4, 1024), (2, 1, 256, 4, 128), (2, 1, 256, 4, 128), (1, 1, 30, 512), (1, 1, 2, 512),
        (1, 8, 30, 512), (1, 8, 2, 512)]


def kernel(**inputs):
    import numpy as np
    import concourse.bacc as bacc
    from concourse.bass_utils import run_bass_kernel_spmd

    nc = bacc.Bacc("TRN2", target_bir_lowering=False, num_devices=1)
    arrays, ins = {}, {}
    for name in INS:
        a = np.ascontiguousarray(inputs[name])
        arrays[f"in_{name}"] = a
        ins[name] = nc.dram_tensor(f"in_{name}", a.shape, mybir.dt.from_np(a.dtype), kind="ExternalInput").ap()
    outs = [nc.dram_tensor(f"out_{i}", shape, F32, kind="ExternalOutput").ap() for i, shape in enumerate(OUTS)]
    build_program(nc, ins, outs)
    r = run_bass_kernel_spmd(nc, [arrays], core_ids=[0])
    return tuple(r.results[0][f"out_{i}"] for i in range(len(OUTS)))
```

```python
from contextlib import ExitStack

import concourse.bass as bass
from concourse import mybir

F32 = mybir.dt.float32
F32R = mybir.dt.float32r
BF16 = mybir.dt.bfloat16
I32 = mybir.dt.int32
ALU = mybir.AluOpType
ACT = mybir.ActivationFunctionType
AX = mybir.AxisListType

P = 128
D = 1024
C = D // P
SEQ, NB, NS = 256, 8, 4
TOK = SEQ + NB * NS
ROWS = [P, P, NB * NS]
START = [0, P, 2 * P]
T = len(ROWS)
CH = 512
CC = CH // P
H, HD, MEM = 4, 128, 256
DEPTH = 2
ALPHA = (2 * DEPTH) ** 0.25
EPS = 1e-5
SCALE = HD ** -0.5
WIDTH = [31, 3]
E, FF = 64, 256
GROUPS, TOP_GROUPS, ROUTED = 8, 4, 2.5
PAIRS = E // 2
WIN = 64
PASSES = -(-TOK // WIN)
NPARAM = [34, 3]
BIG = 1e30
SLOTS = 6
MIX_TILES = [13, 14]
FIRST_TILE = [0, MIX_TILES[0] + 3 * PAIRS]
NORM_ORDER = [[2, 0, 1], [0, 1, 2]]
NORM1_GROUPS = [[2, 0], [1]]
SUMS = 5
BANKS = 7


def job_list(layer):
    memory = [(("memT", m, hf), "act") for m in range(2) for hf in range(2)]
    memory += [(("kv", n, m), "act") for n in range(2) for m in range(2)]
    memory += [(("kT", hp), "act") for hp in range(2)]
    jobs = [(("xT", t, hf), "act" if hf == 0 else "dve") for t in range(T) for hf in range(2)]
    small = [(("params",), "act")] + [(("hist", q), "dve") for q in range(2 if layer == 0 else 1)]
    if layer == 0:
        jobs += [(("g", m), "act") for m in range(4)] + small + [(("a", m), "dve") for m in range(4)]
    else:
        jobs = memory + jobs + [(("c", m), "act") for m in range(4)] + small
        jobs += [(("h", m), "dve") for m in range(4)] + [(("b", m), "act") for m in range(4)]
    jobs += [(("q", m), "act") for m in range(4)]
    if layer == 0:
        jobs += memory
    jobs += [(("newp",), "act"), (("news",), "act")]
    jobs += [(("KT", b, hp), "act") for b in range(2) for hp in range(2)]
    jobs += [(("sc", hp, t), "act") for hp in range(2) for t in range(2)]
    jobs += [(("KT", b, hp), "act") for b in range(2, NB) for hp in range(2)]
    jobs += [(("scs",), "act")]
    jobs += [(("PT", h), "act") for h in range(H)]
    jobs += [(("mean",), "dve")] if layer == 0 else []
    jobs += [(("o", h), "act") for h in range(H)]
    jobs += [(("var",), "act")] if layer == 0 else []
    jobs += [(("PTs",), "act"), (("os",), "act"), (("osT",), "act")]
    jobs += [(("out", 2), "dve")] + [(("out", t, n), "dve") for t in range(2) for n in range(2)]
    for group in NORM1_GROUPS:
        jobs += [(("x1T", t, hf), "act" if hf == 0 or t != 1 else "dve") for t in group for hf in range(2)]
        jobs += [(("logits", t), "act") for t in group]
    jobs += [(("sgate", f), "act") for f in range(2)] + [(("sup", f), "dve") for f in range(2)]
    jobs += [(("sdown", 2), "dve")] + [(("sdown", t, n), "dve") for t in range(2) for n in range(2)]
    jobs += [(("rank", t), "dve") for t in range(T)] + [(("count",), "dve")]
    return jobs


def number_jobs():
    table, count = {}, {"pe": 0, "act": 0, "dve": 0}
    for layer in range(DEPTH):
        holder, turn = {}, 0
        for name, drainer in job_list(layer):
            if name == ("scs",):
                bank = BANKS
            else:
                bank, turn = turn % BANKS, turn + 1
            count["pe"] += 1
            count[drainer] += 1
            table[(layer, *name)] = (bank, count["pe"], drainer, count[drainer], holder.get(bank))
            holder[bank] = (layer, *name)
    return table


JOBS = number_jobs()


def build_program(nc, I, O):
    with ExitStack() as ctx:
        sem = lambda name: ctx.enter_context(nc.semaphore(name))
        sb = lambda name, shape, dt=F32: ctx.enter_context(nc.sbuf_tensor(name, shape, dt))

        ring = sb("ring", [P, SLOTS, 4096])
        x = sb("x", [P, T, D])
        y = sb("y", [P, T, D])
        xT = sb("xT", [P, C, TOK])
        lnp = sb("lnp", [P, 2, D])
        ident = sb("ident", [P, P])
        tri = sb("tri", [P, P])
        ones = sb("ones", [P, P])
        eps = sb("eps", [P, 1])
        spare = sb("spare", [P, 1])
        iota_win = sb("iota_win", [P, WIN])
        iota_tok = sb("iota_tok", [P, TOK])
        valid = sb("valid", [P, T])
        tokid = sb("tokid", [P, T, 2])
        thresholds = sb("thresholds", [1, PASSES - 1])
        passes = sb("passes", [1, DEPTH], I32)
        passes_f = sb("passes_f", [1, 8])
        bn = sb("bn", [P, T, 2, 6])
        mv = sb("mv", [P, T, 2])
        rstd = sb("rstd", [P, T])
        top = sb("top", [P, T, 9, 8])
        grp = sb("grp", [P, T, 12])
        grpr = sb("grpr", [P, T, 12])
        gsum = sb("gsum", [P, T])
        mx = sb("mx", [P, 10])
        sums = sb("sums", [P, 10])

        mix = ExitStack()
        mb = lambda name, shape, dt=F32: mix.enter_context(nc.sbuf_tensor(name, shape, dt))
        kv = mb("kv", [P, 2, D])
        memT = mb("memT", [P, C, MEM])
        window_cols = SEQ + WIDTH[0] - 1 + NB * (NS + WIDTH[0] - 1)
        cb = mb("cb", [P, CC, window_cols])
        catT = mb("catT", [P, C, TOK])
        kT = mb("kT", [P, H, MEM])
        qm = mb("qm", [P, H, NB * (32 + NS)])
        prow = mb("prow", [NPARAM[0], CH])
        Ps = mb("Ps", [P, MEM])
        PTs = mb("PTs", [P, 2, P])
        pcol = mb("pcol", [P, CC, NPARAM[0]])
        sig = mb("sig", [P, CC, TOK])
        ct = mb("ct", [P, CC, TOK])
        qT = mb("qT", [P, H, TOK])
        wr = mb("wr", [P, C, E])
        rb = mb("rb", [P, E])
        mix.close()
        PT = memT.rearrange("p (h m) q -> p h m q", h=H)
        Pm = y[:, 0:2, :].rearrange("p t (h q) -> p t h q", h=H)
        KT = [xT[:, :, :].rearrange("p c q -> p (c q)")[:, 1024 * b:1024 * b + 1024]
              .rearrange("p (h q) -> p h q", h=H) for b in range(2)]

        spread = cb[:, :, :].rearrange("p c n -> p (c n)")[:, 0:2 * H * MEM].rearrange("p (g z) -> p g z", z=MEM)

        new_cols = lambda n: PTs[:, :, :].rearrange("p m q -> p (m q)")[:, 0:CC * NB * n].rearrange(
            "p (c s) -> p c s", c=CC)

        xb = sb("xb", [P, 2, 3, C, P], BF16)
        xb2 = sb("xb2", [P, C, P], BF16)
        xb2m = sb("xb2m", [P, C, P], BF16)
        ranks = sb("ranks", [P, PAIRS + 1, 2 * T])
        gparts = sb("gparts", [P, PAIRS + 1, 6 * T], BF16)
        score = sb("score", [P, T, E])
        cand = sb("cand", [P, T, E])
        mask = sb("mask", [P, T, E])
        gates = sb("gates", [P, T, E])
        xs = sb("xs", [P, 2, C, P])
        yf = sb("yf", [P, D])
        yh = sb("yh", [P, D], F32R)
        yl = sb("yl", [P, D], F32R)
        selb = sb("selb", [P, 2, T, P], BF16)
        back = sb("back", [P, 2, TOK], F32R)
        rankc = sb("rankc", [P, 2, T, 2])
        cols = sb("cols", [P, 2, T, 8], BF16)
        slotv = sb("slotv", [P, 2, 2])
        sg = sb("sg", [P, FF])
        hs = sb("hs", [P, FF])
        hT = sb("hT", [P, 2, P])
        window = sb("window", [P, WIN])
        rest = [yf[:, :].rearrange("p (c j) -> p c j", c=C), xs[:, 0, :, :], xs[:, 1, :, :]]

        ps = ctx.enter_context(nc.psum_tensor("ps", [P, 8, 512], F32))
        GATHER, GU, SMALL, DOWN, COMBINE = 0, 2, 3, 4, 6

        x_loaded = sem("x_loaded")
        mem_loaded = [sem(f"mem_loaded{layer}") for layer in range(DEPTH)]
        small_loaded = [sem(f"small_loaded{layer}") for layer in range(DEPTH)]
        router_loaded = [sem(f"router_loaded{layer}") for layer in range(DEPTH)]
        ln_loaded = sem("ln_loaded")
        first_landed = [sem(f"first_landed{m}") for m in range(4)]
        landed = [sem(f"landed{s}") for s in range(SLOTS)]
        tile_used = sem("tile_used")
        consts_ready = sem("consts_ready")
        pool_seq = sem("pool_seq")
        filled = sem("filled")
        drained = {"act": sem("drained_act"), "dve": sem("drained_dve")}
        dve_seq = sem("dve_seq")
        max_ready = sem("max_ready")
        prob_ready = sem("prob_ready")
        qmask_ready = sem("qmask_ready")
        spread_cleared = sem("spread_cleared")
        centred = sem("centred")
        var_ready = sem("var_ready")
        rstd_ready = sem("rstd_ready")
        ln_done = sem("ln_done")
        conv_ready = sem("conv_ready")
        mix_ready = sem("mix_ready")
        part0_ready = sem("part0_ready")
        rest_ready = [sem(f"rest_ready{t}") for t in range(T)]
        part1_ready = [sem(f"part1_ready{t}") for t in range(T)]
        part2_ready = [sem(f"part2_ready{t}") for t in range(T)]
        mask_ready = sem("mask_ready")
        passes_ready = sem("passes_ready")
        stored = sem("stored")
        y_stored = sem("y_stored")
        hist_stored = sem("hist_stored")
        cols_ready = sem("cols_ready")
        sel_built = sem("sel_built")
        gathered = sem("gathered")
        slotv_mm = sem("slotv_mm")
        xs_ready = sem("xs_ready")
        slotv_ready = sem("slotv_ready")
        slots_ready = sem("slots_ready")
        silu_done = sem("silu_done")
        h_done = sem("h_done")
        hT_done = sem("hT_done")
        hT_copied = sem("hT_copied")
        yh_done = sem("yh_done")
        yl_done = sem("yl_done")
        yf_done = sem("yf_done")
        combined = sem("combined")
        added = sem("added")
        more_sems = [{n: sem(f"more_{n}{layer}") for n in (
            "landed", "slotm", "cols", "sel", "gathered", "xs", "slotv", "slots", "up", "silu", "h", "hT",
            "hTc", "down", "yf", "yh", "yl", "combined", "added", "shift", "done")} for layer in range(DEPTH)]

        def wait(eng, s, v):
            if not isinstance(v, int) or v > 0:
                eng.wait_ge(s, v)

        def wait_norm(eng, s, q, t):
            eng.wait_ge(s, T * q + NORM_ORDER[q % 2].index(t) + 1)

        def psum_of(layer, *name):
            return ps[:, JOBS[(layer, *name)][0], :]

        def wait_filled(eng, layer, *name):
            eng.wait_ge(filled, JOBS[(layer, *name)][1])

        def wait_drained(eng, layer, *name):
            _, _, drainer, n, _ = JOBS[(layer, *name)]
            eng.wait_ge(drained[drainer], n)

        def rest_of(eng, layer, t):
            r = ROWS[t]
            eng.wait_ge(part0_ready, T * layer + t + 1)
            part0 = xb[:, t, 0, :, :] if t < 2 else xb2[0:r, :, :]
            eng.tensor_tensor(rest[t][0:r, :, :], x[0:r, t, :].rearrange("p (j c) -> p c j", c=C), part0,
                              ALU.subtract).then_inc(rest_ready[t], 1)

        def last_part_of(eng, layer, t):
            r = ROWS[t]
            eng.wait_ge(part1_ready[t], layer + 1)
            part1, part2 = (xb[:, t, 1, :, :], xb[:, t, 2, :, :]) if t < 2 else (xb2m[0:r, :, :], xb2[64:96, :, :])
            eng.tensor_tensor(part2, rest[t][0:r, :, :], part1, ALU.subtract).then_inc(part2_ready[t], 1)

        def conv_parts(layer):
            w = WIDTH[layer]
            return w, SEQ + w - 1, NS + w - 1

        def conv_views(layer, cc, j):
            w, pw, sw = conv_parts(layer)
            per_sample = lambda ap: ap.rearrange("p (b s) -> p b s", b=NB)
            return [(catT[:, cc, 0:SEQ], cb[:, cc, j:j + SEQ]),
                    (per_sample(catT[:, cc, SEQ:TOK]), per_sample(cb[:, cc, pw:pw + NB * sw])[:, :, j:j + NS])]

        def first_tap(eng, layer, cc, out, src):
            if layer == 0:
                return eng.tensor_scalar(out, src, pcol[:, cc, 0:1], pcol[:, cc, 31:32], ALU.mult, ALU.add)
            return eng.tensor_scalar(out, src, pcol[:, cc, 0:1], None, ALU.mult)

        uses = [0] * SLOTS
        landing = {}

        def tile_plan():
            for layer in range(DEPTH):
                g = FIRST_TILE[layer]
                for n in range(g == 0, MIX_TILES[layer]):
                    uses[(g + n) % SLOTS] += 2 if n == MIX_TILES[layer] - 2 else 1
                    landing[g + n] = 16 * uses[(g + n) % SLOTS]
                for n in range(MIX_TILES[layer], MIX_TILES[layer] + 3 * PAIRS):
                    uses[(g + n) % SLOTS] += 1
                    landing[g + n] = 16 * uses[(g + n) % SLOTS]

        tile_plan()

        def tile_at(layer, n):
            return ring[:, (FIRST_TILE[layer] + n) % SLOTS, :]

        def wait_tile(eng, layer, n):
            g = FIRST_TILE[layer] + n
            eng.wait_ge(landed[g % SLOTS], landing[g])

        IN_PARTS = [["g", "a", "q"], ["c", "h", "b", "q"]]
        tiles = []
        for layer in range(DEPTH):
            ins = [(("in", i), (part, 3)) for i, part in enumerate(IN_PARTS[layer])]
            kvs = [(("kv", n), ("kv", n, 1)) for n in range(2)]
            tiles.append((ins + kvs if layer == 0 else kvs + ins)
                         + [(("K", 0), ("KT", 3, 1)), (("K", 1), ("KT", 7, 1)),
                            (("V", 0), ("os",)), (("V", 1), ("os",)),
                            (("out", 0), ("out", 1, 0)), (("out", 1), ("out", 1, 1)),
                            (("sgu", 0), ("sup", 1)), (("sd", 0), ("sdown", 1, 1))])

        def tile_no(layer, what, i=0):
            return [name for name, _ in tiles[layer]].index((what, i))

        def last_job(layer, n):
            return tiles[layer][n][1]

        def wait_tile_used(eng, g):
            if g < 0:
                return
            layer = int(g >= FIRST_TILE[1])
            n = g - FIRST_TILE[layer]
            if n < MIX_TILES[layer]:
                wait_filled(eng, layer, *last_job(layer, n))
            else:
                pair, part = divmod(n - MIX_TILES[layer], 3)
                eng.wait_ge(tile_used, 2 * (PAIRS * layer + pair) + (2 if part == 2 else 1))

        IN_COLS = [[1, 0, 2], [1, 2, 0, 3]]
        w_in = [I["w_in_a"][0].rearrange("(p c) n -> p c n", c=C), I["w_in_b"][0].rearrange("(p c) n -> p c n", c=C)]
        experts = {}
        for layer in range(DEPTH):
            experts[layer] = [I["w_gate"][layer].rearrange("e (p c) f -> e p (c f)", c=C),
                              I["w_up"][layer].rearrange("e (p c) f -> e p (c f)", c=C),
                              I["w_down"][layer].rearrange("e (p c) d -> e p (c d)", c=2)]

        BEFORE_QUERIES, BEFORE_SCORES, BEFORE_SAMPLES = 6, 10, 8
        POOL_TAPS = 24
        pool_conv_end = []
        conv_end = []
        block = ctx.enter_context(nc.Block())

        @block.sync
        def _(sp):
            sp.dma_start(x[:, 0:2, :], I["x_prompt"][0].rearrange("(t p) d -> p t d", p=P)).then_inc(x_loaded, 16)
            sp.dma_start(x[0:ROWS[2], 2, :], I["x_sample"].rearrange("b s d -> (b s) d")).then_inc(x_loaded, 16)

            def load_tile(layer, n):
                g = FIRST_TILE[layer] + n
                dst = ring[:, g % SLOTS, :]
                wait_tile_used(sp, g - SLOTS)
                what, i = tiles[layer][n][0]
                if g == 0:
                    for m in range(4):
                        col = 512 * IN_COLS[0][0] + P * m
                        sp.dma_start(dst.rearrange("p (c n) -> p c n", c=C)[:, :, P * m:P * m + P],
                                     w_in[0][:, :, col:col + P]).then_inc(first_landed[m], 16)
                elif what == "in":
                    m = IN_COLS[layer][i]
                    sp.dma_start(dst.rearrange("p (c n) -> p c n", c=C),
                                 w_in[layer][:, :, 512 * m:512 * m + 512]).then_inc(landed[g % SLOTS], 16)
                elif what == "kv":
                    sp.dma_start(dst.rearrange("p (c n) -> p c n", c=C),
                                 I["w_kv"][layer].rearrange("(p c) n -> p c n", c=C)[:, :, 512 * i:512 * i + 512]
                                 ).then_inc(landed[g % SLOTS], 16)
                elif what in ("K", "V"):
                    cache = I["cache_mem_k"] if what == "K" else I["cache_mem_v"]
                    sp.dma_start(dst.rearrange("p (b n) -> p b n", b=4),
                                 cache[layer, 4 * i:4 * i + 4].rearrange("b (p m) h d -> p b (m h d)", m=2)
                                 ).then_inc(landed[g % SLOTS], 16)
                elif what == "out":
                    sp.dma_start(dst.rearrange("p (c n) -> p c n", c=C),
                                 I["w_out"][layer].rearrange("(c p) n -> p c n", c=C)[:, :, 512 * i:512 * i + 512]
                                 ).then_inc(landed[g % SLOTS], 16)
                elif what == "sgu":
                    for i, w in enumerate(("ws_gate", "ws_up")):
                        sp.dma_start(dst[:, 2048 * i:2048 * i + 2048],
                                     I[w][layer].rearrange("(p c) f -> p (c f)", c=C)).then_inc(landed[g % SLOTS], 16)
                else:
                    sp.dma_start(dst[:, 0:2048], I["ws_down"][layer].rearrange("(p c) d -> p (c d)", c=2)
                                 ).then_inc(landed[g % SLOTS], 16)

            for layer in range(DEPTH):
                more = more_sems[layer]
                for n in range(MIX_TILES[layer]):
                    load_tile(layer, n)
                    if n == (2 if layer == 0 else 1):
                        if layer == 1:
                            sp.wait_ge(gathered, 2 * (PAIRS + 1))
                        sp.dma_start(kv[:, :, :], I["mem_prompt"][0].rearrange("(m p) d -> p m d", p=P)
                                     ).then_inc(mem_loaded[layer], 16)
                g0 = FIRST_TILE[layer] + MIX_TILES[layer]

                def load_pair(k, b, c):
                    g = g0 + 3 * b + c
                    sp.dma_start(ring[:, g % SLOTS, :].rearrange("p (e n) -> p e n", e=2),
                                 experts[layer][c][bass.ds(2 * k, 2)].rearrange("e p n -> p e n")
                                 ).then_inc(landed[g % SLOTS], 16)

                for b in range(2):
                    for c in range(3):
                        wait_tile_used(sp, g0 + 3 * b + c - SLOTS)
                        load_pair(b, b, c)
                with sp.Fori(1, PAIRS // 2) as j:
                    for b in range(2):
                        for c in range(3):
                            sp.wait_ge(tile_used, 2 * PAIRS * layer + 4 * j + 2 * b - 4 + (2 if c == 2 else 1))
                            load_pair(2 * j + b, b, c)
                sp.wait_ge(passes_ready, layer + 1)
                npass = sp.value_load(passes[0:1, layer:layer + 1], min_val=1, max_val=PASSES)
                with sp.If(npass > 1):
                    sp.wait_ge(added, SUMS * PAIRS * (layer + 1))
                    with sp.Fori(1, npass) as p:
                        with sp.Fori(0, PAIRS) as k:
                            sp.wait_ge(more["added"], SUMS * PAIRS * (p - 1) + SUMS * k + 1)
                            for c in range(3):
                                sp.dma_start(ring[:, c, :].rearrange("p (e n) -> p e n", e=2),
                                             experts[layer][c][bass.ds(2 * k, 2)].rearrange("e p n -> p e n")
                                             ).then_inc(more["landed"], 16)
                    sp.wait_ge(more["done"], 1)
            for t in range(2):
                wait_norm(sp, ln_done, 2 * DEPTH - 1, t)
                sp.dma_start(O[0][0, P * t:P * t + P, :], x[:, t, :]).then_inc(y_stored, 16)
            sp.wait_ge(ln_done, T * 2 * DEPTH)
            sp.dma_start(O[1].rearrange("b s d -> (b s) d"), x[0:ROWS[2], 2, :]).then_inc(y_stored, 16)
            sp.wait_ge(y_stored, 48)
            sp.wait_ge(stored, 16 * 4 * DEPTH)
            sp.wait_ge(hist_stored, 16)

        @block.gpsimd
        def _(pool):
            def load_norm(q):
                g, b = (I["ln1_g"], I["ln1_b"]) if q % 2 == 0 else (I["ln2_g"], I["ln2_b"])
                pool.dma_start(lnp[:, 0, :], g[q // 2:q // 2 + 1, :].to_broadcast([P, D])).then_inc(ln_loaded, 16)
                pool.dma_start(lnp[:, 1, :], b[q // 2:q // 2 + 1, :].to_broadcast([P, D])).then_inc(ln_loaded, 16)

            pool.memset(ident[:, :], 0.0).then_inc(pool_seq, 1)
            pool.memset(ones[:, :], 1.0).then_inc(pool_seq, 1)
            pool.memset(valid[:, :], 1.0).then_inc(pool_seq, 1)
            pool.memset(eps[:, :], EPS)
            pool.iota(iota_win[:, :], pattern=[[1, WIN]], base=0, channel_multiplier=0,
                      allow_small_or_imprecise_dtypes=True)
            pool.iota(iota_tok[:, :], pattern=[[1, TOK]], base=1, channel_multiplier=0,
                      allow_small_or_imprecise_dtypes=True)
            pool.iota(tokid[:, :, 0], pattern=[[P, T]], base=0, channel_multiplier=0,
                      allow_small_or_imprecise_dtypes=True)
            pool.iota(tokid[:, :, 1], pattern=[[0, T]], base=1, channel_multiplier=1,
                      allow_small_or_imprecise_dtypes=True)
            pool.iota(thresholds[:, :], pattern=[[WIN, PASSES - 1]], base=WIN, channel_multiplier=0,
                      allow_small_or_imprecise_dtypes=True)
            pool.wait_ge(pool_seq, 3)
            pool.affine_select(out=ident[:, :], in_=ident[:, :], compare_op=ALU.not_equal, fill=1.0, base=0,
                               pattern=[[-1, P]], channel_multiplier=1)
            pool.affine_select(out=tri[:, :], in_=ones[:, :], compare_op=ALU.is_gt, fill=0.0, base=0,
                               pattern=[[1, P]], channel_multiplier=-1)
            pool.affine_select(out=valid[:, 2:3], in_=valid[:, 2:3], compare_op=ALU.is_gt, fill=0.0,
                               base=ROWS[2], pattern=[[0, 1]], channel_multiplier=-1).then_inc(consts_ready, 1)
            load_norm(0)
            wait_drained(pool, 0, "params")
            wait_drained(pool, 0, "a", CC - 1)
            steps_done = 3
            cc = CC - 1
            scaled = [ct[:, cc, 0:SEQ], ct[:, cc, SEQ:TOK].rearrange("p (b s) -> p b s", b=NB)]
            for j in range(POOL_TAPS):
                views = conv_views(0, cc, j)
                for part, (out, src) in enumerate(views):
                    if j == 0:
                        ins = first_tap(pool, 0, cc, out, src)
                    else:
                        if j > 1:
                            pool.wait_ge(pool_seq, steps_done - 1)
                        ins = pool.tensor_scalar(scaled[part], src, pcol[:, cc, j:j + 1], None, ALU.mult)
                    ins.then_inc(pool_seq, 1)
                    steps_done += 1
                for part, (out, src) in enumerate(views):
                    if j > 0:
                        pool.wait_ge(pool_seq, steps_done - 1)
                        pool.tensor_tensor(out, out, scaled[part], ALU.add).then_inc(pool_seq, 1)
                        steps_done += 1
            pool_conv_end.append(steps_done)
            pool.dma_start(O[6][0, :, 0:26, :], I["state_conv_a"][0, :, 4:30, :]).then_inc(hist_stored, 16)

            for layer in range(DEPTH):
                newp, news = (O[4], O[6]) if layer == 0 else (O[5], O[7])
                np_, ns_ = (30, 4) if layer == 0 else (2, 2)
                wait_drained(pool, layer, "newp")
                pool.dma_start(newp[0, 0], y[0:np_, 2, 0:CH]).then_inc(stored, 16)
                wait_drained(pool, layer, "news")
                dst = news[0, :, 26:30, :] if layer == 0 else news[0]
                pool.dma_start(dst, y[0:NB * ns_, 2, CH:2 * CH]).then_inc(stored, 16)
                wait_drained(pool, layer, "kv", 0, 1)
                pool.dma_start(O[2][layer, 0].rearrange("(m p) h d -> p m (h d)", p=P), kv[:, :, 0:CH]
                               ).then_inc(stored, 16)
                wait_drained(pool, layer, "kv", 1, 1)
                pool.dma_start(O[3][layer, 0].rearrange("(m p) h d -> p m (h d)", p=P), kv[:, :, CH:2 * CH]
                               ).then_inc(stored, 16)
                pool.wait_ge(ln_done, T * (2 * layer + 1))
                load_norm(2 * layer + 1)
                rest_of(pool, layer, 0)
                rest_of(pool, layer, 1)
                last_part_of(pool, layer, 0)
                last_part_of(pool, layer, 1)
                if layer + 1 < DEPTH:
                    pool.wait_ge(ln_done, T * (2 * layer + 2))
                    load_norm(2 * layer + 2)

        @block.scalar
        def _(act):
            copy = lambda out, in_: act.activation(out, in_, ACT.Copy)

            def norm_std(q):
                act.activation(spare[:, :], eps[:, :], ACT.Sqrt)
                for t in NORM_ORDER[q % 2]:
                    wait_norm(act, var_ready, q, t)
                    act.activation(rstd[0:ROWS[t], t:t + 1], mv[0:ROWS[t], t, 1:2], ACT.Sqrt,
                                   bias=eps[0:ROWS[t], :]).then_inc(rstd_ready, 1)

            def drain(layer, *name):
                wait_filled(act, layer, *name)
                return psum_of(layer, *name)

            def load_small(layer):
                if layer == 0:
                    act.dma_start(prow[0:31, :], I["conv_a_w"][0]).then_inc(small_loaded[layer], 16)
                    act.dma_start(prow[31:32, :], I["conv_a_b"]).then_inc(small_loaded[layer], 16)
                    act.dma_start(prow[32:33, :], I["norm_a_g"]).then_inc(small_loaded[layer], 16)
                    act.dma_start(prow[33:34, :], I["norm_a_b"]).then_inc(small_loaded[layer], 16)
                    act.dma_start(y[0:120, 2, :].rearrange("r (q n) -> r q n", q=2),
                                   I["state_conv_a"][0].rearrange("(q b) r n -> (b r) q n", q=2)
                                   ).then_inc(small_loaded[layer], 16)
                else:
                    act.dma_start(prow[0:3, :], I["conv_b_w"][0]).then_inc(small_loaded[layer], 16)
                    act.dma_start(y[0:16, 2, 0:CH], I["state_conv_b"][0].rearrange("b r n -> (b r) n")
                                   ).then_inc(small_loaded[layer], 16)
                act.dma_start(wr[:, :, :], I["w_router"][layer].rearrange("(p c) e -> p c e", c=C)
                               ).then_inc(router_loaded[layer], 16)
                act.dma_start(rb[:, :], I["router_bias"][layer:layer + 1, :].to_broadcast([P, E])
                               ).then_inc(router_loaded[layer], 16)

            load_small(0)
            act.wait_ge(consts_ready, 1)
            for layer in range(DEPTH):
                more = more_sems[layer]
                done = drained["act"]

                def drain_memT():
                    for m in range(2):
                        for hf in range(2):
                            b = drain(layer, "memT", m, hf)
                            copy(memT[:, 4 * hf:4 * hf + 4, P * m:P * m + P], b.rearrange("p (c r) -> p c r", c=4)
                                 ).then_inc(done, 1)

                def drain_kv():
                    wait_filled(act, layer, "memT", 1, 1)
                    for n in range(2):
                        for m in range(2):
                            b = drain(layer, "kv", n, m)
                            copy(kv[:, m, 512 * n:512 * n + 512], b).then_inc(done, 1)
                    for hp in range(2):
                        b = drain(layer, "kT", hp)
                        copy(kT[:, 2 * hp:2 * hp + 2, :], b.rearrange("p (h q) -> p h q", h=2)).then_inc(done, 1)

                if layer == 1:
                    drain_memT()
                    norm_std(1)
                    act.wait_ge(ln_done, 6 * layer)
                    load_small(1)
                if layer == 1:
                    drain_kv()
                for t in range(T):
                    b = drain(layer, "xT", t, 0)
                    r = ROWS[t]
                    copy(xT[:, 0:4, START[t]:START[t] + r], b[:, 0:4 * r].rearrange("p (c r) -> p c r", c=4)
                         ).then_inc(done, 1)
                for m in range(4):
                    b = drain(layer, "g" if layer == 0 else "c", m)
                    act.activation(sig[:, m, :], b[:, 0:TOK], ACT.Sigmoid if layer == 0 else ACT.Copy).then_inc(done, 1)
                b = drain(layer, "params")
                n = NPARAM[layer]
                copy(pcol[:, :, 0:n], b[:, 0:CC * n].rearrange("p (c n) -> p c n", c=CC)).then_inc(done, 1)
                if layer == 1:
                    for m in range(4):
                        b = drain(layer, "b", m)
                        copy(ct[:, m, :], b[:, 0:TOK]).then_inc(done, 1)
                for m in range(4):
                    b = drain(layer, "q", m)
                    copy(qT[:, m, :], b[:, 0:TOK]).then_inc(done, 1)
                if layer == 0:
                    drain_memT()
                    drain_kv()
                np_, ns_ = (30, 32) if layer == 0 else (2, 16)
                b = drain(layer, "newp")
                copy(y[0:np_, 2, 0:CH], b[0:np_, :]).then_inc(done, 1)
                b = drain(layer, "news")
                copy(y[0:ns_, 2, CH:2 * CH], b[0:ns_, :]).then_inc(done, 1)

                def drain_keys(samples):
                    for s in samples:
                        for hp in range(2):
                            b = drain(layer, "KT", s, hp)
                            copy(KT[s % 2][:, 2 * hp:2 * hp + 2, :], b.rearrange("p (h q) -> p h q", h=2)
                                 ).then_inc(done, 1)

                drain_keys(range(2))
                for j, (hp, t) in enumerate([(hp, t) for hp in range(2) for t in range(2)]):
                    act.wait_ge(max_ready, 5 * layer + j + 1)
                    b = psum_of(layer, "sc", hp, t)
                    for i in range(2):
                        k = 2 * j + i
                        ins = act.activation(Pm[:, t, 2 * hp + i, :], b[:, MEM * i:MEM * i + MEM], ACT.Exp,
                                             bias=mx[:, k:k + 1], scale=SCALE, accum_out=sums[:, k:k + 1])
                    ins.then_inc(done, 1)
                drain_keys(range(2, NB))
                act.wait_ge(max_ready, 5 * layer + 5)
                act.activation(Ps[:, :], ps[:, BANKS, 0:MEM], ACT.Exp, bias=mx[:, 8:9], scale=SCALE,
                               accum_out=sums[:, 8:9]).then_inc(done, 1)
                for h in range(H):
                    b = drain(layer, "PT", h)
                    copy(PT[:, h, :, :], b.rearrange("p (m q) -> p m q", m=2)).then_inc(done, 1)
                for h in range(H):
                    b = drain(layer, "o", h)
                    copy(catT[:, CC + h, 0:SEQ], b[:, 0:SEQ]).then_inc(done, 1)
                if layer == 0:
                    b = drain(layer, "var")
                    act.activation(sig[:, 1, :], b[:, 0:TOK], ACT.Sqrt, bias=eps[:, :], scale=1.0 / CH
                                   ).then_inc(done, 1)
                b = drain(layer, "PTs")
                act.wait_ge(spread_cleared, layer + 1)
                bv = b[:, 0:2 * P].rearrange("p (g s n) -> p g s n", g=2 * H, s=NB)
                copy(spread[:, :, 0:(32 + NS) * (NB - 1)].rearrange("p g (s z) -> p g s z", z=32 + NS)[:, :, :, 0:NS],
                     bv[:, :, 0:NB - 1, :])
                copy(spread[:, :, (32 + NS) * (NB - 1):MEM], bv[:, :, NB - 1, :]).then_inc(done, 1)
                if layer == 0:
                    for cc in range(CC):
                        act.wait_ge(conv_ready, cc + 1)
                        act.activation(catT[:, cc, :], ct[:, cc, :], ACT.Silu, bias=pcol[:, cc, 33:34],
                                       scale=pcol[:, cc, 32:33]).then_inc(mix_ready, 1)
                b = drain(layer, "os")
                copy(PTs[:, 0, :], b[:, 0:P]).then_inc(done, 1)
                b = drain(layer, "osT")
                copy(catT[:, CC:C, SEQ:TOK], b[:, 0:P].rearrange("p (h q) -> p h q", h=H)).then_inc(done, 1)
                norm_std(2 * layer)
                act.wait_ge(stored, 16 * (4 * layer + 4))
                for group in NORM1_GROUPS:
                    for t in group:
                        for hf in range(1 if t == 1 else 2):
                            b = drain(layer, "x1T", t, hf)
                            r = ROWS[t]
                            copy(xT[:, 4 * hf:4 * hf + 4, START[t]:START[t] + r],
                                 b[:, 0:4 * r].rearrange("p (c r) -> p c r", c=4)).then_inc(done, 1)
                    for t in group:
                        b = drain(layer, "logits", t)
                        act.activation(score[0:ROWS[t], t, :], b[0:ROWS[t], 0:E], ACT.Sigmoid).then_inc(done, 1)
                for t in range(T):
                    part0 = xb[:, t, 0, :, :] if t < 2 else xb2[0:ROWS[t], :, :]
                    copy(part0, x[0:ROWS[t], t, :].rearrange("p (j c) -> p c j", c=C)).then_inc(part0_ready, 1)
                def second_part_of(t):
                    act.wait_ge(rest_ready[t], layer + 1)
                    r = ROWS[t]
                    if t < 2:
                        copy(xb[:, t, 1, :, :], rest[t][:, :, :]).then_inc(part1_ready[t], 1)
                    else:
                        copy(xb2[32:64, :, :], rest[t][0:r, :, :])
                        copy(xb2m[0:r, :, :], rest[t][0:r, :, :]).then_inc(part1_ready[t], 1)

                second_part_of(0)
                for f in range(2):
                    b = drain(layer, "sgate", f)
                    act.activation(sig[:, f, :], b[:, 0:TOK], ACT.Silu).then_inc(done, 1)
                second_part_of(1)
                second_part_of(2)

                def copy_xs(k, b):
                    for hf in range(2):
                        act.wait_ge(gathered, 2 * ((PAIRS + 1) * layer + k) + hf + 1)
                        ins = copy(xs[:, b, 4 * hf:4 * hf + 4, :].rearrange("p c s -> p (c s)"), ps[:, GATHER + hf, :])
                    ins.then_inc(xs_ready, 1)

                def round_y(k):
                    act.wait_ge(tile_used, 2 * PAIRS * layer + 2 * k + 2)
                    copy(yf[:, :], ps[:, DOWN:DOWN + 2, :].rearrange("p b n -> p (b n)")).then_inc(yf_done, 1)
                    act.wait_ge(yf_done, PAIRS * layer + k + 1)
                    copy(yh[:, :], yf[:, :]).then_inc(yh_done, 1)

                def step(k, b):
                    act.wait_ge(tile_used, 2 * PAIRS * layer + 2 * k + 1)
                    act.activation(sg[:, :], ps[:, GU, 0:FF], ACT.Silu).then_inc(silu_done, 1)
                    copy_xs(k + 1, 1 - b)
                    act.wait_ge(hT_done, PAIRS * layer + k + 1)
                    copy(hT[:, :, :], ps[:, SMALL, 0:FF].rearrange("p (f s) -> p f s", f=2)).then_inc(hT_copied, 1)

                copy_xs(0, 0)
                step(0, 0)
                round_y(0)
                step(1, 1)
                with act.Fori(1, PAIRS // 2) as j:
                    for b in range(2):
                        round_y(2 * j + (b - 1))
                        step(2 * j + b, b)
                round_y(PAIRS - 1)

                act.wait_ge(passes_ready, layer + 1)
                npass = act.value_load(passes[0:1, layer:layer + 1], min_val=1, max_val=PASSES)
                with act.If(npass > 1):
                    with act.Fori(1, npass) as p:
                        with act.Fori(0, PAIRS) as k:
                            n = (p - 1) * PAIRS + k
                            act.wait_ge(more["gathered"], n + 1)
                            copy(xs[:, 0, :, :].rearrange("p c s -> p (c s)"),
                                 ps[:, GATHER:GATHER + 2, :].rearrange("p b n -> p (b n)")).then_inc(more["xs"], 1)
                            act.wait_ge(more["up"], n + 1)
                            act.activation(sg[:, :], ps[:, GU, 0:FF], ACT.Silu).then_inc(more["silu"], 1)
                            act.wait_ge(more["hT"], n + 1)
                            copy(hT[:, :, :], ps[:, SMALL, 0:FF].rearrange("p (f s) -> p f s", f=2)
                                 ).then_inc(more["hTc"], 1)
                            act.wait_ge(more["down"], n + 1)
                            copy(yf[:, :], ps[:, DOWN:DOWN + 2, :].rearrange("p b n -> p (b n)")
                                 ).then_inc(more["yf"], 1)
                            act.wait_ge(more["yf"], n + 1)
                            copy(yh[:, :], yf[:, :]).then_inc(more["yh"], 1)
            norm_std(2 * DEPTH - 1)

        @block.vector
        def _(dve):
            links = [0]

            def link(ins):
                links[0] += 1
                ins.then_inc(dve_seq, 1)
                dve.wait_ge(dve_seq, links[0])

            done = drained["dve"]

            def drain(layer, *name):
                wait_filled(dve, layer, *name)
                return psum_of(layer, *name)

            def norm_half(src, t, n):
                r = ROWS[t]
                links[0] += 1
                dve.bn_stats(bn[0:r, t, n, :], src[0:r, t, 512 * n:512 * n + 512]).then_inc(dve_seq, 1)

            def norm_stats(t):
                r = ROWS[t]
                dve.wait_ge(dve_seq, links[0])
                dve.bn_aggr(mv[0:r, t, :], bn[0:r, t, :, :].rearrange("p a b -> p (a b)")).then_inc(var_ready, 1)

            def add_strips(out, src, b):
                r = ROWS[2]
                for n in range(2):
                    ov, sv = (v[0:r, 2, 512 * n:512 * n + 512] for v in (out, src))
                    links[0] += 1
                    dve.scalar_tensor_tensor(ov, sv, ALPHA, b[64 * n:64 * n + r, :], ALU.mult, ALU.add
                                             ).then_inc(dve_seq, 1)
                dve.wait_ge(dve_seq, links[0])
                for n in range(2):
                    ov = out[0:r, 2, 512 * n:512 * n + 512]
                    ins = dve.tensor_tensor(ov, ov, b[64 * n + 32:64 * n + 32 + r, :], ALU.add)
                return ins

            def norm_apply(q, src, t):
                r = ROWS[t]
                wait_norm(dve, rstd_ready, q, t)
                link(dve.reciprocal(rstd[0:r, t:t + 1], rstd[0:r, t:t + 1]))
                dve.wait_ge(ln_loaded, 32 * (q + 1))
                link(dve.scalar_tensor_tensor(x[0:r, t, :], src[0:r, t, :], mv[0:r, t, 0:1], lnp[0:r, 0, :],
                                              ALU.subtract, ALU.mult))
                dve.scalar_tensor_tensor(x[0:r, t, :], x[0:r, t, :], rstd[0:r, t:t + 1], lnp[0:r, 1, :],
                                         ALU.mult, ALU.add).then_inc(ln_done, 1)

            dve.wait_ge(consts_ready, 1)

            for layer in range(DEPTH):
                more = more_sems[layer]
                w, pw, sw = conv_parts(layer)
                for t in range(T):
                    b = drain(layer, "xT", t, 1)
                    r = ROWS[t]
                    dve.tensor_copy(xT[:, 4:8, START[t]:START[t] + r],
                                    b[:, 0:4 * r].rearrange("p (c r) -> p c r", c=4)).then_inc(done, 1)
                dve.memset(cb[:, :, 0:w - 1], 0.0)
                link(dve.memset(qm[:, :, :], 0.0))
                samples = cb[:, :, pw:pw + NB * sw].rearrange("p c (b s) -> p c b s", b=NB)
                for q in range(2 if layer == 0 else 1):
                    b = drain(layer, "hist", q)
                    nb = 4 if layer == 0 else 8
                    for cc in range(CC):
                        n = nb * (w - 1)
                        ins = dve.tensor_copy(samples[:, cc, nb * q:nb * q + nb, 0:w - 1],
                                              b[:, cc * n:cc * n + n].rearrange("p (b r) -> p b r", b=nb))
                    ins.then_inc(done, 1)
                steps = [(cc, j, min(j + 4, w)) for cc in range(CC) for j in range(0, w, 4)
                         if layer == 1 or cc < CC - 1 or j >= POOL_TAPS]

                def conv_taps(cc, j0, j1):
                    for j in range(j0, j1):
                        for out, src in conv_views(layer, cc, j):
                            if j == 0:
                                ins = first_tap(dve, layer, cc, out, src)
                            else:
                                dve.wait_ge(dve_seq, links[0] - 1)
                                ins = dve.scalar_tensor_tensor(out, src, pcol[:, cc, j:j + 1], out, ALU.mult, ALU.add)
                            ins.then_inc(dve_seq, 1)
                            links[0] += 1

                def conv_some(n):
                    for _ in range(min(n, len(steps))):
                        cc, j0, j1 = steps.pop(0)
                        if layer == 0 and (cc, j0) == (CC - 1, POOL_TAPS):
                            dve.wait_ge(pool_seq, pool_conv_end[0])
                        conv_taps(cc, j0, j1)

                wait_drained(dve, layer, "params")
                for m in range(CC):
                    b = drain(layer, "a" if layer == 0 else "h", m)
                    wait_drained(dve, layer, "g" if layer == 0 else "c", m)
                    dve.tensor_tensor(cb[:, m, w - 1:pw], b[:, 0:SEQ], sig[:, m, 0:SEQ], ALU.mult)
                    dve.tensor_tensor(samples[:, m, :, w - 1:sw], b[:, SEQ:TOK].rearrange("p (b s) -> p b s", b=NB),
                                      sig[:, m, SEQ:TOK].rearrange("p (b s) -> p b s", b=NB), ALU.mult
                                      ).then_inc(done, 1)
                    wait_drained(dve, layer, "a" if layer == 0 else "h", m)
                    if layer == 0:
                        conv_some(1)
                nn = min(w - 1, NS)
                dve.tensor_copy(new_cols(nn).rearrange("p c (b s) -> p c b s", b=NB), samples[:, :, :, sw - nn:sw])
                conv_some(BEFORE_QUERIES)
                for h in range(H):
                    wait_drained(dve, layer, "q", h)
                    ins = dve.tensor_copy(qm[:, h, :].rearrange("p (b z) -> p b z", z=32 + NS)[:, :, 0:NS],
                                          qT[:, h, SEQ:TOK].rearrange("p (b s) -> p b s", b=NB))
                ins.then_inc(qmask_ready, 1)
                dve.wait_ge(qmask_ready, layer + 1)

                conv_some(BEFORE_SCORES)
                order = [(hp, t) for hp in range(2) for t in range(2)]

                def soft_max(j):
                    b = drain(layer, "sc", *order[j])
                    link(dve.tensor_reduce(mx[:, 2 * j:2 * j + 2], b.rearrange("p (h q) -> p h q", h=2), AX.X, ALU.max))
                    dve.tensor_scalar(mx[:, 2 * j:2 * j + 2], mx[:, 2 * j:2 * j + 2], -SCALE, None, ALU.mult
                                      ).then_inc(max_ready, 1)

                def soft_norm(j):
                    hp, t = order[j]
                    wait_drained(dve, layer, "sc", hp, t)
                    link(dve.reciprocal(sums[:, 2 * j:2 * j + 2], sums[:, 2 * j:2 * j + 2]))
                    for i in range(2):
                        pr = Pm[:, t, 2 * hp + i, :]
                        ins = dve.tensor_scalar(pr, pr, sums[:, 2 * j + i:2 * j + i + 1], None, ALU.mult)
                    ins.then_inc(prob_ready, 1)

                def soft_norm_samples():
                    wait_drained(dve, layer, "scs")
                    link(dve.reciprocal(sums[:, 8:9], sums[:, 8:9]))
                    dve.tensor_scalar(Ps[:, :], Ps[:, :], sums[:, 8:9], None, ALU.mult).then_inc(prob_ready, 1)

                soft_max(0)
                for j in range(4):
                    if j + 1 < 4:
                        soft_max(j + 1)
                    soft_norm(j)
                conv_some(BEFORE_SAMPLES)
                drain(layer, "scs")
                link(dve.tensor_reduce(mx[:, 8:9], ps[:, BANKS, 0:MEM], AX.X, ALU.max))
                dve.tensor_scalar(mx[:, 8:9], mx[:, 8:9], -SCALE, None, ALU.mult).then_inc(max_ready, 1)
                conv_some(2)
                soft_norm_samples()
                conv_some(len(steps))
                if layer == 0:
                    conv_end.append(links[0])

                def clear_spread():
                    wait_filled(dve, layer, "newp")
                    dve.wait_ge(dve_seq, links[0])
                    dve.memset(spread, 0.0).then_inc(spread_cleared, 1)

                if layer == 0:
                    b = drain(layer, "mean")
                    for cc in range(CC):
                        ins = dve.scalar_tensor_tensor(ct[:, cc, :], b[:, 0:TOK], -1.0 / CH, catT[:, cc, :],
                                                       ALU.mult, ALU.add)
                    ins.then_inc(done, 1)
                    wait_drained(dve, layer, "mean")
                    for cc in range(CC):
                        ins = dve.tensor_tensor(catT[:, cc, :], ct[:, cc, :], ct[:, cc, :], ALU.mult)
                    ins.then_inc(centred, 1)
                    clear_spread()
                    wait_drained(dve, layer, "var")
                    link(dve.reciprocal(sig[:, 0, :], sig[:, 1, :]))
                    for cc in range(CC):
                        dve.tensor_tensor(ct[:, cc, :], ct[:, cc, :], sig[:, 0, :], ALU.mult).then_inc(conv_ready, 1)
                else:
                    clear_spread()
                    wait_drained(dve, layer, "b", 3)
                    for cc in range(CC):
                        dve.tensor_tensor(catT[:, cc, :], catT[:, cc, :], ct[:, cc, :], ALU.mult).then_inc(mix_ready, 1)
                add_strips(x, x, drain(layer, "out", 2)).then_inc(done, 1)
                wait_drained(dve, layer, "out", 2)
                norm_half(x, 2, 0)
                norm_half(x, 2, 1)
                norm_stats(2)
                for t, before in ((0, 2), (1, 0)):
                    for n in range(2):
                        b = drain(layer, "out", t, n)
                        xv = x[:, t, 512 * n:512 * n + 512]
                        dve.scalar_tensor_tensor(xv, xv, ALPHA, b, ALU.mult, ALU.add).then_inc(done, 1)
                        wait_drained(dve, layer, "out", t, n)
                        norm_half(x, t, n)
                        if n == 0:
                            norm_apply(2 * layer, x, before)
                    norm_stats(t)
                norm_apply(2 * layer, x, 1)
                b = drain(layer, "x1T", 1, 1)
                dve.tensor_copy(xT[:, 4:8, START[1]:START[2]], b.rearrange("p (c r) -> p c r", c=4)).then_inc(done, 1)

                if layer == 0:
                    dve.wait_ge(stored, 16 * 4)
                else:
                    dve.wait_ge(stored, 16 * 8)
                dve.memset(ranks[:, :, :], -1.0)
                dve.memset(gparts[:, PAIRS, :], 0.0)
                for b in range(2):
                    dve.tensor_copy(cols[:, b, :, 6:8], tokid[:, :, :])
                dve.memset(score[32:64, 2, :], 0.0)
                dve.memset(score[64:128, 2, :], 0.0)
                link(dve.memset(grp[:, :, 8:12], -BIG))
                wait_drained(dve, layer, "logits", NORM_ORDER[0][-1])
                dve.wait_ge(router_loaded[layer], 32)
                rbb = rb[:, :].unsqueeze(1).to_broadcast([P, T, E])
                link(dve.tensor_tensor(cand[:, :, :], score[:, :, :], rbb, ALU.add))
                for t in range(T):
                    for g in range(GROUPS):
                        ins = dve.max(top[:, t, g, :], cand[:, t, 8 * g:8 * g + 8])
                link(ins)
                link(dve.tensor_tensor(grp[:, :, 0:8], top[:, :, 0:8, 0], top[:, :, 0:8, 1], ALU.add))
                for t in range(T):
                    ins = dve.max(top[:, t, 8, :], grp[:, t, 0:8])
                link(ins)
                link(dve.memset(top[:, :, 8, TOP_GROUPS:8], -BIG))
                for t in range(T):
                    ins = dve.match_replace(out=grpr[:, t, :], in_to_replace=top[:, t, 8, :], in_values=grp[:, t, :],
                                            imm_value=BIG)
                link(ins)
                link(dve.tensor_scalar(grpr[:, :, 0:8], grpr[:, :, 0:8], BIG * 0.5, None, ALU.is_ge))
                link(dve.tensor_scalar(grp[:, :, 0:8], grpr[:, :, 0:8], BIG, -BIG, ALU.mult, ALU.add))
                c4 = cand[:, :, :].rearrange("p t (g e) -> p t g e", g=GROUPS)
                link(dve.tensor_tensor(c4, c4, grpr[:, :, 0:8].unsqueeze(3).to_broadcast([P, T, GROUPS, 8]), ALU.mult))
                link(dve.tensor_tensor(c4, c4, grp[:, :, 0:8].unsqueeze(3).to_broadcast([P, T, GROUPS, 8]), ALU.add))
                for t in range(T):
                    ins = dve.max(top[:, t, 0, :], cand[:, t, :])
                link(ins)
                for t in range(T):
                    ins = dve.match_replace(out=mask[:, t, :], in_to_replace=top[:, t, 0, :], in_values=cand[:, t, :],
                                            imm_value=BIG)
                link(ins)
                for t in range(T):
                    ins = dve.tensor_scalar(mask[:, t, :], mask[:, t, :], BIG * 0.5, valid[:, t:t + 1],
                                            ALU.is_ge, ALU.mult)
                ins.then_inc(mask_ready, 1)
                dve.wait_ge(mask_ready, layer + 1)
                for t in range(T):
                    ins = dve.tensor_tensor(gates[:, t, :], score[:, t, :], mask[:, t, :], ALU.mult)
                link(ins)
                link(dve.tensor_reduce(gsum[:, :], gates[:, :, :], AX.X, ALU.add))
                link(dve.reciprocal(gsum[:, :], gsum[:, :]))
                for t in range(T):
                    r = ROWS[t]
                    ins = dve.tensor_scalar(gates[0:r, t, :], gates[0:r, t, :], gsum[0:r, t:t + 1], ROUTED,
                                            ALU.mult, ALU.mult)
                link(ins)
                gv = gates[:, :, :].rearrange("p t (k h) -> p t k h", h=2)
                gp = gparts[:, 0:PAIRS, :].rearrange("p k (t h i) -> p t k h i", t=T, h=2)
                for i in range(3):
                    link(dve.tensor_copy(gp[:, :, :, :, i], gv))
                    if i < 2:
                        link(dve.tensor_tensor(gv, gv, gp[:, :, :, :, i], ALU.subtract))
                for f in range(2):
                    b = drain(layer, "sup", f)
                    wait_drained(dve, layer, "sgate", f)
                    dve.tensor_tensor(qT[:, f, :], b[:, 0:TOK], sig[:, f, :], ALU.mult).then_inc(done, 1)
                rest_of(dve, layer, 2)
                add_strips(y, x, drain(layer, "sdown", 2)).then_inc(done, 1)
                for t in range(2):
                    for n in range(2):
                        b = drain(layer, "sdown", t, n)
                        dve.scalar_tensor_tensor(y[:, t, 512 * n:512 * n + 512], x[:, t, 512 * n:512 * n + 512],
                                                 ALPHA, b, ALU.mult, ALU.add).then_inc(done, 1)
                    if t == 0:
                        last_part_of(dve, layer, 2)
                for t in range(T):
                    r = ROWS[t]
                    b = drain(layer, "rank", t)
                    dve.scalar_tensor_tensor(cand[0:r, t, :], b[0:r, 0:E], 1.0, mask[0:r, t, :], ALU.add, ALU.mult
                                             ).then_inc(done, 1)
                wait_drained(dve, layer, "rank", T - 1)
                for t in range(T):
                    r = ROWS[t]
                    ins = dve.tensor_scalar(ranks[0:r, 0:PAIRS, 2 * t:2 * t + 2],
                                            cand[0:r, t, :].rearrange("p (k h) -> p k h", h=2), -1.0, None, ALU.add)
                link(ins)
                b = drain(layer, "count")
                dve.tensor_reduce(passes_f[:, 0:1], b[0:1, 0:E], AX.X, ALU.max).then_inc(done, 1)
                for i in (1, 2):
                    ins = dve.tensor_copy(ranks[32 * i:32 * i + 32, :, 4:6], ranks[0:32, :, 4:6])
                link(ins)

                s0 = (PAIRS + 1) * layer
                def build_sel(k, b, iota, ready, built, n, shifted=None):
                    dve.tensor_copy(rankc[:, b, :, :], ranks[:, :, :].rearrange("p k f -> p (k f)")[
                        :, bass.ds(2 * T * k, 2 * T)].rearrange("p (t f) -> p t f", t=T)).then_inc(ready, 1)
                    dve.tensor_copy(cols[:, b, :, 0:6], gparts[:, :, :].rearrange("p k f -> p (k f)")[
                        :, bass.ds(6 * T * k, 6 * T)].rearrange("p (t f) -> p t f", t=T))
                    dve.wait_ge(ready, n)
                    if shifted is not None:
                        dve.wait_ge(more["shift"], shifted)
                    dve.tensor_tensor(selb[:, b, :, :].rearrange("p t (h s) -> p t h s", h=2),
                                      iota[:, :].unsqueeze(1).unsqueeze(1).to_broadcast([P, T, 2, WIN]),
                                      rankc[:, b, :, :].unsqueeze(3).to_broadcast([P, T, 2, WIN]),
                                      ALU.is_equal).then_inc(built, 1)

                def take_slotv(b):
                    for e in range(2):
                        dve.tensor_reduce(slotv[WIN * e:WIN * e + WIN, b, 0:1],
                                          ps[WIN * e:WIN * e + WIN, SMALL, FF + 3 * e:FF + 3 * e + 3], AX.X, ALU.add)
                    return dve.tensor_reduce(slotv[:, b, 1:2], ps[:, SMALL, FF + 6:FF + 8], AX.X, ALU.add)

                def build_back(b, built):
                    dve.tensor_scalar(back[:, b, :], iota_tok[:, :], slotv[:, b, 1:2], None, ALU.is_equal
                                      ).then_inc(built, 1)

                def swiglu(b):
                    return dve.scalar_tensor_tensor(hs[:, :], ps[:, GU, FF:2 * FF], slotv[:, b, 0:1], sg[:, :],
                                                    ALU.mult, ALU.mult)

                def low_y():
                    return dve.tensor_tensor(yl[:, :], yf[:, :],
                                             yh[:, :].bitcast(F32), ALU.subtract)

                def add_back(m, b):
                    bank = COMBINE + (m + b) % 2
                    if m < 4:
                        yv = y[:, m // 2, 512 * (m % 2):512 * (m % 2) + 512]
                        return dve.tensor_tensor(yv, yv, ps[:, bank, :], ALU.add)
                    for g in range(4):
                        yv = y[0:32, 2, 256 * g:256 * g + 256]
                        ins = dve.tensor_tensor(yv, yv, ps[32 * g:32 * g + 32, bank, 0:256], ALU.add)
                    return ins

                def add_some(k, b, m0, m1):
                    for m in range(m0, m1):
                        dve.wait_ge(combined, SUMS * PAIRS * layer + SUMS * k + m + 1)
                        wait(dve, added, SUMS * PAIRS * layer + SUMS * k + m + 1 - SUMS)
                        add_back(m, b).then_inc(added, 1)

                def slots_of(k, b):
                    dve.wait_ge(slotv_ready, s0 + k + 1)
                    build_back(b, slots_ready)

                def select(k, b):
                    build_sel(k, b, iota_win, cols_ready, sel_built, s0 + k + 1)

                def step(k, b, first):
                    select(k + 1, 1 - b)
                    if not first:
                        dve.wait_ge(yh_done, PAIRS * layer + k)
                        low_y().then_inc(yl_done, 1)
                        add_some(k - 1, 1 - b, 0, 2)
                    dve.wait_ge(silu_done, PAIRS * layer + k + 1)
                    dve.wait_ge(slots_ready, s0 + k + 1)
                    swiglu(b).then_inc(h_done, 1)
                    if not first:
                        add_some(k - 1, 1 - b, 2, 3)
                    dve.wait_ge(slotv_mm, s0 + k + 2)
                    take_slotv(1 - b).then_inc(slotv_ready, 1)
                    if not first:
                        add_some(k - 1, 1 - b, 3, SUMS)
                    slots_of(k + 1, 1 - b)

                select(0, 0)
                wait_drained(dve, layer, "count")
                link(dve.tensor_scalar(passes_f[:, 1:PASSES], thresholds[:, :], passes_f[:, 0:1], None, ALU.is_lt))
                link(dve.tensor_reduce(passes_f[:, 6:7], passes_f[:, 1:PASSES], AX.X, ALU.add))
                dve.tensor_scalar(passes[:, layer:layer + 1], passes_f[:, 6:7], 1.0, None, ALU.add
                                  ).then_inc(passes_ready, 1)
                dve.wait_ge(passes_ready, layer + 1)
                dve.wait_ge(slotv_mm, s0 + 1)
                take_slotv(0).then_inc(slotv_ready, 1)
                slots_of(0, 0)
                step(0, 0, True)
                step(1, 1, False)
                with dve.Fori(1, PAIRS // 2) as j:
                    for b in range(2):
                        step(2 * j + b, b, False)
                dve.wait_ge(yh_done, PAIRS * (layer + 1))
                low_y().then_inc(yl_done, 1)
                add_some(PAIRS - 1, 1, 0, SUMS)

                npass = dve.value_load(passes[0:1, layer:layer + 1], min_val=1, max_val=PASSES)
                with dve.If(npass > 1):
                    dve.wait_ge(added, SUMS * PAIRS * (layer + 1))
                    dve.tensor_copy(window[:, 0:WIN // 2], iota_win[:, 0:WIN // 2]).then_inc(more["added"], 1)
                    dve.tensor_copy(window[:, WIN // 2:], iota_win[:, WIN // 2:]).then_inc(more["shift"], 1)
                    with dve.Fori(1, npass) as p:
                        dve.wait_ge(more["shift"], p)
                        dve.tensor_scalar(window[:, :], window[:, :], float(WIN), None,
                                          ALU.add).then_inc(more["shift"], 1)
                        with dve.Fori(0, PAIRS) as k:
                            n = (p - 1) * PAIRS + k
                            build_sel(k, 0, window, more["cols"], more["sel"], n + 1, p + 1)
                            dve.wait_ge(more["slotm"], n + 1)
                            take_slotv(0).then_inc(more["slotv"], 1)
                            dve.wait_ge(more["slotv"], n + 1)
                            build_back(0, more["slots"])
                            dve.wait_ge(more["silu"], n + 1)
                            dve.wait_ge(more["slots"], n + 1)
                            swiglu(0).then_inc(more["h"], 1)
                            dve.wait_ge(more["yh"], n + 1)
                            low_y().then_inc(more["yl"], 1)
                            for m in range(SUMS):
                                dve.wait_ge(more["combined"], SUMS * n + m + 1)
                                add_back(m, 0).then_inc(more["added"], 1)
                            dve.wait_ge(more["added"], SUMS * (n + 1) + 1)
                    dve.tensor_copy(window[:, :], iota_win[:, :]).then_inc(more["done"], 1)
                dve.wait_ge(added, SUMS * PAIRS * (layer + 1))
                for t in range(T):
                    norm_half(y, t, 0)
                    norm_half(y, t, 1)
                    norm_stats(t)
                    if t > 0:
                        norm_apply(2 * layer + 1, y, t - 1)
                norm_apply(2 * layer + 1, y, T - 1)

        @block.tensor
        def _(pe):
            def start(layer, *name):
                bank, _, _, _, before = JOBS[(layer, *name)]
                if before is not None:
                    wait_drained(pe, *before)
                return ps[:, bank, :]

            def turn(out, in_, r, c):
                return pe.transpose(out, in_, ident[0:r, 0:r])

            pe.wait_ge(consts_ready, 1)
            pe.wait_ge(x_loaded, 32)
            for layer in range(DEPTH):
                more = more_sems[layer]
                w = WIDTH[layer]
                pw, sw = SEQ + w - 1, NS + w - 1

                def transpose_x(name, q, t):
                    if q >= 0:
                        wait_norm(pe, ln_done, q, t)
                    r = ROWS[t]
                    xv = x[0:r, t, :].rearrange("p (j c) -> p c j", c=C)
                    for hf in range(2):
                        b = start(layer, name, t, hf)
                        for c in range(4):
                            ins = turn(b[:, r * c:r * c + r], xv[:, 4 * hf + c, :], r, P)
                        ins.then_inc(filled, 1)

                def strips(b, lhs, w, chunks):
                    for c in range(0, chunks, 2):
                        for n in range(2):
                            for odd in range(2):
                                g = 32 * (2 * n + odd)
                                ins = pe.matmul(b[g:g + 32, :], lhs[:, c + odd, START[2]:TOK], w[n][:, c + odd, :],
                                                start=c == 0, stop=c == chunks - 2)
                    return ins

                def project_memory():
                    pe.wait_ge(mem_loaded[layer], 16)
                    for m in range(2):
                        mv_ = kv[:, m, :].rearrange("p (j c) -> p c j", c=C)
                        for hf in range(2):
                            b = start(layer, "memT", m, hf)
                            for c in range(4):
                                ins = turn(b[:, P * c:P * c + P], mv_[:, 4 * hf + c, :], P, P)
                            ins.then_inc(filled, 1)
                    wait_drained(pe, layer, "memT", 1, 1)
                    if layer > 0:
                        pe.wait_ge(added, SUMS * PAIRS * layer)
                    for n in range(2):
                        tn = tile_no(layer, "kv", n)
                        wait_tile(pe, layer, tn)
                        wt = tile_at(layer, tn).rearrange("p (c n) -> p c n", c=C)
                        for m in range(2):
                            b = start(layer, "kv", n, m)
                            for c in range(C):
                                ins = pe.matmul(b, memT[:, c, P * m:P * m + P], wt[:, c, :],
                                                start=c == 0, stop=c == C - 1)
                            ins.then_inc(filled, 1)
                    wait_drained(pe, layer, "kv", 0, 1)
                    for hp in range(2):
                        b = start(layer, "kT", hp)
                        for i in range(2):
                            for m in range(2):
                                h = 2 * hp + i
                                ins = turn(b[:, MEM * i + P * m:MEM * i + P * m + P], kv[:, m, HD * h:HD * h + HD], P, P)
                        ins.then_inc(filled, 1)

                def turn_small():
                    b = start(layer, "params")
                    pe.wait_ge(small_loaded[layer], 16 * (5 if layer == 0 else 2))
                    n = NPARAM[layer]
                    for cc in range(CC):
                        ins = turn(b[:, n * cc:n * cc + n], prow[0:n, P * cc:P * cc + P], n, P)
                    ins.then_inc(filled, 1)
                    for q in range(2 if layer == 0 else 1):
                        b = start(layer, "hist", q)
                        n = (4 if layer == 0 else 8) * (w - 1)
                        for cc in range(CC):
                            ins = turn(b[:, n * cc:n * cc + n], y[0:n, 2, CH * q + P * cc:CH * q + P * cc + P], n, P)
                        ins.then_inc(filled, 1)

                if layer == 1:
                    pe.wait_ge(xs_ready, (PAIRS + 1) * layer)
                    project_memory()
                for t in range(T):
                    transpose_x("xT", 2 * layer - 1, t)
                wait_drained(pe, layer, "xT", T - 1, 0)
                wait_drained(pe, layer, "xT", T - 1, 1)
                for n, part in enumerate(IN_PARTS[layer]):
                    in_blocks = layer == 0 and n == 0
                    if not in_blocks:
                        wait_tile(pe, layer, tile_no(layer, "in", n))
                    wt = tile_at(layer, tile_no(layer, "in", n)).rearrange("p (c n) -> p c n", c=C)
                    for m in range(4):
                        if in_blocks:
                            pe.wait_ge(first_landed[m], 16)
                        b = start(layer, part, m)
                        for c in range(C):
                            ins = pe.matmul(b[:, 0:TOK], wt[:, c, P * m:P * m + P], xT[:, c, :],
                                            start=c == 0, stop=c == C - 1)
                        ins.then_inc(filled, 1)
                    if n == 0:
                        turn_small()
                if layer == 0:
                    project_memory()
                wait_drained(pe, layer, "a" if layer == 0 else "h", 3)
                b = start(layer, "newp")
                n = w - 1
                for cc in range(CC):
                    ins = turn(b[0:n, P * cc:P * cc + P], cb[:, cc, pw - n:pw], P, n)
                ins.then_inc(filled, 1)
                b = start(layer, "news")
                n = min(w - 1, NS)
                pe.wait_ge(qmask_ready, layer + 1)
                for cc in range(CC):
                    ins = turn(b[0:NB * n, P * cc:P * cc + P], new_cols(n)[:, cc, :], P, NB * n)
                ins.then_inc(filled, 1)
                def turn_keys(s):
                    tn = tile_no(layer, "K", s // 4)
                    if s % 4 == 0:
                        wait_tile(pe, layer, tn)
                    kt = tile_at(layer, tn).rearrange("p (b m n) -> p b m n", b=4, m=2)
                    for hp in range(2):
                        b = start(layer, "KT", s, hp)
                        for i in range(2):
                            for m in range(2):
                                h = 2 * hp + i
                                ins = turn(b[:, MEM * i + P * m:MEM * i + P * m + P],
                                           kt[:, s % 4, m, HD * h:HD * h + HD], P, P)
                        ins.then_inc(filled, 1)

                turn_keys(0)
                turn_keys(1)
                wait_drained(pe, layer, "kT", 1)
                wait_drained(pe, layer, "q", 3)
                for hp in range(2):
                    for t in range(2):
                        b = start(layer, "sc", hp, t)
                        for i in range(2):
                            h = 2 * hp + i
                            ins = pe.matmul(b[:, MEM * i:MEM * i + MEM], qT[:, h, P * t:P * t + P], kT[:, h, :],
                                            start=True, stop=True)
                        ins.then_inc(filled, 1)
                for s in range(NB):
                    wait_drained(pe, layer, "KT", s, 1)
                    for h in range(H):
                        ins = pe.matmul(ps[32 * h:32 * h + 32, BANKS, 0:MEM], qm[:, h, 32 * s:32 * s + 32],
                                        KT[s % 2][:, h, :], start=s == 0, stop=s == NB - 1)
                    if s + 2 < NB:
                        turn_keys(s + 2)
                ins.then_inc(filled, 1)
                for h in range(H):
                    pe.wait_ge(prob_ready, 5 * layer + 2 * (h // 2) + 2)
                    b = start(layer, "PT", h)
                    for m in range(2):
                        for t in range(2):
                            ins = turn(b[:, MEM * m + P * t:MEM * m + P * t + P], Pm[:, t, h, P * m:P * m + P], P, P)
                    ins.then_inc(filled, 1)
                if layer == 0:
                    pe.wait_ge(dve_seq, conv_end[0])
                    b = start(layer, "mean")
                    for cc in range(CC):
                        ins = pe.matmul(b[:, 0:TOK], ones[:, :], catT[:, cc, :], start=cc == 0, stop=cc == CC - 1)
                    ins.then_inc(filled, 1)
                wait_drained(pe, layer, "kv", 1, 1)
                for h in range(H):
                    wait_drained(pe, layer, "PT", h)
                    b = start(layer, "o", h)
                    for m in range(2):
                        ins = pe.matmul(b[:, 0:SEQ], kv[:, m, CH + HD * h:CH + HD * h + HD], PT[:, h, m, :],
                                        start=m == 0, stop=m == 1)
                    ins.then_inc(filled, 1)
                if layer == 0:
                    pe.wait_ge(centred, 1)
                    b = start(layer, "var")
                    for cc in range(CC):
                        ins = pe.matmul(b[:, 0:TOK], ones[:, :], catT[:, cc, :], start=cc == 0, stop=cc == CC - 1)
                    ins.then_inc(filled, 1)
                pe.wait_ge(prob_ready, 5 * layer + 5)
                b = start(layer, "PTs")
                for m in range(2):
                    ins = turn(b[:, P * m:P * m + P], Ps[:, P * m:P * m + P], P, P)
                ins.then_inc(filled, 1)
                wait_drained(pe, layer, "PTs")
                b = start(layer, "os")
                for s in range(NB):
                    tn = tile_no(layer, "V", s // 4)
                    if s % 4 == 0:
                        wait_tile(pe, layer, tn)
                    vt = tile_at(layer, tn).rearrange("p (b m n) -> p b m n", b=4, m=2)
                    for m in range(2):
                        for h in range(H):
                            ins = pe.matmul(b[32 * h:32 * h + 32, 0:P], spread[:, H * m + h, 32 * s:32 * s + 32],
                                            vt[:, s % 4, m, HD * h:HD * h + HD],
                                            start=s == 0 and m == 0, stop=s == NB - 1 and m == 1)
                ins.then_inc(filled, 1)
                wait_drained(pe, layer, "os")
                b = start(layer, "osT")
                turn(b[:, 0:P], PTs[:, 0, :], P, P).then_inc(filled, 1)
                wait_drained(pe, layer, "osT")
                pe.wait_ge(mix_ready, 4 * layer + 4)
                wo = []
                for n in range(2):
                    tn = tile_no(layer, "out", n)
                    wait_tile(pe, layer, tn)
                    wo.append(tile_at(layer, tn).rearrange("p (c n) -> p c n", c=C))
                strips(start(layer, "out", 2), catT, wo, C).then_inc(filled, 1)
                for t in range(2):
                    for n in range(2):
                        b = start(layer, "out", t, n)
                        for c in range(C):
                            ins = pe.matmul(b, catT[:, c, START[t]:START[t] + P], wo[n][:, c, :],
                                            start=c == 0, stop=c == C - 1)
                        ins.then_inc(filled, 1)

                def shared_mm(part, f, q):
                    wt = tile_at(layer, tile_no(layer, "sgu"))[:, 2048 * (part == "sup"):][:, 0:2048].rearrange(
                        "p (c j f) -> p c f j", c=C, f=2)
                    for c in range(C):
                        ins = pe.matmul(psum_of(layer, part, f)[:, q], wt[:, c, f, :], xT[:, c, q],
                                        start=c == 0, stop=c == C - 1)
                    return ins

                for group in NORM1_GROUPS:
                    for t in group:
                        transpose_x("x1T", 2 * layer, t)
                    pe.wait_ge(router_loaded[layer], 32)
                    for t in group:
                        wait_drained(pe, layer, "x1T", t, 0)
                        wait_drained(pe, layer, "x1T", t, 1)
                        r = ROWS[t]
                        b = start(layer, "logits", t)
                        for c in range(C):
                            ins = pe.matmul(b[0:r, 0:E], xT[:, c, START[t]:START[t] + r], wr[:, c, :],
                                            start=c == 0, stop=c == C - 1)
                        ins.then_inc(filled, 1)
                    if group == NORM1_GROUPS[0]:
                        wait_tile(pe, layer, tile_no(layer, "sgu"))
                        for f in range(2):
                            start(layer, "sgate", f)
                            shared_mm("sgate", f, slice(0, P))
                for f in range(2):
                    shared_mm("sgate", f, slice(P, TOK)).then_inc(filled, 1)
                for f in range(2):
                    start(layer, "sup", f)
                    shared_mm("sup", f, slice(0, TOK)).then_inc(filled, 1)
                tn = tile_no(layer, "sd")
                wait_tile(pe, layer, tn)
                wt = tile_at(layer, tn)[:, 0:2048].rearrange("p (f n) -> p f n", f=2)
                wait_drained(pe, layer, "sup", 1)
                strips(start(layer, "sdown", 2), qT, [wt[:, :, 512 * n:512 * n + 512] for n in range(2)], 2
                       ).then_inc(filled, 1)
                for t in range(2):
                    for n in range(2):
                        b = start(layer, "sdown", t, n)
                        for f in range(2):
                            ins = pe.matmul(b, qT[:, f, START[t]:START[t] + P], wt[:, f, 512 * n:512 * n + 512],
                                            start=f == 0, stop=f == 1)
                        ins.then_inc(filled, 1)
                pe.wait_ge(mask_ready, layer + 1)
                for t in range(T):
                    r = ROWS[t]
                    b = start(layer, "rank", t)
                    for u in range(t):
                        pe.matmul(b[0:r, 0:E], ones[:, 0:r], mask[:, u, :], start=u == 0, stop=False)
                    pe.matmul(b[0:r, 0:E], tri[0:r, 0:r], mask[0:r, t, :], start=t == 0, stop=True).then_inc(filled, 1)
                b = start(layer, "count")
                for t in range(T):
                    ins = pe.matmul(b[:, 0:E], ones[:, :], mask[:, t, :], start=t == 0, stop=t == T - 1)
                ins.then_inc(filled, 1)

                s0 = (PAIRS + 1) * layer
                g0 = FIRST_TILE[layer] + MIX_TILES[layer]

                def slot_mm(b):
                    for t in range(T):
                        r = ROWS[t]
                        ins = pe.matmul(ps[:, SMALL, FF:FF + 8], selb[0:r, b, t, :], cols[0:r, b, t, :],
                                        start=t == 0, stop=t == T - 1)
                    return ins

                def gather_mm(b, hf):
                    for c in range(4 * hf, 4 * hf + 4):
                        out = ps[:, GATHER + c // 4, P * (c % 4):P * (c % 4) + P]
                        for t in range(2):
                            for part in range(3):
                                pe.matmul(out, xb[:, t, part, c, :], selb[:, b, t, :],
                                          start=t == 0 and part == 0, stop=False)
                        ins = pe.matmul(out, xb2[0:96, c, :], selb[0:96, b, 2, :], start=False, stop=True)
                    return ins

                def hidden_mm(slot, b, c0, c1):
                    wt = ring[:, slot:slot + 2, :].rearrange("p u (e c f) -> p e c u f", e=2, c=C)
                    for c in range(c0, c1):
                        for e in range(2):
                            ins = pe.matmul(ps[WIN * e:WIN * e + WIN, GU, :], xs[:, b, c, WIN * e:WIN * e + WIN],
                                            wt[:, e, c, :, :], start=c == 0, stop=c == C - 1)
                    return ins

                def turn_hidden():
                    hv = hs[:, :].rearrange("p (j f) -> p f j", f=2)
                    for f in range(2):
                        ins = turn(ps[:, SMALL, P * f:P * f + P], hv[:, f, :], P, P)
                    return ins

                def down_mm(slot):
                    wt = ring[:, slot, :].rearrange("p (e f n) -> p e f n", e=2, f=2)
                    for n in range(2):
                        for f in range(2):
                            for e in range(2):
                                ins = pe.matmul(ps[WIN * e:WIN * e + WIN, DOWN + n, :], hT[:, f, WIN * e:WIN * e + WIN],
                                                wt[:, e, f, 512 * n:512 * n + 512], start=f == 0, stop=f == 1)
                    return ins

                def combine_mm(m, b, parity):
                    bank = COMBINE + (m + parity) % 2
                    if m < 4:
                        t, n = m // 2, m % 2
                        for half in (yh, yl):
                            ins = pe.matmul(ps[:, bank, :], back[:, b, START[t]:START[t] + P],
                                            half[:, 512 * n:512 * n + 512], start=half is yh, stop=half is yl)
                        return ins
                    for g in range(4):
                        ins = pe.matmul(ps[32 * g:32 * g + 32, bank, 0:256], back[:, b, START[2]:TOK].bitcast(F32),
                                        yf[:, 256 * g:256 * g + 256], start=True, stop=True)
                    return ins

                def gather(k, b):
                    pe.wait_ge(sel_built, s0 + k + 1)
                    wait(pe, hT_copied, PAIRS * layer + k - 1)
                    slot_mm(b).then_inc(slotv_mm, 1)
                    wait(pe, xs_ready, s0 + k)
                    for hf in range(2):
                        gather_mm(b, hf).then_inc(gathered, 1)

                def combine(k, b, m0, m1):
                    if m0 == 0:
                        pe.wait_ge(yh_done, PAIRS * layer + k + 1)
                        pe.wait_ge(yl_done, PAIRS * layer + k + 1)
                        pe.wait_ge(slots_ready, s0 + k + 1)
                    for m in range(m0, m1):
                        wait(pe, added, SUMS * PAIRS * layer + SUMS * k + m - 1)
                        combine_mm(m, b, b).then_inc(combined, 1)

                def arrived(c, k, j, b):
                    g = g0 + 3 * b + c
                    pe.wait_ge(landed[g % SLOTS], landing[g] + 16 * j)

                def step(k, j, b, first):
                    pe.wait_ge(xs_ready, s0 + k + 1)
                    wait(pe, h_done, PAIRS * layer + k)
                    arrived(0, k, j, b)
                    arrived(1, k, j, b)
                    slot = (g0 + 3 * b) % SLOTS
                    hidden_mm(slot, b, 0, C // 2)
                    if not first:
                        combine(k - 1, 1 - b, 0, 2)
                    hidden_mm(slot, b, C // 2, C).then_inc(tile_used, 1)
                    if not first:
                        combine(k - 1, 1 - b, 2, 4)
                    gather(k + 1, 1 - b)
                    pe.wait_ge(h_done, PAIRS * layer + k + 1)
                    pe.wait_ge(slotv_ready, s0 + k + 2)
                    turn_hidden().then_inc(hT_done, 1)
                    if not first:
                        combine(k - 1, 1 - b, 4, SUMS)
                    pe.wait_ge(hT_copied, PAIRS * layer + k + 1)
                    arrived(2, k, j, b)
                    down_mm((g0 + 3 * b + 2) % SLOTS).then_inc(tile_used, 1)

                for t in range(T):
                    pe.wait_ge(part2_ready[t], layer + 1)
                wait_drained(pe, layer, "count")
                wait_drained(pe, layer, "sgate", 1)
                gather(0, 0)
                step(0, 0, 0, True)
                step(1, 0, 1, False)
                with pe.Fori(1, PAIRS // 2) as j:
                    for b in range(2):
                        step(2 * j + b, j, b, False)
                combine(PAIRS - 1, 1, 0, SUMS)

                pe.wait_ge(passes_ready, layer + 1)
                npass = pe.value_load(passes[0:1, layer:layer + 1], min_val=1, max_val=PASSES)
                with pe.If(npass > 1):
                    pe.wait_ge(added, SUMS * PAIRS * (layer + 1))
                    with pe.Fori(1, npass) as p:
                        with pe.Fori(0, PAIRS) as k:
                            n = (p - 1) * PAIRS + k
                            pe.wait_ge(more["added"], SUMS * n + 1)
                            pe.wait_ge(more["sel"], n + 1)
                            slot_mm(0).then_inc(more["slotm"], 1)
                            gather_mm(0, 0)
                            gather_mm(0, 1).then_inc(more["gathered"], 1)
                            pe.wait_ge(more["xs"], n + 1)
                            pe.wait_ge(more["landed"], 48 * n + 48)
                            hidden_mm(0, 0, 0, C).then_inc(more["up"], 1)
                            pe.wait_ge(more["h"], n + 1)
                            pe.wait_ge(more["slotv"], n + 1)
                            turn_hidden().then_inc(more["hT"], 1)
                            pe.wait_ge(more["hTc"], n + 1)
                            down_mm(2).then_inc(more["down"], 1)
                            pe.wait_ge(more["yl"], n + 1)
                            pe.wait_ge(more["slots"], n + 1)
                            for m in range(SUMS):
                                pe.wait_ge(more["added"], SUMS * n + m + 1)
                                combine_mm(m, 0, 0).then_inc(more["combined"], 1)
                            pe.wait_ge(more["added"], SUMS * (n + 1) + 1)


INS = ["x_prompt", "x_sample", "mem_prompt", "cache_mem_k", "cache_mem_v", "state_conv_a", "state_conv_b",
       "w_in_a", "conv_a_w", "conv_a_b", "norm_a_g", "norm_a_b", "w_in_b", "conv_b_w", "w_kv", "w_out", "ln1_g",
       "ln1_b", "w_router", "router_bias", "w_gate", "w_up", "w_down", "ws_gate", "ws_up", "ws_down", "ln2_g", "ln2_b"]
OUTS = [(1, 256, 1024), (8, 4, 1024), (2, 1, 256, 4, 128), (2, 1, 256, 4, 128), (1, 1, 30, 512), (1, 1, 2, 512),
        (1, 8, 30, 512), (1, 8, 2, 512)]


def kernel(**inputs):
    import numpy as np
    import concourse.bacc as bacc
    from concourse.bass_utils import run_bass_kernel_spmd

    nc = bacc.Bacc("TRN2", target_bir_lowering=False, num_devices=1)
    arrays, ins = {}, {}
    for name in INS:
        a = np.ascontiguousarray(inputs[name])
        arrays[f"in_{name}"] = a
        ins[name] = nc.dram_tensor(f"in_{name}", a.shape, mybir.dt.from_np(a.dtype), kind="ExternalInput").ap()
    outs = [nc.dram_tensor(f"out_{i}", shape, F32, kind="ExternalOutput").ap() for i, shape in enumerate(OUTS)]
    build_program(nc, ins, outs)
    r = run_bass_kernel_spmd(nc, [arrays], core_ids=[0])
    return tuple(r.results[0][f"out_{i}"] for i in range(len(OUTS)))
```
